# Optimizing a Trainium2 kernel written in Bass

```python
import math
import jax
import jax.numpy as jnp
from jax import lax
import numpy as np

D_MODEL = 1024
BATCH = 1
SEQ = 2048
DEPTH = 1

GRID_W = 64
CTX_LEN = 256
D_MIX = D_MODEL
D_CONV = D_MIX // 4
CONV_WIDTH = 3
D_SSM = D_MIX // 4
SSM_GROUP = 16
SSM_GROUPS = D_SSM // SSM_GROUP
SSM_STATE = 64
HEAD_DIM = 64
D_ATTN = D_MIX - D_CONV - D_SSM
N_Q_HEADS = D_ATTN // HEAD_DIM
N_KV_HEADS = 2
Q_PER_KV = N_Q_HEADS // N_KV_HEADS
D_KV = N_KV_HEADS * HEAD_DIM
AXIS_PAIRS = HEAD_DIM // 4
ROPE_BASE = 10000.0
WINDOW = 128
BLOCK = 128
N_EXPERTS = 32
TOP_K = 4
D_EXPERT = 128
D_SHARED = 128
ROUTED_SCALE = 2.5
NORM_EPS = 1e-6
NEG_INF = -1e30
PROJ_SPLITS = (D_CONV, 2 * D_CONV, 3 * D_CONV, 3 * D_CONV + D_SSM,
               3 * D_CONV + D_SSM + D_ATTN, 3 * D_CONV + D_SSM + D_ATTN + D_KV)
D_IN_PROJ = 3 * D_CONV + D_SSM + D_ATTN + 2 * D_KV

kernel_name = 'hybrid_conv_s5_swa_moe_dit_block'

def rms_norm(x, g):
    xf = x.astype(jnp.float32)
    y = xf * lax.rsqrt(jnp.mean(xf * xf, axis=-1, keepdims=True) + NORM_EPS)
    return (y * g.astype(jnp.float32)).astype(x.dtype)

def modulate(x, shift, scale):
    return x * (1.0 + scale) + shift

def axial_rope_angles(n_tokens):
    rows = n_tokens // GRID_W
    row = jnp.repeat(jnp.arange(rows, dtype=jnp.float32), GRID_W)
    col = jnp.tile(jnp.arange(GRID_W, dtype=jnp.float32), rows)
    inv_freq = ROPE_BASE ** (-jnp.arange(AXIS_PAIRS, dtype=jnp.float32) / AXIS_PAIRS)
    return jnp.stack([row[:, None] * inv_freq, col[:, None] * inv_freq], axis=1)

def apply_axial_rope(t, ang):
    b, l, h, _ = t.shape
    t4 = t.reshape(b, l, h, 2, 2, AXIS_PAIRS)
    t1, t2 = t4[..., 0, :], t4[..., 1, :]
    cos = jnp.cos(ang)[None, :, None]
    sin = jnp.sin(ang)[None, :, None]
    out = jnp.stack([t1 * cos - t2 * sin, t1 * sin + t2 * cos], axis=-2)
    return out.reshape(b, l, h, HEAD_DIM)

def head_rms(t, n_heads, g):
    b, l, _ = t.shape
    return rms_norm(t.reshape(b, l, n_heads, HEAD_DIM), g).astype(jnp.float32)

def short_conv_mixer(conv_x, conv_b, conv_c, conv_w):
    v = conv_c * conv_x
    y = lax.conv_general_dilated(v, conv_w.astype(v.dtype)[:, None, :], window_strides=(1,),
                                 padding=((1, 1),), dimension_numbers=('NWC', 'WIO', 'NWC'),
                                 feature_group_count=D_CONV)
    return conv_b * y

def ssm_drive(u, b_bar):
    b, l, _ = u.shape
    ug = u.reshape(b, l, SSM_GROUPS, SSM_GROUP).astype(jnp.complex64)
    return jnp.einsum('blgh,gph->blgp', ug, b_bar)

def ssm_readout(h, c_mat):
    b, l = h.shape[:2]
    return jnp.einsum('blgp,ghp->blgh', h, c_mat).real.reshape(b, l, D_SSM)

def diag_scan(lam_bar, bu, reverse):
    a = jnp.broadcast_to(lam_bar, bu.shape)

    def combine(e1, e2):
        a1, b1 = e1
        a2, b2 = e2
        return a1 * a2, a2 * b1 + b2

    _, h = lax.associative_scan(combine, (a, bu), reverse=reverse, axis=1)
    return h

def ssm_glu(y, w_glu, b_glu):
    g = jax.nn.gelu(y)
    return g * jax.nn.sigmoid(g @ w_glu + b_glu)

def ssm_mixer(u_lat, u_ctx, lam_re, lam_im, log_dt, b_re, b_im, c_re, c_im, d_skip, w_glu, b_glu,
              with_ctx_out):
    f32 = jnp.float32
    d = d_skip.astype(f32)
    ul = u_lat.astype(f32)
    uc = u_ctx.astype(f32)
    y_lat = d * ul
    y_ctx = d * uc if with_ctx_out else None
    for direction, reverse in ((0, False), (1, True)):
        lam = lax.complex(lam_re[direction].astype(f32), lam_im[direction].astype(f32))
        dt = jnp.exp(log_dt[direction].astype(f32))[:, None]
        lam_bar = jnp.exp(lam * dt)
        b_mat = lax.complex(b_re[direction].astype(f32), b_im[direction].astype(f32))
        b_bar = ((lam_bar - 1.0) / lam)[..., None] * b_mat
        c_mat = lax.complex(c_re[direction].astype(f32), c_im[direction].astype(f32))
        h_ctx = diag_scan(lam_bar, ssm_drive(uc, b_bar), reverse)
        h0 = h_ctx[:, 0] if reverse else h_ctx[:, -1]
        bu = ssm_drive(ul, b_bar)
        bu = bu.at[:, -1 if reverse else 0].add(lam_bar * h0)
        y_lat = y_lat + ssm_readout(diag_scan(lam_bar, bu, reverse), c_mat)
        if with_ctx_out:
            y_ctx = y_ctx + ssm_readout(h_ctx, c_mat)
    out_lat = ssm_glu(y_lat, w_glu, b_glu)
    out_ctx = ssm_glu(y_ctx, w_glu, b_glu) if with_ctx_out else None
    return out_lat, out_ctx

def window_attention(q, k, v, k_ctx, v_ctx, sink):
    b, l = q.shape[:2]
    n_blk = l // BLOCK
    n_ctx = k_ctx.shape[1]
    scale = HEAD_DIM ** -0.5
    qb = q.reshape(b, n_blk, BLOCK, N_KV_HEADS, Q_PER_KV, HEAD_DIM)

    def band(t):
        tp = jnp.pad(t, ((0, 0), (BLOCK, BLOCK), (0, 0), (0, 0)))
        tp = tp.reshape(b, n_blk + 2, BLOCK, N_KV_HEADS, HEAD_DIM)
        return jnp.concatenate([tp[:, :-2], tp[:, 1:-1], tp[:, 2:]], axis=2)

    kb, vb = band(k), band(v)
    s_win = jnp.einsum('bnqgrd,bnkgd->bgrnqk', qb, kb) * scale
    blk = jnp.arange(n_blk)[:, None, None]
    qpos = blk * BLOCK + jnp.arange(BLOCK)[None, :, None]
    kpos = (blk - 1) * BLOCK + jnp.arange(3 * BLOCK)[None, None, :]
    valid = (jnp.abs(qpos - kpos) <= WINDOW) & (kpos >= 0) & (kpos < l)
    s_win = jnp.where(valid, s_win, NEG_INF)
    s_ctx = jnp.einsum('bnqgrd,bcgd->bgrnqc', qb, k_ctx) * scale
    s_sink = jnp.broadcast_to(
        sink.astype(jnp.float32).reshape(N_KV_HEADS, Q_PER_KV)[None, :, :, None, None, None],
        s_win.shape[:-1] + (1,))
    p = jax.nn.softmax(jnp.concatenate([s_win, s_ctx, s_sink], axis=-1), axis=-1)
    p_win = p[..., :3 * BLOCK]
    p_ctx = p[..., 3 * BLOCK:3 * BLOCK + n_ctx]
    o = (jnp.einsum('bgrnqk,bnkgd->bnqgrd', p_win, vb)
         + jnp.einsum('bgrnqc,bcgd->bnqgrd', p_ctx, v_ctx))
    return o.reshape(b, l, D_ATTN)

def context_attention(q_ctx, k_ctx, v_ctx, sink):
    b, n_ctx = q_ctx.shape[:2]
    qg = q_ctx.reshape(b, n_ctx, N_KV_HEADS, Q_PER_KV, HEAD_DIM)
    s = jnp.einsum('bqgrd,bkgd->bgrqk', qg, k_ctx) * HEAD_DIM ** -0.5
    s_sink = jnp.broadcast_to(
        sink.astype(jnp.float32).reshape(N_KV_HEADS, Q_PER_KV)[None, :, :, None, None],
        s.shape[:-1] + (1,))
    p = jax.nn.softmax(jnp.concatenate([s, s_sink], axis=-1), axis=-1)
    o = jnp.einsum('bgrqk,bkgd->bqgrd', p[..., :n_ctx], v_ctx)
    return o.reshape(b, n_ctx, D_ATTN)

def moe_ffn(x, router_w, router_bias, w_exp_gate, w_exp_up, w_exp_down, w_sh_gate, w_sh_up, w_sh_down):
    shp = x.shape
    t = x.reshape(-1, D_MODEL)
    scores = jax.nn.sigmoid(t.astype(jnp.float32) @ router_w.astype(jnp.float32))
    _, idx = lax.top_k(scores + router_bias.astype(jnp.float32), TOP_K)
    sel = jnp.take_along_axis(scores, idx, axis=-1)
    wts = sel / jnp.sum(sel, axis=-1, keepdims=True) * ROUTED_SCALE
    gates = jnp.sum(jax.nn.one_hot(idx, N_EXPERTS, dtype=jnp.float32) * wts[..., None], axis=1)
    hg = jnp.einsum('td,def->tef', t, w_exp_gate)
    hu = jnp.einsum('td,def->tef', t, w_exp_up)
    hidden = jax.nn.silu(hg) * hu * gates[..., None]
    y = jnp.einsum('tef,efd->td', hidden, w_exp_down)
    y = y + (jax.nn.silu(t @ w_sh_gate) * (t @ w_sh_up)) @ w_sh_down
    return y.reshape(shp)

def setup_inputs(seed: int = 0) -> dict:
    key = jax.random.key(seed)
    ks = jax.random.split(key, 32)
    f32 = jnp.float32

    def nrm(i, shape, scale):
        return scale * jax.random.normal(ks[i], shape, f32)

    n_idx = jnp.arange(SSM_STATE, dtype=f32)
    ssm_shape = (DEPTH, 2, SSM_GROUPS, SSM_STATE)
    return {
        'x': nrm(0, (BATCH, SEQ, D_MODEL), 1.0),
        'c': nrm(1, (BATCH, D_MODEL), 1.0),
        'ctx': nrm(2, (BATCH, CTX_LEN, D_MODEL), 1.0),
        'c_ctx': nrm(3, (D_MODEL,), 1.0),
        'w_mod': nrm(4, (DEPTH, D_MODEL, 6 * D_MODEL), 0.5 * D_MODEL ** -0.5),
        'b_mod': nrm(5, (DEPTH, 6 * D_MODEL), 0.01),
        'norm1_g': 1.0 + nrm(6, (DEPTH, D_MODEL), 0.02),
        'norm2_g': 1.0 + nrm(7, (DEPTH, D_MODEL), 0.02),
        'w_in': nrm(8, (DEPTH, D_MODEL, D_IN_PROJ), D_MODEL ** -0.5),
        'conv_w': nrm(9, (DEPTH, CONV_WIDTH, D_CONV), CONV_WIDTH ** -0.5),
        'ssm_lam_re': -0.5 + nrm(10, ssm_shape, 0.01),
        'ssm_lam_im': jnp.pi * n_idx + nrm(11, ssm_shape, 0.01),
        'ssm_log_dt': jax.random.uniform(ks[12], (DEPTH, 2, SSM_GROUPS), dtype=f32,
                                         minval=math.log(1e-3), maxval=math.log(1e-1)),
        'ssm_b_re': nrm(13, (DEPTH, 2, SSM_GROUPS, SSM_STATE, SSM_GROUP), (2 * SSM_GROUP) ** -0.5),
        'ssm_b_im': nrm(14, (DEPTH, 2, SSM_GROUPS, SSM_STATE, SSM_GROUP), (2 * SSM_GROUP) ** -0.5),
        'ssm_c_re': nrm(15, (DEPTH, 2, SSM_GROUPS, SSM_GROUP, SSM_STATE), SSM_STATE ** -0.5),
        'ssm_c_im': nrm(16, (DEPTH, 2, SSM_GROUPS, SSM_GROUP, SSM_STATE), SSM_STATE ** -0.5),
        'ssm_d': nrm(17, (DEPTH, D_SSM), 1.0),
        'w_glu': nrm(18, (DEPTH, D_SSM, D_SSM), D_SSM ** -0.5),
        'b_glu': nrm(19, (DEPTH, D_SSM), 0.01),
        'q_norm_g': 1.0 + nrm(20, (DEPTH, HEAD_DIM), 0.02),
        'k_norm_g': 1.0 + nrm(21, (DEPTH, HEAD_DIM), 0.02),
        'attn_sink': nrm(22, (DEPTH, N_Q_HEADS), 1.0),
        'w_out': nrm(23, (DEPTH, D_MIX, D_MODEL), D_MIX ** -0.5),
        'router_w': nrm(24, (DEPTH, D_MODEL, N_EXPERTS), D_MODEL ** -0.5),
        'router_bias': nrm(25, (DEPTH, N_EXPERTS), 0.01),
        'w_exp_gate': nrm(26, (DEPTH, D_MODEL, N_EXPERTS, D_EXPERT), D_MODEL ** -0.5),
        'w_exp_up': nrm(27, (DEPTH, D_MODEL, N_EXPERTS, D_EXPERT), D_MODEL ** -0.5),
        'w_exp_down': nrm(28, (DEPTH, N_EXPERTS, D_EXPERT, D_MODEL), D_EXPERT ** -0.5),
        'w_sh_gate': nrm(29, (DEPTH, D_MODEL, D_SHARED), D_MODEL ** -0.5),
        'w_sh_up': nrm(30, (DEPTH, D_MODEL, D_SHARED), D_MODEL ** -0.5),
        'w_sh_down': nrm(31, (DEPTH, D_SHARED, D_MODEL), D_SHARED ** -0.5),
    }

def reference(x, c, ctx, c_ctx, w_mod, b_mod, norm1_g, norm2_g, w_in, conv_w,
              ssm_lam_re, ssm_lam_im, ssm_log_dt, ssm_b_re, ssm_b_im, ssm_c_re, ssm_c_im,
              ssm_d, w_glu, b_glu, q_norm_g, k_norm_g, attn_sink, w_out,
              router_w, router_bias, w_exp_gate, w_exp_up, w_exp_down,
              w_sh_gate, w_sh_up, w_sh_down):
    n_lat = x.shape[1]
    rope_ang = axial_rope_angles(n_lat)
    silu_c = jax.nn.silu(c)[:, None, :]
    silu_cc = jax.nn.silu(c_ctx)[None, None, :]
    h, hc = x, ctx
    for l in range(DEPTH):
        ctx_out = l < DEPTH - 1
        sh1, sc1, g1, sh2, sc2, g2 = jnp.split(silu_c @ w_mod[l] + b_mod[l], 6, axis=-1)
        csh1, csc1, cg1, csh2, csc2, cg2 = jnp.split(silu_cc @ w_mod[l] + b_mod[l], 6, axis=-1)

        p = modulate(rms_norm(h, norm1_g[l]), sh1, sc1) @ w_in[l]
        pc = modulate(rms_norm(hc, norm1_g[l]), csh1, csc1) @ w_in[l]
        conv_x, conv_b, conv_c, u, q, k, v = jnp.split(p, PROJ_SPLITS, axis=-1)
        conv_xc, conv_bc, conv_cc, uc, qc, kc, vc = jnp.split(pc, PROJ_SPLITS, axis=-1)

        y_conv = short_conv_mixer(conv_x, conv_b, conv_c, conv_w[l])
        y_ssm, y_ssm_c = ssm_mixer(u, uc, ssm_lam_re[l], ssm_lam_im[l], ssm_log_dt[l], ssm_b_re[l],
                                   ssm_b_im[l], ssm_c_re[l], ssm_c_im[l], ssm_d[l], w_glu[l], b_glu[l],
                                   ctx_out)
        q_lat = apply_axial_rope(head_rms(q, N_Q_HEADS, q_norm_g[l]), rope_ang)
        k_lat = apply_axial_rope(head_rms(k, N_KV_HEADS, k_norm_g[l]), rope_ang)
        v_lat = v.reshape(v.shape[0], n_lat, N_KV_HEADS, HEAD_DIM)
        k_ctx = head_rms(kc, N_KV_HEADS, k_norm_g[l])
        v_ctx = vc.reshape(vc.shape[0], vc.shape[1], N_KV_HEADS, HEAD_DIM)
        y_att = window_attention(q_lat, k_lat, v_lat, k_ctx, v_ctx, attn_sink[l])

        mix = jnp.concatenate([y_conv, y_ssm, y_att], axis=-1) @ w_out[l]
        h_mid = h + g1 * mix
        h_new = h_mid + g2 * moe_ffn(modulate(rms_norm(h_mid, norm2_g[l]), sh2, sc2),
                                     router_w[l], router_bias[l], w_exp_gate[l], w_exp_up[l],
                                     w_exp_down[l], w_sh_gate[l], w_sh_up[l], w_sh_down[l])

        if ctx_out:
            y_conv_c = short_conv_mixer(conv_xc, conv_bc, conv_cc, conv_w[l])
            q_ctx = head_rms(qc, N_Q_HEADS, q_norm_g[l])
            y_att_c = context_attention(q_ctx, k_ctx, v_ctx, attn_sink[l])
            mix_c = jnp.concatenate([y_conv_c, y_ssm_c, y_att_c], axis=-1) @ w_out[l]
            hc_mid = hc + cg1 * mix_c
            hc = hc_mid + cg2 * moe_ffn(modulate(rms_norm(hc_mid, norm2_g[l]), csh2, csc2),
                                        router_w[l], router_bias[l], w_exp_gate[l], w_exp_up[l],
                                        w_exp_down[l], w_sh_gate[l], w_sh_up[l], w_sh_down[l])
        h = h_new
    return h


_drawn_inputs = setup_inputs


def setup_inputs(seed=0):
    import zlib

    import numpy as np

    out = dict(_drawn_inputs(seed))
    spreads = {}
    factors = {'ssm_lam_re': 200.0,
     'ssm_b_re': 38.617,
     'b_glu': 44.821,
     'q_norm_g': 8.0,
     'k_norm_g': 8.0,
     'attn_sink': 8.0,
     'ssm_lam_im': 17.666,
     'ssm_log_dt': 17.566,
     'ssm_b_im': 24.88,
     'ssm_c_re': 18.059,
     'ssm_c_im': 16.361}
    for name, (base, spread) in spreads.items():
        noise = np.random.default_rng([zlib.crc32(name.encode()), seed]).standard_normal(out[name].shape)
        drawn = base * np.exp(spread * noise) if base else spread * noise
        out[name] = jnp.asarray(drawn.astype(out[name].dtype))
    for name, factor in factors.items():
        out[name] = (out[name] * factor).astype(out[name].dtype)
    return out
```

```python
import math
from contextlib import ExitStack

import concourse.bass as bass
from concourse import mybir

F32 = mybir.dt.float32
BF16 = mybir.dt.bfloat16
ALU = mybir.AluOpType
ACT = mybir.ActivationFunctionType
AX = mybir.AxisListType

P = 128
D = 1024
KD = D // P
SEQ, CTX = 2048, 256
BLK = 256
TPB = BLK // P
NBLK = (SEQ + CTX) // BLK
NTILE = SEQ // P
N_IN = 1792
COL_B, COL_C, COL_U, COL_Q, COL_K = 256, 512, 768, 1024, 1536
HD = 64
NHEAD, NKV, QPK = 8, 2, 4
SCALE = HD ** -0.5
EPS = 1e-6

CH = 8
NG, GH, NS = 16, 16, 64
UP = NG // 2
NU = 2 * UP
CCTX, CLAT = CTX // CH, SEQ // CH
NCHUNK = CCTX + CLAT
CB = BLK // CH
DOUBLINGS = 8
MULTS = list(range(CH, -1, -1)) + list(range(0, CH + 1)) + [CH << j for j in range(1, DOUBLINGS + 1)]
RISE, DBL = CH + 1, 2 * (CH + 1)
NPOW, NM = 2 * (CH + 1), len(MULTS)
KW = (2 * CH - 1) * GH
INV_2PI = 1.0 / (2.0 * math.pi)
PI_A = 6.28125
PI_B = 0.0019350051879882812
PI_C = 2.0 * math.pi - PI_A - PI_B
LN2_A = 0.693359375
LN2_B = math.log(2.0) - LN2_A
ROUND = 1.5 * 2.0 ** 23

NR, TOPK, ROUTED = 32, 4, 2.5
NE = NR + 1
EF = 128
TB = 4
TW = SEQ // TB

PACK = {}
_at = 0
for _name, _n in (("c", 2 * KD), ("b_mod", 48), ("norm1", KD), ("norm2", KD), ("lam_re", NU), ("lam_im", NU),
                  ("log_dt", NU), ("q_g", HD), ("k_g", HD), ("sink", NHEAD), ("b_glu", 2), ("conv_w", 6),
                  ("r_bias", NR), ("mults", NM), ("d_skip", NG)):
    PACK[_name] = (_at, _n)
    _at += _n
N_PACK = _at


def block_kernel(nc, a, out):
    ctx = ExitStack()
    with ctx:
        def sb(name, shape, dt=F32):
            return ctx.enter_context(nc.sbuf_tensor(name, shape, dt))

        def sem(name):
            return ctx.enter_context(nc.semaphore(name))

        arena = sb("arena", [P, 51584])

        def cut(at, *shape, rows=P):
            n = math.prod(shape)
            assert at + n <= 51584
            v = arena[0:rows, at:at + n]
            if len(shape) == 2:
                v = v.rearrange("p (a b) -> p a b", b=shape[1])
            if len(shape) == 3:
                v = v.rearrange("p (a b c) -> p a b c", b=shape[1], c=shape[2])
            return v

        mixT = cut(0, 8, SEQ)
        kT = cut(16384, SEQ + CTX)
        V = cut(18688, (SEQ + CTX) // P, P)
        tab = cut(0, UP, 2, NCHUNK)
        drv = cut(4608, 2, NU, P)
        Kfull = cut(4608, NG, KW, rows=GH)
        cA = cut(8704, 2, NU, (CH + 1) * GH)
        bbar = cut(13312, 2, NU, GH)
        raw = cut(13824, 4, NU, GH)
        tmpA = cut(14848, 1152)
        tmpB = cut(16000, 1152)
        drvT_st = cut(17152, 2, 512)
        ptmp = cut(18176, 2, UP * 128)
        mask_st = cut(18176, 2 * P)
        wmod = cut(39424, 2, KD, 512)
        SM = [cut(47616 + i * NU * NM, NU, NM) for i in range(7)]
        w_in = cut(20992, KD, N_IN)
        xs = cut(35328, 2, TPB, D)
        xnT = cut(39424, 2, KD, BLK)
        U_st = cut(43520, 2, NG * CB)
        Uc = cut(44544, NG, CH, GH, rows=CB)
        uT = cut(46592, 2, BLK)
        qg = cut(47104, 10, HD)
        sq = cut(47744, 10, HD)
        rc = cut(48384, 10, HD)
        qkr = cut(49024, TPB, 640)
        rope = cut(50304, 2, TPB, 2 * HD)
        junk = cut(50816, 512).bitcast(BF16)
        xtmp = cut(51328, BLK)
        wm2 = cut(29696, KD, 512)
        U = cut(20992, NG, NCHUNK)
        S = cut(25600, NU, 2, CLAT)
        ctmp = cut(28672, 2, 512)
        R = cut(33792, NU, 2, P)
        M = cut(37888, NG, P)
        Pb = cut(39936, 8, 640)
        PT = cut(45056, 2, 512)
        ust = cut(46080, 2, 832)
        rot = cut(47744, 6, NCHUNK)
        g1bc = cut(49472, D)
        g2bc = cut(50496, D)
        Yc = cut(16384, 2, CH, 256)
        w_glu = cut(20480, 2, 256)
        th = cut(20992, 2, 512)
        w_out = cut(39936, KD, D)
        tT = cut(20992, KD, SEQ)
        xo = cut(16384, 2, TPB, D)
        hm = cut(37376, TPB, D)
        gT = cut(37376, SEQ, rows=NE)
        lgt = cut(48128, NTILE, NR)
        r_w = cut(48640, KD, NR)
        junk2 = cut(48896, 512).bitcast(BF16)
        restart = cut(0, NTILE * NR)
        rt = [cut(512 * (i + 1), NTILE, NR) for i in range(6)]
        rsm = cut(512 * 7, 4, NTILE)
        top8 = cut(512 * 8, NTILE, 8)
        y = cut(0, NTILE, D)
        wx = [cut(16384, 3, D), cut(37376 + 2048, 3, D), cut(42496, 3, D)]
        gbc = cut(45568, TB, TW)
        sl = cut(47616, 2, 512)
        hT = cut(48640, 2, 512)
        hfin = cut(20992, NTILE, D)

        ident = sb("ident", [P, P])
        identb = sb("identb", [P, P], BF16)
        maskb = sb("maskb", [P, 2 * P], BF16)
        pack = sb("pack", [P, N_PACK])

        def pk(name, lo=0, n=None):
            at, size = PACK[name]
            return pack[:, at + lo:at + lo + (n or size)]

        silu_c = sb("silu_c", [P, KD, 2])
        scale1 = sb("scale1", [P, KD, 2])
        shift1 = sb("shift1", [P, KD, 2])
        mod2 = sb("mod2", [P, 2 * KD])
        scale2 = sb("scale2", [P, KD])
        nsink = sb("nsink", [P, NHEAD])
        hbglu = sb("hbglu", [P, 2])
        eps = sb("eps", [P, 1])
        r8 = sb("r8", [P, NU])
        ss = sb("ss", [P, 2, TPB])
        rstd = sb("rstd", [P, TPB])
        hs = sb("hs", [P, 10])
        hstd = sb("hstd", [P, 10])
        hrs = sb("hrs", [P, 10])
        mx = sb("mx", [P, 2, QPK])
        negm = sb("negm", [P, 2, QPK])
        rs = sb("rs", [P, 2, QPK])
        esink = sb("esink", [P, 2, QPK])
        rden = sb("rden", [P, 2, QPK])

        banks = ctx.enter_context(nc.psum_tensor("banks", [P, 8, 512], F32))
        PS = [banks[:, i, :] for i in range(8)]

        drvT_d = nc.dram_tensor("drvT_d", [NU, P, 2, P], F32).ap()
        tab_d = nc.dram_tensor("tab_d", [NU, P, 2, NCHUNK], F32).ap()
        R_d = nc.dram_tensor("R_d", [P, NU, 2, P], F32).ap()
        M_d = nc.dram_tensor("M_d", [P, NG, P], F32).ap()
        U_d = nc.dram_tensor("U_d", [P, NG, NCHUNK], F32).ap()
        h_d = nc.dram_tensor("h_d", [NTILE, P, D], F32).ap()
        gT_d = nc.dram_tensor("gT_d", [NE, SEQ], F32).ap()

        pack_in = sem("pack_in")
        ident_in = sem("ident_in")
        raw_in = sem("raw_in")
        mask_in = sem("mask_in")
        mask_done = sem("mask_done")
        wmod_in = [sem(f"wmod_in{i}") for i in range(2)]
        wmod_used = sem("wmod_used")
        w_in_in = [sem(f"w_in_in{i}") for i in range(3)]
        x_in = [sem(f"x_in{i}") for i in range(2)]
        rope_in = [sem(f"rope_in{i}") for i in range(2)]
        silu_done = sem("silu_done")
        args_done = sem("args_done")
        trig_done = sem("trig_done")
        dve_step = sem("dve_step")
        act_step = sem("act_step")
        pool_step = sem("pool_step")
        unit_cs = sem("unit_cs")
        drv_done = sem("drv_done")
        drvT_ps = sem("drvT_ps")
        drvT_out = sem("drvT_out")
        drvT_stored = [sem(f"drvT_stored{i}") for i in range(2)]
        tab_done = sem("tab_done")
        tab_stored = sem("tab_stored")
        mats_done = sem("mats_done")
        K_ps = sem("K_ps")
        K_out = sem("K_out")
        K_done = sem("K_done")
        mats_stored = sem("mats_stored")
        mod1_done = sem("mod1_done")
        std_done = sem("std_done")
        x_scaled = sem("x_scaled")
        xn_ps = sem("xn_ps")
        xn_out = sem("xn_out")
        cx_ps, cx_out = sem("cx_ps"), sem("cx_out")
        cc_ps, cc_out = sem("cc_ps"), sem("cc_out")
        cb_ps, cb_out = sem("cb_ps"), sem("cb_out")
        u_ps, u_out = sem("u_ps"), sem("u_out")
        q_ps, q_sq, q_out = sem("q_ps"), sem("q_sq"), sem("q_out")
        kv_ps, k_sq, v_out, k_out = sem("kv_ps"), sem("k_sq"), sem("v_out"), sem("k_out")
        hs_done = sem("hs_done")
        hstd_done = sem("hstd_done")
        qk_done = sem("qk_done")
        turn_ps, turn_out = sem("turn_ps"), sem("turn_out")
        U_stored = [sem(f"U_stored{i}") for i in range(2)]
        U_in = sem("U_in")
        mats_in = sem("mats_in")
        ust_in = [sem(f"ust_in{i}") for i in range(2)]
        wm2_in, m2_ps, m2_out = sem("wm2_in"), sem("m2_ps"), sem("m2_out")
        bias_in = sem("bias_in")
        s_ps, negm_done, exp_done = sem("s_ps"), sem("negm_done"), sem("exp_done")
        es_in, es_done, rden_done, P_done = sem("es_in"), sem("es_done"), sem("rden_done"), sem("P_done")
        pt_ps, pt_dve, pt_act = sem("pt_ps"), sem("pt_dve"), sem("pt_act")
        pv_ps, o_out = sem("pv_ps"), sem("o_out")
        xr_ps, xr_out, rotated, unit_done = sem("xr_ps"), sem("xr_out"), sem("rotated"), sem("unit_done")
        conv_done = sem("conv_done")
        y_ps, y_out, yt_ps, yt_out = sem("y_ps"), sem("y_out"), sem("yt_ps"), sem("yt_out")
        wglu_in, z_ps, z_out, glu_done = sem("wglu_in"), sem("z_ps"), sem("z_out"), sem("glu_done")
        w_out_in, r_w_in = sem("w_out_in"), sem("r_w_in")
        xo_in = [sem(f"xo_in{i}") for i in range(2)]
        o2_ps, o2_out, hm_done, h_stored = sem("o2_ps"), sem("o2_out"), sem("hm_done"), sem("h_stored")
        std2_done, x2_scaled, t2_ps, t2_out = sem("std2_done"), sem("x2_scaled"), sem("t2_ps"), sem("t2_out")
        lg_ps, lg_out, sig_done, gates_done = sem("lg_ps"), sem("lg_out"), sem("sig_done"), sem("gates_done")
        restart_in, gT_ps, gT_out, gT_stored = sem("restart_in"), sem("gT_ps"), sem("gT_out"), sem("gT_stored")
        y_clear = sem("y_clear")
        wx_in = [sem(f"wx_in{i}") for i in range(3)]
        gbc_in = [sem(f"gbc_in{i}") for i in range(TB)]
        hg_ps, hu_ps, sl_out, hu_out, h_done = (sem(n) for n in ("hg_ps", "hu_ps", "sl_out", "hu_out", "h_done"))
        yd_ps, yd_out = sem("yd_ps"), sem("yd_out")
        hfin_in = [sem(f"hfin_in{i}") for i in range(4)]
        fin_dve, out_stored = sem("fin_dve"), sem("out_stored")

        block = ctx.enter_context(nc.Block())

        def turns(b):
            return 6 if b == 0 else 8

        def turns_before(b):
            return 0 if b == 0 else 6 + 8 * (b - 1)

        NGRP = 2 * NTILE
        NPP = NTILE // TPB

        def window(i):
            return list(range(max(0, i - 1), min(NTILE, i + 2)))

        def key_tiles(g):
            w = window(g // 2)
            return [(n * P, CTX // P + t) for n, t in enumerate(w)] + [(len(w) * P + c * P, c) for c in range(CTX // P)]

        def n_keys(g):
            return len(key_tiles(g)) * P

        def pt_before(g):
            return sum(len(key_tiles(x)) for x in range(g))

        def odd_before(g):
            return pt_before(g) // 2

        def even_before(g):
            return (pt_before(g) + 1) // 2

        @block.sync
        def _(sp):
            sp.dma_start(pack[:, :], a["pack"]).then_inc(pack_in, 16)
            sp.dma_start(raw, a["raw"]).then_inc(raw_in, 16)
            sp.dma_start(ident[:, :], a["ident"]).then_inc(ident_in, 16)
            sp.dma_start(mask_st, a["mask"]).then_inc(mask_in, 16)
            wm_src = a["w_mod"].rearrange("(k p) n -> p k n", p=P)

            def load_wmod(n):
                if n >= 2:
                    sp.wait_ge(wmod_used, n - 1)
                sp.dma_start(wmod[:, n % 2], wm_src[:, :, n * 512:(n + 1) * 512]).then_inc(wmod_in[n % 2], 16)

            def load_x(b):
                if b >= 2:
                    sp.wait_ge(xn_ps, 4 * (b - 1))
                src = a["ctx"] if b == 0 else a["x"][(b - 1) * BLK:b * BLK, :]
                sp.dma_start(xs[:, b % 2], src.rearrange("(t p) d -> p t d", p=P)).then_inc(x_in[b % 2], 16)

            load_wmod(0)
            load_wmod(1)
            load_x(0)
            for i, (lo, hi) in enumerate(((COL_U, COL_Q), (COL_Q, N_IN), (0, COL_U))):
                sp.dma_start(w_in[:, :, lo:hi], a["w_in"][:, :, lo:hi]).then_inc(w_in_in[i], 16)
            load_wmod(2)
            load_wmod(3)
            load_x(1)

            def store_U(b):
                sp.wait_ge(turn_out, turns_before(b + 1))
                sp.dma_start(U_d[:, :, b * CB:(b + 1) * CB], U_st[:, b % 2].rearrange("p (g c) -> p g c", c=CB)).then_inc(U_stored[b % 2], 16)

            for b in range(NBLK):
                if b >= 1:
                    if b >= 3:
                        sp.wait_ge(qk_done, TPB * (b - 1))
                    sp.dma_start(rope[:, b % 2], a["rope"][b - 1]).then_inc(rope_in[b % 2], 16)
                if b + 2 < NBLK:
                    load_x(b + 2)
                if b >= 1:
                    store_U(b - 1)
            store_U(NBLK - 1)

            sp.wait_ge(kv_ps, TPB * NBLK)
            sp.wait_ge(xn_ps, 4 * NBLK)
            sp.wait_ge(U_stored[0], 16 * 5)
            sp.wait_ge(U_stored[1], 16 * 4)
            sp.dma_start(U, U_d).then_inc(U_in, 16)

            def load_wm2(c):
                if c > 4:
                    sp.wait_ge(m2_ps, c - 4)
                sp.dma_start(wm2, wm_src[:, :, c * 512:(c + 1) * 512]).then_inc(wm2_in, 16)

            load_wm2(4)
            sp.wait_ge(turn_ps, turns_before(NBLK))
            sp.dma_start(g1bc, a["b_mod"][2:3, :].to_broadcast([P, D])).then_inc(bias_in, 16)
            sp.dma_start(g2bc, a["b_mod"][5:6, :].to_broadcast([P, D])).then_inc(bias_in, 16)
            load_wm2(5)
            sp.dma_start(R, R_d).then_inc(mats_in, 16)
            sp.dma_start(M, M_d).then_inc(mats_in, 16)
            for c in range(6, 12):
                load_wm2(c)
            sp.wait_ge(pv_ps, pt_before(NGRP))
            sp.dma_start(w_glu, a["w_glu"].rearrange("(k p) n -> p k n", p=P)).then_inc(wglu_in, 16)
            sp.wait_ge(unit_done, NU)
            sp.dma_start(w_out, a["w_out"]).then_inc(w_out_in, 16)
            sp.dma_start(r_w, a["router_w"]).then_inc(r_w_in, 16)

            def load_xo(pp):
                if pp < 2:
                    sp.wait_ge(yt_ps, 8)
                else:
                    sp.wait_ge(t2_ps, 4 * (pp - 1))
                sp.dma_start(xo[:, pp % 2], a["x"][pp * BLK:(pp + 1) * BLK, :].rearrange("(t p) d -> p t d", p=P))\
                    .then_inc(xo_in[pp % 2], 16)

            load_xo(0)
            load_xo(1)
            for pp in range(NPP):
                sp.wait_ge(hm_done, pp + 1)
                sp.dma_start(h_d[TPB * pp:TPB * (pp + 1)].rearrange("t p d -> p t d"), hm).then_inc(h_stored, 16)
                if pp + 2 < NPP:
                    load_xo(pp + 2)
            sp.wait_ge(o2_ps, 4 * NPP)
            sp.dma_start(restart, a["restart"]).then_inc(restart_in, 16)
            sp.wait_ge(t2_ps, 4 * NPP)

            def load_wx(e, slot):
                sp.dma_start(wx[slot].unsqueeze(1), a["wx"][bass.ds(e, 1)].rearrange("e p c n -> p e c n"))\
                    .then_inc(wx_in[slot], 16)

            def load_gate(e, tb):
                sp.dma_start(gbc[:, tb:tb + 1], gT_d[bass.ds(e, 1), tb * TW:(tb + 1) * TW].unsqueeze(0)
                             .to_broadcast([P, 1, TW])).then_inc(gbc_in[tb], 16)

            load_wx(0, 0)
            sp.wait_ge(gT_out, 4)
            sp.dma_start(gT_d, gT).then_inc(gT_stored, 16)
            sp.wait_ge(gT_stored, 16)
            sp.wait_ge(gT_ps, 4)
            load_wx(1, 1)
            load_wx(2, 2)
            for tb in range(TB):
                load_gate(0, tb)
            with sp.Fori(0, NE // 3 - 1) as it:
                for j in range(3):
                    e = it * 3 + (j + 1)
                    for tb in range(TB):
                        sp.wait_ge(h_done, it * 12 + (4 * j + tb + 1))
                        load_gate(e, tb)
                    sp.wait_ge(yd_ps, it * 96 + 32 * (j + 1))
                    load_wx(e + 2, j)
            for e in (NE - 2, NE - 1):
                for tb in range(TB):
                    sp.wait_ge(h_done, 4 * (e - 1) + tb + 1)
                    load_gate(e, tb)
            sp.wait_ge(yd_ps, 8 * 4 * NE)
            sp.wait_ge(h_stored, 16 * NPP)
            for q in range(4):
                sp.dma_start(hfin[:, 4 * q:4 * q + 4], h_d[4 * q:4 * q + 4].rearrange("t p d -> p t d"))\
                    .then_inc(hfin_in[q], 16)
            for q in range(8):
                sp.wait_ge(fin_dve, q + 1)
                sp.dma_start(out[2 * q * P:2 * (q + 1) * P, :].rearrange("(t p) d -> p t d", p=P),
                             y[:, 2 * q:2 * q + 2]).then_inc(out_stored, 16)
            sp.wait_ge(out_stored, 16 * 8)

        @block.gpsimd
        def _(pool):
            steps = [0]

            def link(ins):
                steps[0] += 1
                ins.then_inc(pool_step, 1)
                pool.wait_ge(pool_step, steps[0])

            pool.wait_ge(ident_in, 16)
            pool.tensor_copy(identb[:, :], ident[:, :])
            pool.wait_ge(mask_in, 16)
            pool.tensor_copy(maskb[:, :], mask_st).then_inc(mask_done, 1)
            pool.wait_ge(mask_done, 1)
            pool.wait_ge(trig_done, 2)
            pool.wait_ge(unit_cs, 1)
            cosm, sinm = SM[4], SM[3]
            for d in range(2):
                if d == 1:
                    pool.wait_ge(tab_stored, 16)
                us = slice(d * UP, (d + 1) * UP)
                pool.memset(tab[:, :, 0, 0:1], 1.0)
                pool.memset(tab[:, :, 1, 0:1], 0.0)
                pool.tensor_copy(tab[:, :, 0, 1:2], cosm[:, us, RISE + CH:RISE + CH + 1])
                link(pool.tensor_copy(tab[:, :, 1, 1:2], sinm[:, us, RISE + CH:RISE + CH + 1]))
                for j in range(1, DOUBLINGS + 1):
                    lo = 1 << j
                    n = min(lo, NCHUNK - lo)
                    co, si = tab[:, :, 0, 0:n], tab[:, :, 1, 0:n]
                    cm = cosm[:, us, DBL + j - 1:DBL + j].to_broadcast([P, UP, n])
                    sm = sinm[:, us, DBL + j - 1:DBL + j].to_broadcast([P, UP, n])
                    t0 = ptmp[:, 0, 0:UP * n].rearrange("p (u n) -> p u n", n=n)
                    t1 = ptmp[:, 1, 0:UP * n].rearrange("p (u n) -> p u n", n=n)
                    pool.tensor_tensor(t0, si, sm, ALU.mult)
                    link(pool.tensor_tensor(t1, si, cm, ALU.mult))
                    pool.tensor_tensor(tab[:, :, 0, lo:lo + n], co, cm, ALU.mult)
                    link(pool.tensor_tensor(tab[:, :, 1, lo:lo + n], co, sm, ALU.mult))
                    pool.tensor_tensor(tab[:, :, 0, lo:lo + n], tab[:, :, 0, lo:lo + n], t0, ALU.subtract)
                    link(pool.tensor_tensor(tab[:, :, 1, lo:lo + n], tab[:, :, 1, lo:lo + n], t1, ALU.add))
                pool.dma_start(tab_d[us].rearrange("u p c n -> p u c n"), tab).then_inc(tab_stored, 16)
            pool.wait_ge(mats_done, 2)
            for ri in range(2):
                pool.dma_start(R_d[:, 0:UP, ri, :], cA[:, ri, 0:UP, GH:(CH + 1) * GH]).then_inc(mats_stored, 16)
                pool.dma_start(R_d[:, UP:NU, ri, :], cA[:, ri, UP:NU, 0:CH * GH]).then_inc(mats_stored, 16)
            pool.wait_ge(K_done, 1)
            for s in range(CH):
                pool.dma_start(M_d[s * GH:(s + 1) * GH, :, :],
                               Kfull[:, :, (CH - 1 - s) * GH:(2 * CH - 1 - s) * GH]).then_inc(mats_stored, 16)
            pool.wait_ge(mats_stored, 16 * 12)

            pool.wait_ge(turn_ps, turns_before(NBLK))
            pool.wait_ge(qk_done, TPB * NBLK)
            pool.wait_ge(cc_out, 16)
            pool.wait_ge(cb_out, 16)

            def load_unit(u):
                if u >= 2:
                    pool.wait_ge(unit_done, u - 1)
                pool.dma_start(ust[:, u % 2, 0:2 * P].rearrange("p (c m) -> p c m", m=P), drvT_d[u])\
                    .then_inc(ust_in[u % 2], 16)
                pool.dma_start(ust[:, u % 2, 2 * P:].rearrange("p (c m) -> p c m", m=NCHUNK), tab_d[u])\
                    .then_inc(ust_in[u % 2], 16)

            def conv_piece(n):
                h, q = n // 4, n % 4
                lo, hi = q * 512, (q + 1) * 512
                v = mixT[:, 2 + h]
                acc, t = ctmp[:, 0], ctmp[:, 1]
                w = [pk("conv_w", 3 * h + j, 1) for j in range(3)]
                if n == 0:
                    pool.wait_ge(kv_ps, TPB * NBLK)
                lo1 = max(lo, 1)
                hi1 = min(hi, SEQ - 1)
                pool.tensor_scalar(acc, v[:, lo:hi], w[1], 1.0, ALU.mult, ALU.mult)
                link(pool.tensor_scalar(t[:, lo1 - lo:512], v[:, lo1 - 1:hi - 1], w[0], 1.0, ALU.mult, ALU.mult))
                link(pool.tensor_tensor(acc[:, lo1 - lo:512], acc[:, lo1 - lo:512], t[:, lo1 - lo:512], ALU.add))
                link(pool.tensor_scalar(t[:, 0:hi1 - lo], v[:, lo + 1:hi1 + 1], w[2], 1.0, ALU.mult, ALU.mult))
                link(pool.tensor_tensor(acc[:, 0:hi1 - lo], acc[:, 0:hi1 - lo], t[:, 0:hi1 - lo], ALU.add))
                pool.tensor_tensor(mixT[:, h, lo:hi], mixT[:, h, lo:hi], acc, ALU.mult).then_inc(conv_done, 1)
                pool.wait_ge(conv_done, n + 1)

            load_unit(0)
            load_unit(1)
            for g in range(NGRP):
                pool.wait_ge(rden_done, g + 1)
                n = n_keys(g)
                for j in range(QPK):
                    p = Pb[:, (g % 2) * QPK + j, 0:n]
                    ins = pool.tensor_scalar(p, p, rden[:, g % 2, j:j + 1], 1.0, ALU.mult, ALU.mult)
                ins.then_inc(P_done, 1)
                if g < 8:
                    conv_piece(g)
                if g % 2 == 1 and g // 2 >= 1 and g // 2 + 1 < NU:
                    load_unit(g // 2 + 1)
            pool.wait_ge(gT_ps, 4)
            for q in range(4):
                pool.memset(y[:, 4 * q:4 * q + 4], 0.0).then_inc(y_clear, 1)

        @block.scalar
        def _(act):
            steps = [0]

            def link(ins):
                steps[0] += 1
                ins.then_inc(act_step, 1)
                act.wait_ge(act_step, steps[0])

            act.wait_ge(pack_in, 16)
            act.activation(silu_c[:, :, :], pk("c").rearrange("p (k j) -> p k j", j=2), ACT.Silu).then_inc(silu_done, 1)
            act.wait_ge(args_done, 1)
            act.activation(SM[3], SM[0], ACT.Sin).then_inc(trig_done, 1)
            act.activation(SM[5], SM[0], ACT.Sin, scale=0.5).then_inc(trig_done, 1)
            for q in range(8):
                act.wait_ge(drvT_ps, q + 1)
                if q >= 2:
                    act.wait_ge(drvT_stored[q % 2], 16 * (q // 2))
                act.activation(drvT_st[:, q % 2], PS[1 + q % 2][:, :], ACT.Copy).then_inc(drvT_out, 1)
                act.wait_ge(drvT_out, q + 1)
                ri, u0 = q // 4, 4 * (q % 4)
                act.dma_start(drvT_d[u0:u0 + 4, :, ri, :].rearrange("u p m -> p u m"),
                              drvT_st[:, q % 2].rearrange("p (u m) -> p u m", m=P)).then_inc(drvT_stored[q % 2], 16)

            act.wait_ge(unit_cs, 1)

            def norm(b):
                act.wait_ge(x_in[b % 2], 16 * (b // 2 + 1))
                if b >= 2:
                    act.wait_ge(x_scaled, b - 1)
                for t in range(TPB):
                    link(act.activation(junk, xs[:, b % 2, t], ACT.Square, accum_out=ss[:, b % 2, t:t + 1]))
                act.activation(ss[:, b % 2], ss[:, b % 2], ACT.Sqrt, scale=1.0 / D, bias=eps[:, :]).then_inc(std_done, 1)

            norm(0)
            for b in range(NBLK):
                if b + 1 < NBLK:
                    norm(b + 1)
                tok = slice((b - 1) * BLK, b * BLK)
                if b >= 1:
                    for h in range(2):
                        n = 2 * (b - 1) + h
                        act.wait_ge(cx_ps, n + 1)
                        if n >= 1:
                            act.wait_ge(cc_out, n)
                        act.activation(xtmp, PS[2][:, 0:BLK], ACT.Copy).then_inc(cx_out, 1)
                        act.wait_ge(cb_ps, n + 1)
                        act.activation(mixT[:, h, tok], PS[4][:, 0:BLK], ACT.Copy).then_inc(cb_out, 1)
                act.wait_ge(u_ps, b + 1)
                if b >= 1:
                    act.wait_ge(turn_ps, turns_before(b - 1) + 4)
                act.activation(uT, PS[4][:, :].rearrange("p (a b) -> p a b", b=BLK), ACT.Copy).then_inc(u_out, 1)
                for t in range(TPB):
                    m = TPB * b + t
                    if m >= 1:
                        act.wait_ge(qk_done, m)
                    if b >= 1:
                        act.wait_ge(q_out, m - TPB + 1)
                        act.activation(sq[:, 0:8], PS[5][:, :].rearrange("p (h d) -> p h d", d=HD),
                                       ACT.Square).then_inc(q_sq, 1)
                    act.wait_ge(k_out, m + 1)
                    act.activation(sq[:, 8:10], PS[6][:, 0:P].rearrange("p (h d) -> p h d", d=HD),
                                   ACT.Square).then_inc(k_sq, 1)
                    act.activation(V[:, m], PS[6][:, P:2 * P], ACT.Copy).then_inc(v_out, 1)
                    act.wait_ge(hs_done, m + 1)
                    act.activation(hstd[:, :], hs[:, :], ACT.Sqrt, scale=1.0 / HD, bias=eps[:, :]).then_inc(hstd_done, 1)

            for g in range(NGRP + 1):
                if g < NGRP:
                    half = n_keys(g) // 2
                    for j in range(QPK):
                        H = QPK * g + j
                        act.wait_ge(negm_done, H + 1)
                        if g >= 2:
                            act.wait_ge(pt_ps, pt_before(g - 1))
                        src = banks[:, 2 * (H % 2):2 * (H % 2) + 2, 0:half]
                        act.activation(Pb[:, (g % 2) * QPK + j, 0:2 * half].rearrange("p (a b) -> p a b", b=half), src,
                                       ACT.Exp, bias=negm[:, g % 2, j:j + 1], scale=SCALE,
                                       accum_out=rs[:, g % 2, j:j + 1]).then_inc(exp_done, 1)
                    act.wait_ge(es_in, g + 1)
                    act.activation(esink[:, g % 2], esink[:, g % 2], ACT.Exp).then_inc(es_done, 1)
                if g >= 1:
                    for J in range(pt_before(g - 1), pt_before(g)):
                        if J % 2 == 1:
                            act.wait_ge(pt_ps, J + 1)
                            if J >= 2:
                                act.wait_ge(pv_ps, J - 1)
                            act.activation(PT[:, 1], PS[5], ACT.Copy).then_inc(pt_act, 1)
                if g < 2 * NU:
                    u, ri = g // 2, g % 2
                    act.wait_ge(xr_ps, g + 1)
                    if u >= 1:
                        act.wait_ge(rotated, u)
                    if u < UP:
                        act.activation(rot[:, ri], PS[7][:, 0:NCHUNK], ACT.Copy).then_inc(xr_out, 1)
                    else:
                        act.activation(rot[:, ri, 0:CCTX], PS[7][:, 0:CCTX][:, ::-1], ACT.Copy)
                        act.activation(rot[:, ri, CCTX:NCHUNK], PS[7][:, CCTX:NCHUNK][:, ::-1], ACT.Copy)\
                            .then_inc(xr_out, 1)
            for r in range(8):
                act.wait_ge(y_ps, r + 1)
                dst = Yc[:, r // 4].rearrange("p t (a s q h) -> p a q s t h", a=2, q=2, h=GH)
                src = PS[r].rearrange("p (s t h) -> p s t h", t=CH, h=GH)
                act.activation(dst[:, (r // 2) % 2, r % 2], src, ACT.Gelu_apprx_tanh).then_inc(y_out, 1)
            for w in range(8):
                act.wait_ge(z_ps, w + 1)
                if w >= 2:
                    act.wait_ge(glu_done, w - 1)
                act.activation(th[:, w % 2], PS[w], ACT.Tanh, scale=0.5, bias=hbglu[:, w % 2:w % 2 + 1]).then_inc(z_out, 1)
            for pp in range(NPP):
                act.wait_ge(hm_done, pp + 1)
                if pp >= 2:
                    act.wait_ge(x2_scaled, pp - 1)
                for t in range(TPB):
                    link(act.activation(junk2, hm[:, t], ACT.Square, accum_out=ss[:, pp % 2, t:t + 1]))
                act.activation(ss[:, pp % 2], ss[:, pp % 2], ACT.Sqrt, scale=1.0 / D, bias=eps[:, :]).then_inc(std2_done, 1)
            act.wait_ge(lg_out, NPP)
            act.activation(lgt, lgt, ACT.Sigmoid).then_inc(sig_done, 1)

            def silu(it, s):
                n = it * 12 + s
                act.wait_ge(hg_ps, n + 1)
                if not (type(it) is int and n < 2):
                    act.wait_ge(h_done, it * 12 + (s - 1))
                act.activation(sl[:, s % 2], PS[s % 2], ACT.Silu).then_inc(sl_out, 1)

            for s in range(12):
                silu(0, s)
            with act.Fori(1, NE // 3) as it:
                for s in range(12):
                    silu(it, s)

        @block.vector
        def _(dve):
            steps = [0]

            def link(ins):
                steps[0] += 1
                ins.then_inc(dve_step, 1)
                dve.wait_ge(dve_step, steps[0])

            def tt(o, x, z, op):
                return dve.tensor_tensor(o, x, z, op)

            dve.memset(eps[:, :], EPS)
            dve.wait_ge(pack_in, 16)
            dve.tensor_scalar(nsink[:, :], pk("sink"), -1.0, None, ALU.mult)
            dve.tensor_scalar(hbglu[:, :], pk("b_glu"), 0.5, None, ALU.mult)
            rr, am, e_, sn, cs, sh = SM[0], SM[1], SM[2], SM[3], SM[4], SM[5]
            w = SM[6].rearrange("p a b -> p (a b)")
            dt, la, lo_, t0, t1, nr, ni, rd, kr, ki = (w[:, NU * i:NU * (i + 1)] for i in range(10))

            def exact_exp(o, x, n, bits):
                link(dve.tensor_scalar(n, x, 1.0 / math.log(2.0), ROUND, ALU.mult, ALU.add))
                link(dve.tensor_scalar(n, n, ROUND, None, ALU.subtract))
                for part in (LN2_A, LN2_B):
                    link(dve.scalar_tensor_tensor(out=x, in0=n, scalar=-part, in1=x, op0=ALU.mult, op1=ALU.add))
                link(dve.tensor_scalar(o, x, 1.0 / math.factorial(8), None, ALU.mult))
                for j in range(7, 0, -1):
                    link(dve.scalar_tensor_tensor(out=o, in0=o, scalar=1.0 / math.factorial(j), in1=x,
                                                  op0=ALU.add, op1=ALU.mult))
                dve.tensor_scalar(o, o, 1.0, None, ALU.add)
                link(dve.tensor_scalar(n, n, -127.0, 128.0, ALU.max, ALU.min))
                link(dve.tensor_scalar(n, n, 127.0, 2.0 ** 23, ALU.add, ALU.mult))
                link(dve.tensor_copy(bits, n))
                link(tt(o, o, bits.bitcast(F32), ALU.mult))

            link(dve.tensor_copy(t0, pk("log_dt")))
            exact_exp(dt, t0, t1, nr.bitcast(mybir.dt.int32))
            tt(la, pk("lam_re"), dt, ALU.mult)
            link(tt(lo_, pk("lam_im"), dt, ALU.mult))

            def reduce_angle(x, n):
                link(dve.tensor_scalar(n, x, INV_2PI, ROUND, ALU.mult, ALU.add))
                link(dve.tensor_scalar(n, n, ROUND, None, ALU.subtract))
                for part in (PI_A, PI_B):
                    link(dve.scalar_tensor_tensor(out=x, in0=n, scalar=-part, in1=x, op0=ALU.mult, op1=ALU.add))
                return dve.scalar_tensor_tensor(out=x, in0=n, scalar=-PI_C, in1=x, op0=ALU.mult, op1=ALU.add)

            link(reduce_angle(lo_, t0))
            mult = pk("mults").unsqueeze(1).to_broadcast([P, NU, NM])
            tt(rr, lo_.unsqueeze(2).to_broadcast([P, NU, NM]), mult, ALU.mult)
            link(tt(am, la.unsqueeze(2).to_broadcast([P, NU, NM]), mult, ALU.mult))
            flat = [s.rearrange("p a b -> p (a b)") for s in (rr, cs)]
            reduce_angle(flat[0], flat[1]).then_inc(args_done, 1)
            link(tt(t0, pk("lam_re"), pk("lam_re"), ALU.mult))
            link(tt(t1, pk("lam_im"), pk("lam_im"), ALU.mult))
            link(tt(t0, t0, t1, ALU.add))
            link(dve.reciprocal(rd, t0))
            three = "p (u n) -> p u n"
            exact_exp(e_[:, :, 0:NPOW], am[:, :, 0:NPOW], tmpA[:, 0:NU * NPOW].rearrange(three, n=NPOW),
                      tmpB[:, 0:NU * NPOW].rearrange(three, n=NPOW).bitcast(mybir.dt.int32))
            dve.wait_ge(trig_done, 2)
            link(tt(cs, sh, sh, ALU.mult))
            dve.tensor_scalar(cs, cs, -2.0, 1.0, ALU.mult, ALU.add).then_inc(unit_cs, 1)
            dve.wait_ge(unit_cs, 1)
            dve.tensor_copy(r8[:, :], e_[:, :, RISE + CH])
            pr, pi_ = am, sh
            tt(pr[:, :, 0:NPOW], e_[:, :, 0:NPOW], cs[:, :, 0:NPOW], ALU.mult)
            link(tt(pi_[:, :, 0:NPOW], e_[:, :, 0:NPOW], sn[:, :, 0:NPOW], ALU.mult))
            dve.tensor_copy(ni, pi_[:, :, RISE + 1])
            link(dve.tensor_scalar(nr, pr[:, :, RISE + 1], -1.0, None, ALU.add))
            lr, li = pk("lam_re"), pk("lam_im")
            tt(t0, nr, lr, ALU.mult)
            link(tt(t1, ni, li, ALU.mult))
            link(tt(kr, t0, t1, ALU.add))
            tt(t0, ni, lr, ALU.mult)
            link(tt(t1, nr, li, ALU.mult))
            link(tt(ki, t0, t1, ALU.subtract))
            tt(kr, kr, rd, ALU.mult)
            link(tt(ki, ki, rd, ALU.mult))

            def b3(v, n):
                return v.unsqueeze(2).to_broadcast([P, v.shape[1], n])

            dve.wait_ge(raw_in, 16)
            v0 = tmpA[:, 0:256].rearrange("p (u h) -> p u h", h=GH)
            v1 = tmpB[:, 0:256].rearrange("p (u h) -> p u h", h=GH)
            for ri, (x, z, op) in enumerate(((0, 1, ALU.subtract), (1, 0, ALU.add))):
                tt(v0, raw[:, x], b3(kr, GH), ALU.mult)
                link(tt(v1, raw[:, z], b3(ki, GH), ALU.mult))
                link(tt(bbar[:, ri], v0, v1, op))

            def cmul(o_re, o_im, x_re, x_im, z_re, z_im, n, negate):
                tA = tmpA[:, 0:UP * n * GH].rearrange("p (u n h) -> p u n h", n=n, h=GH)
                tB = tmpB[:, 0:UP * n * GH].rearrange("p (u n h) -> p u n h", n=n, h=GH)

                def pw(v):
                    return v.unsqueeze(3).to_broadcast([P, UP, n, GH])

                def vec(v):
                    return v.unsqueeze(2).to_broadcast([P, UP, n, GH])

                tt(tA, pw(x_re), vec(z_re), ALU.mult)
                link(tt(tB, pw(x_im), vec(z_im), ALU.mult))
                link(tt(o_re, tA, tB, ALU.subtract))
                tt(tA, pw(x_re), vec(z_im), ALU.mult)
                link(tt(tB, pw(x_im), vec(z_re), ALU.mult))
                if negate:
                    link(dve.tensor_scalar(tA, tA, -1.0, None, ALU.mult))
                    return tt(o_im, tA, tB, ALU.subtract)
                return tt(o_im, tA, tB, ALU.add)

            for d in range(2):
                us = slice(d * UP, (d + 1) * UP)
                lo = 1 if d == 0 else RISE
                o = [drv[:, ri, us].rearrange("p u (s h) -> p u s h", h=GH) for ri in range(2)]
                cmul(o[0], o[1], pr[:, us, lo:lo + CH], pi_[:, us, lo:lo + CH], bbar[:, 0, us], bbar[:, 1, us], CH,
                     False).then_inc(drv_done, 1)
                dve.wait_ge(drv_done, d + 1)
            for d in range(2):
                us = slice(d * UP, (d + 1) * UP)
                lo = RISE if d == 0 else 0
                o = [cA[:, ri, us].rearrange("p u (s h) -> p u s h", h=GH) for ri in range(2)]
                cmul(o[0], o[1], pr[:, us, lo:lo + CH + 1], pi_[:, us, lo:lo + CH + 1], raw[:, 2, us], raw[:, 3, us],
                     CH + 1, True).then_inc(mats_done, 1)
                dve.wait_ge(mats_done, d + 1)
            dve.wait_ge(wmod_used, 4)
            mp = PS[0][:, 0:4 * KD].rearrange("p (m j) -> p m j", j=2)
            tt(shift1[:, :, :], mp[:, 0:KD], b3(pk("b_mod", 0, KD), 2), ALU.add)
            link(tt(scale1[:, :, :], mp[:, KD:2 * KD], b3(pk("b_mod", KD, KD), 2), ALU.add))
            link(dve.tensor_scalar(scale1[:, :, :], scale1[:, :, :], 1.0, None, ALU.add))
            tt(scale1[:, :, :], scale1[:, :, :], b3(pk("norm1"), 2), ALU.mult).then_inc(mod1_done, 1)
            dve.wait_ge(mod1_done, 1)
            dve.wait_ge(drvT_ps, 8)
            for q in range(8):
                dve.wait_ge(K_ps, q + 1)
                for gi in range(2):
                    bank = PS[3 + 2 * (q % 2) + gi][0:GH, :]
                    g = 2 * q + gi
                    dve.tensor_copy(Kfull[:, g, P:KW], bank[:, GH:P])
                    link(dve.tensor_copy(Kfull[:, g, 0:P], bank[:, P:2 * P]))
                    ins = tt(Kfull[:, g, P - GH:P], Kfull[:, g, P - GH:P], bank[:, 0:GH], ALU.add)
                ins.then_inc(K_out, 1)
            dve.wait_ge(K_out, 8)
            dve.wait_ge(ident_in, 16)
            skip = tmpA[0:GH, 0:NG * GH].rearrange("p (g h) -> p g h", h=GH)
            link(tt(skip, ident[0:GH, 0:GH].unsqueeze(1).to_broadcast([GH, NG, GH]),
                    pk("d_skip")[0:GH, :].unsqueeze(2).to_broadcast([GH, NG, GH]), ALU.mult))
            tt(Kfull[:, :, P - GH:P], Kfull[:, :, P - GH:P], skip, ALU.add).then_inc(K_done, 1)
            dve.wait_ge(mats_stored, 16 * 12)
            dve.wait_ge(tab_stored, 32)
            for i in range(2):
                dve.wait_ge(drvT_stored[i], 16 * 4)

            def scale_x(b):
                dve.wait_ge(std_done, b + 1)
                link(dve.reciprocal(rstd[:, :], ss[:, b % 2]))
                for t in range(TPB):
                    ins = dve.tensor_scalar(xs[:, b % 2, t], xs[:, b % 2, t], rstd[:, t:t + 1], None, ALU.mult)
                ins.then_inc(x_scaled, 1)
                dve.wait_ge(x_scaled, b + 1)

            def modulate_xT(b):
                if b >= 2:
                    dve.wait_ge(kv_ps, TPB * (b - 1))
                j = 1 if b == 0 else 0
                for q in range(4):
                    dve.wait_ge(xn_ps, 4 * b + q + 1)
                    for i in range(2):
                        k = 2 * q + i
                        ins = dve.tensor_scalar(xnT[:, b % 2, k], PS[q % 2][:, i * BLK:(i + 1) * BLK],
                                                scale1[:, k, j:j + 1], shift1[:, k, j:j + 1], ALU.mult, ALU.add)
                    ins.then_inc(xn_out, 1)

            def take_turns(b):
                base = turns_before(b)

                for i in range(4):
                    dve.wait_ge(turn_ps, base + i + 1)
                    if i == 0 and b >= 1:
                        dve.wait_ge(turn_out, base)
                    src = PS[7 - i % 2][0:CB, :].rearrange("p (s g h) -> p s g h", s=2, h=GH)
                    dst = Uc[:, :, 2 * i:2 * i + 2, :].rearrange("p g s h -> p s g h")
                    dve.tensor_copy(dst, src).then_inc(turn_out, 1)
                i = 4
                if b >= 1:
                    for t in range(TPB):
                        tile = TPB * (b - 1) + t
                        dve.wait_ge(turn_ps, base + i + 1)
                        dst = mixT[:, 4:8, tile * P:(tile + 1) * P]
                        dve.tensor_copy(dst, PS[7 - i % 2][:, :].rearrange("p (j q) -> p j q", q=P)).then_inc(turn_out, 1)
                        i += 1
                dve.wait_ge(turn_ps, base + i + 1)
                dve.tensor_copy(kT[:, b * BLK:(b + 1) * BLK], PS[7 - i % 2][:, 0:BLK]).then_inc(turn_out, 1)
                i += 1
                dve.wait_ge(turn_ps, base + i + 1)
                if b >= 2:
                    dve.wait_ge(U_stored[b % 2], 16 * (b // 2))
                dve.tensor_copy(U_st[:, b % 2], PS[7 - i % 2][:, :]).then_inc(turn_out, 1)

            def head_norm(b, t):
                m = TPB * b + t
                h0 = 8 if b == 0 else 0
                if b >= 1:
                    dve.wait_ge(q_ps, m - TPB + 1)
                    tt(qg[:, 0:8], PS[5][:, :].rearrange("p (h d) -> p h d", d=HD),
                       pk("q_g").unsqueeze(1).to_broadcast([P, 8, HD]), ALU.mult).then_inc(q_out, 1)
                dve.wait_ge(kv_ps, m + 1)
                tt(qg[:, 8:10], PS[6][:, 0:P].rearrange("p (h d) -> p h d", d=HD),
                   pk("k_g").unsqueeze(1).to_broadcast([P, 2, HD]), ALU.mult).then_inc(k_out, 1)
                dve.wait_ge(k_sq, m + 1)
                if b == 0:
                    dve.memset(hs[:, 0:8], 1.0)
                dve.tensor_reduce(hs[:, h0:10], sq[:, h0:10], AX.X, ALU.add).then_inc(hs_done, 1)
                dve.wait_ge(hstd_done, m + 1)
                link(dve.reciprocal(hrs[:, :], hstd[:, :]))
                rs3 = hrs[:, h0:10].unsqueeze(2).to_broadcast([P, 10 - h0, HD])
                if b == 0:
                    tt(qkr[:, t, 512:640].rearrange("p (h d) -> p h d", d=HD), qg[:, 8:10], rs3,
                       ALU.mult).then_inc(qk_done, 1)
                    dve.wait_ge(qk_done, m + 1)
                    return
                if t == 0:
                    dve.wait_ge(turn_ps, turns_before(b))
                    dve.wait_ge(rope_in[b % 2], 16 * ((b + 1) // 2))
                link(tt(qg, qg, rs3, ALU.mult))
                cosv = rope[:, b % 2, t, 0:HD].unsqueeze(1).to_broadcast([P, 10, HD])
                tt(rc, qg, cosv, ALU.mult)
                halves = "p h (a f i) -> p h a f i"
                sv = sq.rearrange(halves, a=2, f=2)
                qv = qg.rearrange(halves, a=2, f=2)
                nv = rope[:, b % 2, t, HD:2 * HD].rearrange("p (a f i) -> p a f i", a=2, f=2)
                for f in range(2):
                    last = tt(sv[:, :, :, f], qv[:, :, :, 1 - f], nv[:, :, f].unsqueeze(1).to_broadcast([P, 10, 2, 16]),
                              ALU.mult)
                link(last)
                tt(qkr[:, t].rearrange("p (h d) -> p h d", d=HD), rc, sq, ALU.add).then_inc(qk_done, 1)
                dve.wait_ge(qk_done, m + 1)

            scale_x(0)
            modulate_xT(0)
            for b in range(NBLK):
                if b + 1 < NBLK:
                    scale_x(b + 1)
                    modulate_xT(b + 1)
                if b >= 1:
                    tok = slice((b - 1) * BLK, b * BLK)
                    for h in range(2):
                        n = 2 * (b - 1) + h
                        dve.wait_ge(cc_ps, n + 1)
                        dve.wait_ge(cx_out, n + 1)
                        tt(mixT[:, 2 + h, tok], PS[3][:, 0:BLK], xtmp, ALU.mult).then_inc(cc_out, 1)
                    take_turns(b - 1)
                for t in range(TPB):
                    head_norm(b, t)
            take_turns(NBLK - 1)

            def rotate(u):
                dve.wait_ge(xr_out, 2 * u + 2)
                dve.wait_ge(ust_in[u % 2], 32 * (u // 2 + 1))
                x = [rot[:, i] for i in range(6)]
                c, s_ = ust[:, u % 2, 256:256 + NCHUNK], ust[:, u % 2, 256 + NCHUNK:]
                tt(x[2], c, x[0], ALU.mult)
                link(tt(x[3], s_, x[1], ALU.mult))
                tt(x[4], x[2], x[3], ALU.add)
                link(tt(x[5], c, x[1], ALU.mult))
                link(tt(x[3], s_, x[0], ALU.mult))
                tt(x[5], x[5], x[3], ALU.subtract).then_inc(rotated, 1)
                dve.wait_ge(rotated, u + 1)
                decay = r8[:, u:u + 1].to_broadcast([P, NCHUNK])
                dve.tensor_tensor_scan(x[2], decay, x[4], 0.0, ALU.mult, ALU.add)
                link(dve.tensor_tensor_scan(x[3], decay, x[5], 0.0, ALU.mult, ALU.add))

            def unrotate(u):
                x = [rot[:, i, CCTX - 1:NCHUNK - 1] for i in range(6)]
                c, s_ = (ust[:, u % 2, 256 + i * NCHUNK + CCTX - 1:256 + (i + 1) * NCHUNK - 1] for i in range(2))
                if u == 6:
                    dve.wait_ge(conv_done, 8)
                if u == 7:
                    dve.wait_ge(m2_ps, 8)
                st = [S[:, u, ri] if u < UP else S[:, u, ri][:, ::-1] for ri in range(2)]
                tt(x[4], c, x[2], ALU.mult)
                link(tt(x[5], s_, x[3], ALU.mult))
                link(tt(st[0], x[4], x[5], ALU.subtract))
                tt(x[4], c, x[3], ALU.mult)
                link(tt(x[5], s_, x[2], ALU.mult))
                tt(st[1], x[4], x[5], ALU.add).then_inc(unit_done, 1)
                dve.wait_ge(unit_done, u + 1)

            for g in range(NGRP + 1):
                if g < NGRP:
                    half = n_keys(g) // 2
                    for j in range(QPK):
                        H = QPK * g + j
                        dve.wait_ge(s_ps, H + 1)
                        src = banks[:, 2 * (H % 2):2 * (H % 2) + 2, 0:half]
                        if g >= 2:
                            dve.wait_ge(es_done, g - 1)
                        link(dve.tensor_reduce(mx[:, g % 2, j:j + 1], src, AX.XY, ALU.max))
                        head = QPK * (g % 2) + j
                        dve.tensor_scalar(negm[:, g % 2, j:j + 1], mx[:, g % 2, j:j + 1], -SCALE,
                                          nsink[:, head:head + 1], ALU.mult, ALU.min).then_inc(negm_done, 1)
                    dve.wait_ge(negm_done, QPK * (g + 1))
                    tt(esink[:, g % 2], pk("sink", QPK * (g % 2), QPK), negm[:, g % 2], ALU.add).then_inc(es_in, 1)
                if g >= 1:
                    for J in range(pt_before(g - 1), pt_before(g)):
                        if J % 2 == 0:
                            dve.wait_ge(pt_ps, J + 1)
                            if J >= 2:
                                dve.wait_ge(pv_ps, J - 1)
                            dve.tensor_copy(PT[:, 0], PS[4]).then_inc(pt_dve, 1)
                    if g % 2 == 0:
                        i = g // 2 - 1
                        dve.wait_ge(pv_ps, pt_before(g))
                        dve.tensor_copy(mixT[:, 4:8, i * P:(i + 1) * P],
                                        PS[6].rearrange("p (j q) -> p j q", q=P)).then_inc(o_out, 1)
                if g < NGRP:
                    dve.wait_ge(es_done, g + 1)
                    if g >= 2:
                        dve.wait_ge(P_done, g - 1)
                    link(tt(rden[:, g % 2], rs[:, g % 2], esink[:, g % 2], ALU.add))
                    dve.reciprocal(rden[:, g % 2], rden[:, g % 2]).then_inc(rden_done, 1)
                if g >= 2:
                    (rotate if g % 2 == 0 else unrotate)(g // 2 - 1)
                if g % 2 == 0 and g // 2 < 8:
                    i = g // 2
                    dve.wait_ge(m2_ps, i + 1)
                    dve.wait_ge(bias_in, 32)
                    if i in (0, 1, 6, 7):
                        dst = (g1bc if i < 2 else g2bc)[:, (i % 2) * 512:(i % 2 + 1) * 512]
                        tt(dst, PS[7], dst, ALU.add).then_inc(m2_out, 1)
                    else:
                        src = PS[7][:, 0:8].rearrange("p (c j) -> p c j", j=2)[:, :, 0]
                        tt(mod2[:, 4 * (i - 2):4 * (i - 1)], src, pk("b_mod", 4 * (i + 4), 4), ALU.add).then_inc(m2_out, 1)
            unrotate(NU - 1)
            dve.wait_ge(conv_done, 8)
            for z in range(8):
                ct, half, tq = z // 4, (z // 2) % 2, z % 2
                dve.wait_ge(yt_ps, z + 1)
                dst = mixT[:, 2 + half, ct * 1024:(ct + 1) * 1024].rearrange("p (c t) -> p t c", t=CH)
                dve.tensor_copy(dst[:, 4 * tq:4 * tq + 4], PS[z].rearrange("p (t c) -> p t c", c=P)).then_inc(yt_out, 1)
            for w in range(8):
                tb, half = w // 2, w % 2
                dve.wait_ge(z_out, w + 1)
                link(dve.tensor_scalar(th[:, half], th[:, half], 0.5, 0.5, ALU.mult, ALU.add))
                dve.wait_ge(z_ps, 2 * tb + 2)
                v = mixT[:, 2 + half, tb * 512:(tb + 1) * 512]
                tt(v, v, th[:, half], ALU.mult).then_inc(glu_done, 1)
            link(dve.tensor_scalar(scale2[:, :], mod2[:, KD:2 * KD], 1.0, None, ALU.add))
            link(tt(scale2[:, :], scale2[:, :], pk("norm2"), ALU.mult))

            def add_mix(pp):
                if pp >= 1:
                    dve.wait_ge(h_stored, 16 * pp)
                for r in range(4):
                    t, half = r // 2, slice((r % 2) * 512, (r % 2 + 1) * 512)
                    dve.wait_ge(o2_ps, 4 * pp + r + 1)
                    tt(hm[:, t, half], PS[r], g1bc[:, half], ALU.mult).then_inc(o2_out, 1)
                dve.wait_ge(o2_out, 4 * (pp + 1))
                dve.wait_ge(xo_in[pp % 2], 16 * (pp // 2 + 1))
                tt(hm, hm, xo[:, pp % 2], ALU.add).then_inc(hm_done, 1)
                dve.wait_ge(std2_done, pp + 1)
                link(dve.reciprocal(rstd[:, :], ss[:, pp % 2]))
                for t in range(TPB):
                    ins = dve.tensor_scalar(xo[:, pp % 2, t], hm[:, t], rstd[:, t:t + 1], None, ALU.mult)
                ins.then_inc(x2_scaled, 1)
                dve.wait_ge(x2_scaled, pp + 1)

            add_mix(0)
            for pp in range(NPP):
                if pp + 1 < NPP:
                    add_mix(pp + 1)
                for q in range(4):
                    dve.wait_ge(t2_ps, 4 * pp + q + 1)
                    for i in range(2):
                        k = 2 * q + i
                        ins = dve.tensor_scalar(tT[:, k, pp * BLK:(pp + 1) * BLK], PS[4 + q % 2][:, i * BLK:(i + 1) * BLK],
                                                scale2[:, k:k + 1], mod2[:, k:k + 1], ALU.mult, ALU.add)
                    ins.then_inc(t2_out, 1)
                dve.wait_ge(lg_ps, pp + 1)
                dve.tensor_copy(lgt[:, TPB * pp:TPB * (pp + 1)], PS[6 + pp % 2][:, 0:TPB * NR]
                                .rearrange("p (t r) -> p t r", r=NR)).then_inc(lg_out, 1)
            biased, above, equal, rank, sel, gates = rt
            dve.wait_ge(sig_done, 1)
            dve.wait_ge(o2_ps, 4 * NPP)
            link(tt(biased, lgt, pk("r_bias").unsqueeze(1).to_broadcast([P, NTILE, NR]), ALU.add))
            for t in range(NTILE):
                last = dve.max(top8[:, t], biased[:, t])
            link(last)
            fourth = top8[:, :, TOPK - 1:TOPK].to_broadcast([P, NTILE, NR])
            tt(above, biased, fourth, ALU.is_gt)
            link(tt(equal, biased, fourth, ALU.is_equal))
            link(dve.tensor_reduce(rsm[:, 0], above, AX.X, ALU.add))
            link(dve.tensor_scalar(rsm[:, 1], rsm[:, 0], -1.0, float(TOPK), ALU.mult, ALU.add))
            dve.wait_ge(restart_in, 16)
            one = "p t r -> p (t r)"
            link(dve.tensor_tensor_scan(rank.rearrange(one), restart, equal.rearrange(one), 0.0, ALU.mult, ALU.add))
            link(tt(rank, rank, rsm[:, 1].unsqueeze(2).to_broadcast([P, NTILE, NR]), ALU.is_le))
            link(tt(sel, equal, rank, ALU.mult))
            link(tt(sel, sel, above, ALU.add))
            link(tt(sel, sel, lgt, ALU.mult))
            link(dve.tensor_reduce(rsm[:, 2], sel, AX.X, ALU.add))
            link(dve.reciprocal(rsm[:, 3], rsm[:, 2]))
            link(tt(gates, sel, rsm[:, 3].unsqueeze(2).to_broadcast([P, NTILE, NR]), ALU.mult))
            dve.tensor_scalar(gates, gates, ROUTED, None, ALU.mult).then_inc(gates_done, 1)
            dve.wait_ge(h_stored, 16 * NPP)
            dve.wait_ge(x2_scaled, NPP)
            link(dve.memset(gT[NR:NE, :], 1.0))
            for q in range(4):
                dve.wait_ge(gT_ps, q + 1)
                dve.tensor_copy(gT[0:NR, q * 512:(q + 1) * 512], PS[q][0:NR, :]).then_inc(gT_out, 1)

            def gate_up(it, s):
                n = it * 12 + s
                tb = s % TB
                dve.wait_ge(sl_out, n + 1)
                dve.wait_ge(hu_ps, n + 1)
                tt(sl[:, s % 2], sl[:, s % 2], PS[2 + s % 2], ALU.mult).then_inc(hu_out, 1)
                dve.wait_ge(hu_out, n + 1)
                dve.wait_ge(gbc_in[tb], it * 48 + 16 * (s // TB + 1))
                if not (type(it) is int and s < 2):
                    dve.wait_ge(yd_ps, it * 96 + 8 * (s - 1))
                tt(hT[:, s % 2], sl[:, s % 2], gbc[:, tb], ALU.mult).then_inc(h_done, 1)

            def add_down(it, s):
                for r in range(8):
                    t, half = 4 * (s % TB) + r // 2, slice((r % 2) * 512, (r % 2 + 1) * 512)
                    dve.wait_ge(yd_ps, it * 96 + (8 * s + r + 1))
                    tt(y[:, t, half], y[:, t, half], PS[4 + r % 4], ALU.add).then_inc(yd_out, 1)

            def three_experts(it):
                for s in range(12):
                    gate_up(it, s)
                    if s >= 1:
                        add_down(it, s - 1)
                add_down(it, 11)

            dve.wait_ge(y_clear, 4)
            three_experts(0)
            with dve.Fori(1, NE // 3) as it:
                three_experts(it)
            dve.wait_ge(yd_out, 8 * 4 * NE)
            for q in range(8):
                dve.wait_ge(hfin_in[q // 2], 16)
                tiles = y[:, 2 * q:2 * q + 2]
                link(tt(tiles, tiles, g2bc.unsqueeze(1).to_broadcast([P, 2, D]), ALU.mult))
                tt(tiles, tiles, hfin[:, 2 * q:2 * q + 2], ALU.add).then_inc(fin_dve, 1)

        @block.tensor
        def _(pe):
            pe.wait_ge(silu_done, 1)
            for n in range(4):
                pe.wait_ge(wmod_in[n % 2], 16 * (n // 2 + 1))
                for cb in range(4):
                    col = 2 * (4 * n + cb)
                    for k in range(KD):
                        mm = pe.matmul(PS[0][:, col:col + 2], wmod[:, n % 2, k, cb * P:(cb + 1) * P], silu_c[:, k, :],
                                       start=(k == 0), stop=(k == KD - 1))
                mm.then_inc(wmod_used, 1)
            pe.wait_ge(ident_in, 16)
            pe.wait_ge(drv_done, 2)
            for q in range(8):
                if q >= 2:
                    pe.wait_ge(drvT_out, q - 1)
                for i in range(4):
                    ri, u = (4 * q + i) // NU, (4 * q + i) % NU
                    mm = pe.transpose(PS[1 + q % 2][:, i * P:(i + 1) * P], drv[:, ri, u], ident[:, :])
                mm.then_inc(drvT_ps, 1)
            pe.wait_ge(mats_done, 2)
            for q in range(8):
                if q >= 2:
                    pe.wait_ge(K_out, q - 1)
                for gi in range(2):
                    rows = slice(NS * gi, NS * gi + NS)
                    for d in range(2):
                        u = d * UP + q
                        cols = slice(d * P, (d + 1) * P)
                        lo = 0 if d == 0 else GH
                        for ri in range(2):
                            mm = pe.matmul(PS[3 + 2 * (q % 2) + gi][0:GH, cols], bbar[rows, ri, u], cA[rows, ri, u, lo:lo + P],
                                           start=(ri == 0), stop=(ri == 1))
                mm.then_inc(K_ps, 1)

            def turn_x(b):
                pe.wait_ge(x_scaled, b + 1)
                if b == 0:
                    pe.wait_ge(mod1_done, 1)
                    pe.wait_ge(drvT_out, 8)
                for q in range(4):
                    job = 4 * b + q
                    if job >= 2:
                        pe.wait_ge(xn_out, job - 1)
                    for i in range(2):
                        k = 2 * q + i
                        for t in range(TPB):
                            mm = pe.transpose(PS[q % 2][:, i * BLK + t * P:i * BLK + (t + 1) * P],
                                              xs[:, b % 2, t, k * P:(k + 1) * P], ident[:, :])
                    mm.then_inc(xn_ps, 1)

            def columns(bank, b, col):
                for k in range(KD):
                    mm = pe.matmul(bank, w_in[:, k, col:col + P], xnT[:, b % 2, k], start=(k == 0), stop=(k == KD - 1))
                return mm

            def turn(b):
                base = turns_before(b)
                pe.wait_ge(u_out, b + 1)
                if b == 0:
                    pe.wait_ge(K_out, 8)
                pe.wait_ge(k_out, TPB * (b + 1))
                pe.wait_ge(v_out, TPB * (b + 1))
                i = 0

                def bank():
                    if base + i >= 2:
                        pe.wait_ge(turn_out, base + i - 1)
                    return PS[7 - i % 2]

                for i in range(4):
                    o = bank()
                    for sl_ in range(2):
                        for h in range(2):
                            s = 2 * i + sl_
                            col = (2 * sl_ + h) * P
                            mm = pe.transpose(o[0:CB, col:col + P], uT[:, h, s:BLK:CH], ident[:, :])
                    mm.then_inc(turn_ps, 1)
                i = 4
                if b >= 1:
                    for t in range(TPB):
                        pe.wait_ge(qk_done, TPB * b + t + 1)
                        o = bank()
                        for j in range(QPK):
                            mm = pe.transpose(o[:, j * P:(j + 1) * P], qkr[:, t, j * P:(j + 1) * P], ident[:, :])
                        mm.then_inc(turn_ps, 1)
                        i += 1
                pe.wait_ge(qk_done, TPB * (b + 1))
                o = bank()
                for t in range(TPB):
                    mm = pe.transpose(o[:, t * P:(t + 1) * P], qkr[:, t, 512:640], ident[:, :])
                mm.then_inc(turn_ps, 1)
                i += 1
                pe.wait_ge(turn_out, base + 4)
                o = bank()
                for g in range(NG):
                    mm = pe.transpose(o[:, g * CB:(g + 1) * CB], Uc[:, g].rearrange("p s h -> p (s h)"),
                                      ident[0:CB, 0:CB])
                mm.then_inc(turn_ps, 1)

            turn_x(0)
            for b in range(NBLK):
                if b + 1 < NBLK:
                    turn_x(b + 1)
                pe.wait_ge(xn_out, 4 * (b + 1))
                if b >= 1:
                    if b == 1:
                        pe.wait_ge(w_in_in[2], 16)
                        pe.wait_ge(K_out, 8)
                    for h in range(2):
                        n = 2 * (b - 1) + h
                        if n >= 1:
                            pe.wait_ge(cx_out, n)
                        columns(PS[2][:, 0:BLK], b, h * P).then_inc(cx_ps, 1)
                        if n >= 1:
                            pe.wait_ge(cc_out, n)
                        columns(PS[3][:, 0:BLK], b, COL_C + h * P).then_inc(cc_ps, 1)
                        if n >= 1:
                            pe.wait_ge(cb_out, n)
                        if h == 0:
                            pe.wait_ge(u_out, b)
                        columns(PS[4][:, 0:BLK], b, COL_B + h * P).then_inc(cb_ps, 1)
                    turn(b - 1)
                if b == 0:
                    pe.wait_ge(w_in_in[0], 16)
                    pe.wait_ge(K_out, 8)
                else:
                    pe.wait_ge(cb_out, 2 * b)
                for h in range(2):
                    mm = columns(PS[4][:, h * BLK:(h + 1) * BLK], b, COL_U + h * P)
                mm.then_inc(u_ps, 1)
                if b == 0:
                    pe.wait_ge(w_in_in[1], 16)
                else:
                    pe.wait_ge(turn_out, turns_before(b))
                for t in range(TPB):
                    m = TPB * b + t
                    if b >= 1:
                        if m > TPB:
                            pe.wait_ge(q_sq, m - TPB)
                            pe.wait_ge(q_out, m - TPB)
                        for k in range(KD):
                            mm = pe.matmul(PS[5][:, :], xnT[:, b % 2, k, t * P:(t + 1) * P],
                                           w_in[:, k, COL_Q:COL_Q + 512], start=(k == 0), stop=(k == KD - 1))
                        mm.then_inc(q_ps, 1)
                    if m >= 1:
                        pe.wait_ge(k_out, m)
                        pe.wait_ge(v_out, m)
                    for k in range(KD):
                        mm = pe.matmul(PS[6][:, 0:2 * P], xnT[:, b % 2, k, t * P:(t + 1) * P],
                                       w_in[:, k, COL_K:N_IN], start=(k == 0), stop=(k == KD - 1))
                    mm.then_inc(kv_ps, 1)
            turn(NBLK - 1)

            pe.wait_ge(xn_out, 4 * NBLK)
            pe.wait_ge(cx_out, 16)
            pe.wait_ge(cc_out, 16)
            pe.wait_ge(u_out, NBLK)
            pe.wait_ge(q_sq, NTILE)
            pe.wait_ge(v_out, TPB * NBLK)
            pe.wait_ge(turn_out, turns_before(NBLK))
            pe.wait_ge(mask_done, 1)

            def scores(g):
                i, kv = g // 2, g % 2
                rows = slice(HD * kv, HD * (kv + 1))
                w = window(i)
                W, half = len(w) * P, n_keys(g) // 2
                k0 = CTX + w[0] * P
                lo = min(W, half)
                masks = []
                if i > 0:
                    masks.append((0, 0, P, 0))
                if i < NTILE - 1:
                    at = (len(w) - 1) * P
                    m = max(0, min(P, half - at))
                    if m:
                        masks.append((0, at, m, P))
                    if m < P:
                        masks.append((1, at + m - half, P - m, P + m))
                for j in range(QPK):
                    H = QPK * g + j
                    if H >= 2:
                        pe.wait_ge(exp_done, H - 1)
                    b = [PS[2 * (H % 2)], PS[2 * (H % 2) + 1]]
                    q = mixT[rows, 4 + j, i * P:(i + 1) * P]
                    mm = pe.matmul(b[1][:, W - half:W - half + CTX], q, kT[rows, 0:CTX], start=True, stop=True)
                    if W > half:
                        mm = pe.matmul(b[1][:, 0:W - half], q, kT[rows, k0 + half:k0 + W], start=True, stop=False)
                    in1 = [m for m in masks if m[0] == 1]
                    for n, (_, at, m, mc) in enumerate(in1):
                        mm = pe.matmul(b[1][:, at:at + m], identb[:, :], maskb[:, mc:mc + m], start=False,
                                       stop=(n == len(in1) - 1))
                    in0 = [m for m in masks if m[0] == 0]
                    mm = pe.matmul(b[0][:, 0:lo], q, kT[rows, k0:k0 + lo], start=True, stop=not in0)
                    for n, (_, at, m, mc) in enumerate(in0):
                        mm = pe.matmul(b[0][:, at:at + m], identb[:, :], maskb[:, mc:mc + m], start=False,
                                       stop=(n == len(in0) - 1))
                    mm.then_inc(s_ps, 1)

            def outputs(g):
                i, kv = g // 2, g % 2
                rows = slice(HD * kv, HD * (kv + 1))
                tiles = key_tiles(g)
                base = pt_before(g)
                pe.wait_ge(P_done, g + 1)
                if kv == 0 and i >= 1:
                    pe.wait_ge(o_out, i)

                def turn_p(n):
                    J = base + n
                    if J >= 2:
                        pe.wait_ge(pt_act if J % 2 else pt_dve, J // 2)
                    for j in range(QPK):
                        mm = pe.transpose(PS[4 + J % 2][:, j * P:(j + 1) * P],
                                          Pb[:, (g % 2) * QPK + j, tiles[n][0]:tiles[n][0] + P], ident[:, :])
                    mm.then_inc(pt_ps, 1)

                def times_v(n):
                    J = base + n
                    pe.wait_ge(pt_act if J % 2 else pt_dve, J // 2 + 1)
                    pe.matmul(PS[6][rows, :], V[:, tiles[n][1], HD * kv:HD * (kv + 1)], PT[:, J % 2],
                              start=(n == 0), stop=(n == len(tiles) - 1)).then_inc(pv_ps, 1)

                turn_p(0)
                for n in range(1, len(tiles)):
                    turn_p(n)
                    times_v(n - 1)
                times_v(len(tiles) - 1)

            def drive(u, ri):
                pe.wait_ge(ust_in[u % 2], 32 * (u // 2 + 1))
                if u + ri >= 1:
                    pe.wait_ge(xr_out, 2 * u + ri)
                if u == 0:
                    pe.wait_ge(U_in, 16)
                if ri == 1 and u < 8:
                    pe.wait_ge(m2_out, u + 1)
                for gi in range(2):
                    mm = pe.matmul(PS[7][NS * gi:NS * (gi + 1), 0:NCHUNK],
                                   ust[:, u % 2, ri * P + NS * gi:ri * P + NS * (gi + 1)], U[:, 2 * (u % UP) + gi, :],
                                   start=True, stop=True)
                mm.then_inc(xr_ps, 1)

            def modulation(i):
                pe.wait_ge(wm2_in, 16 * (i + 1))
                pe.wait_ge(xr_out, 2 * i + 1)
                if i in (0, 1, 6, 7):
                    for k in range(KD):
                        mm = pe.matmul(PS[7], silu_c[:, k, 0:1].to_broadcast([P, P]), wm2[:, k], start=(k == 0),
                                       stop=(k == KD - 1))
                else:
                    for cb in range(4):
                        for k in range(KD):
                            mm = pe.matmul(PS[7][:, 2 * cb:2 * cb + 2], wm2[:, k, cb * P:(cb + 1) * P], silu_c[:, k, :],
                                           start=(k == 0), stop=(k == KD - 1))
                mm.then_inc(m2_ps, 1)

            for g in range(NGRP + 1):
                if g < NGRP:
                    scores(g)
                    drive(g // 2, g % 2)
                if g >= 1:
                    outputs(g - 1)
                if g % 2 == 0 and g // 2 < 8:
                    modulation(g // 2)

            pe.wait_ge(mats_in, 32)
            pe.wait_ge(unit_done, NU)
            pe.wait_ge(exp_done, QPK * NGRP)
            pe.wait_ge(pt_dve, even_before(NGRP))
            pe.wait_ge(pt_act, odd_before(NGRP))
            pe.wait_ge(o_out, NTILE)
            pe.wait_ge(xr_out, 2 * NU)
            for r in range(8):
                ct, a8, par = r // 4, (r // 2) % 2, r % 2
                rows = slice(NS * par, NS * (par + 1))
                for sl_ in range(4):
                    g = 8 * a8 + 2 * sl_ + par
                    o = PS[r][:, sl_ * P:(sl_ + 1) * P]
                    pe.matmul(o, U[:, g, CCTX + ct * P:CCTX + (ct + 1) * P], M[:, g], start=True, stop=False)
                    for d in range(2):
                        for ri in range(2):
                            u = d * UP + g // 2
                            mm = pe.matmul(o, S[rows, u, ri, ct * P:(ct + 1) * P], R[rows, u, ri], start=False,
                                           stop=(d == 1 and ri == 1))
                mm.then_inc(y_ps, 1)
            for z in range(8):
                ct, half, tq = z // 4, (z // 2) % 2, z % 2
                pe.wait_ge(y_out, 4 * (ct + 1))
                for t in range(4):
                    mm = pe.transpose(PS[z][:, t * P:(t + 1) * P], Yc[:, ct, 4 * tq + t, half * P:(half + 1) * P], ident[:, :])
                mm.then_inc(yt_ps, 1)
            pe.wait_ge(wglu_in, 16)
            for w in range(8):
                tb, half = w // 2, w % 2
                pe.wait_ge(yt_out, 4 if tb < 2 else 8)
                for k in range(2):
                    mm = pe.matmul(PS[w], w_glu[:, k, half * P:(half + 1) * P], mixT[:, 2 + k, tb * 512:(tb + 1) * 512],
                                   start=(k == 0), stop=(k == 1))
                mm.then_inc(z_ps, 1)

            def project_out(pp):
                for r in range(4):
                    t, half = r // 2, slice((r % 2) * 512, (r % 2 + 1) * 512)
                    if pp >= 1:
                        pe.wait_ge(o2_out, 4 * (pp - 1) + r + 1)
                    for k in range(KD):
                        mm = pe.matmul(PS[r], mixT[:, k, (TPB * pp + t) * P:(TPB * pp + t + 1) * P], w_out[:, k, half],
                                       start=(k == 0), stop=(k == KD - 1))
                    mm.then_inc(o2_ps, 1)

            pe.wait_ge(z_out, 8)
            pe.wait_ge(glu_done, 8)
            pe.wait_ge(w_out_in, 16)
            pe.wait_ge(r_w_in, 16)
            project_out(0)
            for pp in range(NPP):
                if pp + 1 < NPP:
                    project_out(pp + 1)
                pe.wait_ge(x2_scaled, pp + 1)
                for q in range(4):
                    job = 4 * pp + q
                    if job >= 2:
                        pe.wait_ge(t2_out, job - 1)
                    for i in range(2):
                        k = 2 * q + i
                        for t in range(TPB):
                            mm = pe.transpose(PS[4 + q % 2][:, i * BLK + t * P:i * BLK + (t + 1) * P],
                                              xo[:, pp % 2, t, k * P:(k + 1) * P], ident[:, :])
                    mm.then_inc(t2_ps, 1)
                pe.wait_ge(t2_out, 4 * (pp + 1))
                if pp >= 2:
                    pe.wait_ge(lg_out, pp - 1)
                for t in range(TPB):
                    for k in range(KD):
                        mm = pe.matmul(PS[6 + pp % 2][:, t * NR:(t + 1) * NR],
                                       tT[:, k, (TPB * pp + t) * P:(TPB * pp + t + 1) * P], r_w[:, k, :],
                                       start=(k == 0), stop=(k == KD - 1))
                mm.then_inc(lg_ps, 1)
            pe.wait_ge(gates_done, 1)
            for q in range(4):
                for t in range(4):
                    mm = pe.transpose(PS[q][0:NR, t * P:(t + 1) * P], rt[5][:, 4 * q + t], ident[:, :])
                mm.then_inc(gT_ps, 1)

            def first_half(it, s):
                e, tb = s // TB, s % TB
                if tb == 0:
                    pe.wait_ge(wx_in[e], it * 16 + 16)
                for m, (ps, used) in enumerate(((hg_ps, sl_out), (hu_ps, hu_out))):
                    if not (type(it) is int and s < 2):
                        pe.wait_ge(used, it * 12 + (s - 1))
                    for k in range(KD):
                        mm = pe.matmul(PS[2 * m + s % 2], wx[e][:, m, k * EF:(k + 1) * EF], tT[:, k, tb * TW:(tb + 1) * TW],
                                       start=(k == 0), stop=(k == KD - 1))
                    mm.then_inc(ps, 1)

            def second_half(it, s):
                e = s // TB
                pe.wait_ge(h_done, it * 12 + (s + 1))
                for r in range(8):
                    t, half = r // 2, slice((r % 2) * 512, (r % 2 + 1) * 512)
                    if not (type(it) is int and 8 * s + r < 4):
                        pe.wait_ge(yd_out, it * 96 + (8 * s + r - 3))
                    pe.matmul(PS[4 + r % 4], hT[:, s % 2, t * P:(t + 1) * P], wx[e][:, 2, half], start=True, stop=True)\
                        .then_inc(yd_ps, 1)

            def three_experts(it):
                for s in range(12):
                    first_half(it, s)
                    if s >= 1:
                        second_half(it, s - 1)
                second_half(it, 11)

            pe.wait_ge(gT_out, 4)
            pe.wait_ge(t2_out, 4 * NPP)
            pe.wait_ge(lg_out, NPP)
            three_experts(0)
            with pe.Fori(1, NE // 3) as it:
                three_experts(it)


def lay_out(inputs):
    import numpy as np

    f = {k: np.asarray(v) for k, v in inputs.items()}
    f = {k: (v[0] if v.ndim and v.shape[0] == 1 and k not in ("x", "c") else v) for k, v in f.items()}

    def rows(v):
        return v.reshape(-1, P).T

    def same(v):
        return np.broadcast_to(v, (P, v.shape[-1]))

    def by_state(v):
        v = v.reshape((2, UP, 2, NS) + v.shape[3:])
        return np.ascontiguousarray(np.moveaxis(v, (2, 3), (0, 1))).reshape((P, NU) + v.shape[4:])

    cc = np.stack([f["c"][0], f["c_ctx"]])
    parts = {
        "c": np.ascontiguousarray(cc.reshape(2, KD, P).transpose(2, 1, 0)).reshape(P, 2 * KD),
        "b_mod": rows(f["b_mod"]), "norm1": rows(f["norm1_g"]), "norm2": rows(f["norm2_g"]),
        "lam_re": by_state(f["ssm_lam_re"]), "lam_im": by_state(f["ssm_lam_im"]),
        "log_dt": by_state(np.broadcast_to(f["ssm_log_dt"][:, :, None], (2, NG, NS))),
        "q_g": same(f["q_norm_g"]), "k_g": same(f["k_norm_g"]), "sink": same(f["attn_sink"]),
        "b_glu": rows(f["b_glu"]),
        "conv_w": np.ascontiguousarray(f["conv_w"].reshape(3, 2, P).transpose(2, 1, 0)).reshape(P, 6),
        "r_bias": same(f["router_bias"]),
        "mults": same(np.array(MULTS, np.float32)),
        "d_skip": np.concatenate([f["ssm_d"].reshape(NG, GH).T, np.zeros((P - GH, NG), np.float32)]),
    }
    pack = np.concatenate([parts[k] for k in PACK], axis=1)
    assert pack.shape == (P, N_PACK)
    raw = np.stack([by_state(f["ssm_b_re"]), by_state(f["ssm_b_im"]),
                    by_state(f["ssm_c_re"].transpose(0, 1, 3, 2)), by_state(f["ssm_c_im"].transpose(0, 1, 3, 2))], axis=1)
    w = f["w_in"]
    wq = w[:, 1024:1536].reshape(D, NKV, QPK, HD).transpose(0, 2, 1, 3).reshape(D, 512)
    w_in = np.concatenate([w[:, 0:COL_Q], wq, w[:, 1536:N_IN]], axis=1).reshape(KD, P, N_IN).transpose(1, 0, 2)
    wo = f["w_out"]
    wo_att = wo[512:1024].reshape(NKV, QPK, HD, D).transpose(1, 0, 2, 3).reshape(512, D)
    w_out = np.concatenate([wo[0:512], wo_att]).reshape(KD, P, D).transpose(1, 0, 2)
    pairs = HD // 4
    pos = np.arange(SEQ)
    freq = (np.float32(10000.0) ** (-np.arange(pairs, dtype=np.float32) / pairs)).astype(np.float32)
    ang = np.stack([(pos // 64).astype(np.float32)[:, None] * freq, (pos % 64).astype(np.float32)[:, None] * freq], axis=1)
    co, si = np.cos(ang), np.sin(ang)
    table = np.concatenate([np.stack([co, co], 2).reshape(SEQ, HD), np.stack([-si, si], 2).reshape(SEQ, HD)], axis=1)
    rope = table.reshape(NBLK - 1, TPB, P, 2 * HD).transpose(0, 2, 1, 3)
    q_, k_ = np.arange(P)[:, None], np.arange(P)[None, :]
    mask = np.concatenate([np.where(k_ >= q_, 0.0, -1e30), np.where(k_ <= q_, 0.0, -1e30)], axis=1)

    def experts(we, ws):
        both = np.concatenate([we.transpose(1, 0, 2), ws[None]])
        return both.reshape(NE, KD, P, EF).transpose(0, 2, 1, 3).reshape(NE, P, D)

    wx = np.stack([experts(f["w_exp_gate"], f["w_sh_gate"]), experts(f["w_exp_up"], f["w_sh_up"]),
                   np.concatenate([f["w_exp_down"], f["w_sh_down"][None]])], axis=2)
    arrays = {
        "pack": pack, "raw": raw.reshape(P, 4, NU, GH), "w_mod": f["w_mod"], "b_mod": f["b_mod"].reshape(6, D),
        "x": f["x"][0], "ctx": f["ctx"], "w_in": w_in, "w_glu": f["w_glu"], "w_out": w_out,
        "router_w": f["router_w"].reshape(KD, P, NR).transpose(1, 0, 2), "wx": wx, "rope": rope,
        "ident": np.eye(P, dtype=np.float32), 
        "mask": mask.astype(np.float32),
        "restart": same((np.arange(NTILE * NR) % NR != 0).astype(np.float32)),
    }
    return {k: np.ascontiguousarray(v) for k, v in arrays.items()}


def kernel(**inputs):
    import numpy as np
    import concourse.bacc as bacc
    from concourse.bass_utils import run_bass_kernel_spmd

    nc = bacc.Bacc("TRN2", target_bir_lowering=False, num_devices=1)
    arrays = lay_out(inputs)
    a = {k: nc.dram_tensor(f"in_{k}", v.shape, mybir.dt.from_np(v.dtype), kind="ExternalInput").ap()
         for k, v in arrays.items()}
    out = nc.dram_tensor("out", (SEQ, D), F32, kind="ExternalOutput").ap()
    block_kernel(nc, a, out)
    r = run_bass_kernel_spmd(nc, [{f"in_{k}": v for k, v in arrays.items()}], core_ids=[0])
    return r.results[0]["out"].reshape(1, SEQ, D)
```

```python
import math
from contextlib import ExitStack

import concourse.bass as bass
from concourse import mybir

F32 = mybir.dt.float32
BF16 = mybir.dt.bfloat16
U32 = mybir.dt.uint32
ALU = mybir.AluOpType
ACT = mybir.ActivationFunctionType
AX = mybir.AxisListType

P = 128
D = 1024
KD = D // P
SEQ, CTX = 2048, 256
BLK = 256
TPB = BLK // P
NBLK = (SEQ + CTX) // BLK
NTILE = SEQ // P
N_IN = 1792
COL_B, COL_C, COL_U, COL_Q, COL_K = 256, 512, 768, 1024, 1536
HD = 64
NHEAD, NKV, QPK = 8, 2, 4
SCALE = HD ** -0.5
EPS = 1e-6

CH = 8
NG, GH, NS = 16, 16, 64
UP = NG // 2
NU = 2 * UP
CCTX, CLAT = CTX // CH, SEQ // CH
NCHUNK = CCTX + CLAT
CB = BLK // CH
DOUBLINGS = 8
MULTS = list(range(CH, -1, -1)) + list(range(0, CH + 1)) + [CH << j for j in range(1, DOUBLINGS + 1)]
RISE, DBL = CH + 1, 2 * (CH + 1)
NPOW, NM = 2 * (CH + 1), len(MULTS)
KW = (2 * CH - 1) * GH
INV_2PI = 1.0 / (2.0 * math.pi)
PI_A = 6.28125
PI_B = 0.0019350051879882812
PI_C = 2.0 * math.pi - PI_A - PI_B
LN2_A = 0.693359375
LN2_B = math.log(2.0) - LN2_A
ROUND = 1.5 * 2.0 ** 23

NR, TOPK, ROUTED = 32, 4, 2.5
EF = 128
TB = 4
TW = SEQ // TB
STEPS = 6
LIVE = (SEQ * TOPK - NR) // P + NR
NT = -(-LIVE // STEPS) * STEPS
TURNS = NT // STEPS
SETS = 4

PACK = {}
_at = 0
for _name, _n in (("c", 2 * KD), ("b_mod", 48), ("norm1", KD), ("norm2", KD), ("lam_re", NU), ("lam_im", NU),
                  ("log_dt", NU), ("q_g", HD), ("k_g", HD), ("sink", NHEAD), ("b_glu", 2), ("conv_w", 6),
                  ("r_bias", NR), ("mults", NM), ("d_skip", NG)):
    PACK[_name] = (_at, _n)
    _at += _n
N_PACK = _at


def block_kernel(nc, a, out):
    ctx = ExitStack()
    with ctx:
        def sb(name, shape, dt=F32):
            return ctx.enter_context(nc.sbuf_tensor(name, shape, dt))

        def sem(name):
            return ctx.enter_context(nc.semaphore(name))

        arena = sb("arena", [P, 51584])

        def cut(at, *shape, rows=P):
            n = math.prod(shape)
            assert at + n <= 51584
            v = arena[0:rows, at:at + n]
            if len(shape) == 2:
                v = v.rearrange("p (a b) -> p a b", b=shape[1])
            if len(shape) == 3:
                v = v.rearrange("p (a b c) -> p a b c", b=shape[1], c=shape[2])
            return v

        mixT = cut(0, 8, SEQ)
        kT = cut(16384, SEQ + CTX)
        V = cut(18688, (SEQ + CTX) // P, P)
        tab = cut(0, UP, 2, NCHUNK)
        drv = cut(4608, 2, NU, P)
        Kfull = cut(4608, NG, KW, rows=GH)
        cA = cut(8704, 2, NU, (CH + 1) * GH)
        bbar = cut(13312, 2, NU, GH)
        raw = cut(13824, 4, NU, GH)
        tmpA = cut(14848, 1152)
        tmpB = cut(16000, 1152)
        drvT_st = cut(17152, 2, 512)
        ptmp = cut(18176, 2, UP * 128)
        mask_st = cut(18176, 2 * P)
        wmod = cut(39424, 2, KD, 512)
        SM = [cut(47616 + i * NU * NM, NU, NM) for i in range(7)]
        w_in = cut(20992, KD, N_IN)
        xs = cut(35328, 2, TPB, D)
        xnT = cut(39424, 2, KD, BLK)
        U_st = cut(43520, 2, NG * CB)
        Uc = cut(44544, NG, CH, GH, rows=CB)
        uT = cut(46592, 2, BLK)
        qg = cut(47104, 10, HD)
        sq = cut(47744, 10, HD)
        rc = cut(48384, 10, HD)
        qkr = cut(49024, TPB, 640)
        rope = cut(50304, 2, TPB, 2 * HD)
        junk = cut(50816, 512).bitcast(BF16)
        xtmp = cut(51328, BLK)
        wm2 = cut(29696, KD, 512)
        U = cut(20992, NG, NCHUNK)
        S = cut(25600, NU, 2, CLAT)
        ctmp = cut(28672, 2, 512)
        R = cut(33792, NU, 2, P)
        M = cut(37888, NG, P)
        Pb = cut(39936, 8, 640)
        PT = cut(45056, 2, 512)
        ust = cut(46080, 2, 832)
        rot = cut(47744, 6, NCHUNK)
        g1bc = cut(49472, D)
        g2bc = cut(50496, D)
        Yc = cut(16384, 2, CH, 256)
        w_glu = cut(20480, 2, 256)
        th = cut(20992, 2, 512)
        w_out = cut(39936, KD, D)
        tT = cut(20992, KD, SEQ)
        xo = cut(16384, 2, TPB, D)
        hm = cut(37376, TPB, D)
        lgt = cut(48128, NTILE, NR)
        r_w = cut(48640, KD, NR)
        junk2 = cut(48896, 512).bitcast(BF16)
        wsh = cut(37376, 3, D)
        hsh = cut(40448, TB, TW)
        rt = [cut(42496 + 512 * i, NTILE, NR) for i in range(9)]
        rsm = cut(47104, 4, NTILE)
        top8 = cut(47168, NTILE, 8)
        restart = cut(47296, NTILE * NR)
        counts = cut(47808, 4, NR)
        selb = cut(48896, NTILE * NR // 2).bitcast(BF16)
        earlier = cut(49152, P // 2).bitcast(BF16)
        ones_b = cut(49216, P // 2).bitcast(BF16)
        cst = cut(49472, 384)
        iota_p, iota_t, tile_no = cst[:, 0:P], cst[:, P:P + NT], cst[:, 224:240]
        row_no, ones, earlier_st = cst[:, 240:241], cst[:, 256:256 + NR], cut(49856, P)
        w_idx = cut(49984, NT).bitcast(U32)
        tok_idx = cut(50080, NT).bitcast(U32)
        slot_idx = cut(50176, NTILE, TOPK).bitcast(U32)
        gate_k = cut(50240, NTILE, TOPK)
        slot_f = cut(50304, NTILE, TOPK)
        slot_t = cut(50368, NTILE, TOPK)
        slot_p = cut(50432, NTILE, TOPK)
        reached = cut(0, NT, NR)
        oh_p = cut(16384, NTILE * P // 2).bitcast(BF16)
        oh_t = cut(18432, NTILE * 2 * NT // 2).bitcast(BF16)
        sl2 = cut(15360, 2, TW)
        y = cut(0, NTILE, D)
        wx = [cut(20992 + 3 * D * i, 3, D) for i in range(3)]
        xg = cut(30208, 3, D)
        xT = cut(33280, 2, KD, P)
        hb = cut(35328, D)
        slx = cut(16384, 2, P)
        hx = cut(16640, 2, P)
        yo = cut(42496, 3, D)
        gb = cut(20992, SETS * TOPK, D)

        ident = sb("ident", [P, P])
        identb = sb("identb", [P, P], BF16)
        maskb = sb("maskb", [P, 2 * P], BF16)
        pack = sb("pack", [P, N_PACK])

        def pk(name, lo=0, n=None):
            at, size = PACK[name]
            return pack[:, at + lo:at + lo + (n or size)]

        silu_c = sb("silu_c", [P, KD, 2])
        scale1 = sb("scale1", [P, KD, 2])
        shift1 = sb("shift1", [P, KD, 2])
        mod2 = sb("mod2", [P, 2 * KD])
        scale2 = sb("scale2", [P, KD])
        nsink = sb("nsink", [P, NHEAD])
        hbglu = sb("hbglu", [P, 2])
        eps = sb("eps", [P, 1])
        r8 = sb("r8", [P, NU])
        ss = sb("ss", [P, 2, TPB])
        rstd = sb("rstd", [P, TPB])
        hs = sb("hs", [P, 10])
        hstd = sb("hstd", [P, 10])
        hrs = sb("hrs", [P, 10])
        mx = sb("mx", [P, 2, QPK])
        negm = sb("negm", [P, 2, QPK])
        rs = sb("rs", [P, 2, QPK])
        esink = sb("esink", [P, 2, QPK])
        rden = sb("rden", [P, 2, QPK])
        tok_cur = [sb(f"tok_cur{i}", [P, 1], U32) for i in range(3)]
        w_cur = [sb(f"w_cur{i}", [P, 1], U32) for i in range(3)]
        slot_cur = [[sb(f"slot_cur{i}_{k}", [P, 1], U32) for k in range(TOPK)] for i in range(SETS)]

        banks = ctx.enter_context(nc.psum_tensor("banks", [P, 8, 512], F32))
        PS = [banks[:, i, :] for i in range(8)]

        drvT_d = nc.dram_tensor("drvT_d", [NU, P, 2, P], F32).ap()
        tab_d = nc.dram_tensor("tab_d", [NU, P, 2, NCHUNK], F32).ap()
        R_d = nc.dram_tensor("R_d", [P, NU, 2, P], F32).ap()
        M_d = nc.dram_tensor("M_d", [P, NG, P], F32).ap()
        U_d = nc.dram_tensor("U_d", [P, NG, NCHUNK], F32).ap()
        h_d = nc.dram_tensor("h_d", [NTILE, P, D], F32).ap()
        x2_d = nc.dram_tensor("x2_d", [SEQ, D], F32).ap()
        pair_d = nc.dram_tensor("pair_d", [NT * P, D], F32).ap()
        pair_t = pair_d.rearrange("(n p) d -> n p d", p=P)
        out_t = out.rearrange("(t p) d -> t p d", p=P)

        pack_in = sem("pack_in")
        ident_in = sem("ident_in")
        raw_in = sem("raw_in")
        mask_done = sem("mask_done")
        wmod_in = [sem(f"wmod_in{i}") for i in range(2)]
        wmod_used = sem("wmod_used")
        w_in_in = [sem(f"w_in_in{i}") for i in range(3)]
        x_in = [sem(f"x_in{i}") for i in range(2)]
        rope_in = [sem(f"rope_in{i}") for i in range(2)]
        silu_done = sem("silu_done")
        args_done = sem("args_done")
        trig_done = sem("trig_done")
        dve_step = sem("dve_step")
        act_step = sem("act_step")
        pool_step = sem("pool_step")
        unit_cs = sem("unit_cs")
        drv_done = sem("drv_done")
        drvT_ps = sem("drvT_ps")
        drvT_out = sem("drvT_out")
        drvT_stored = [sem(f"drvT_stored{i}") for i in range(2)]
        tab_stored = sem("tab_stored")
        mats_done = sem("mats_done")
        K_ps = sem("K_ps")
        K_out = sem("K_out")
        K_done = sem("K_done")
        mats_stored = sem("mats_stored")
        mod1_done = sem("mod1_done")
        std_done = sem("std_done")
        x_scaled = sem("x_scaled")
        xn_ps = sem("xn_ps")
        xn_out = sem("xn_out")
        cx_ps, cx_out = sem("cx_ps"), sem("cx_out")
        cc_ps, cc_out = sem("cc_ps"), sem("cc_out")
        cb_ps, cb_out = sem("cb_ps"), sem("cb_out")
        u_ps, u_out = sem("u_ps"), sem("u_out")
        q_ps, q_sq, q_out = sem("q_ps"), sem("q_sq"), sem("q_out")
        kv_ps, k_sq, v_out, k_out = sem("kv_ps"), sem("k_sq"), sem("v_out"), sem("k_out")
        hs_done = sem("hs_done")
        hstd_done = sem("hstd_done")
        qk_done = sem("qk_done")
        turn_ps, turn_out = sem("turn_ps"), sem("turn_out")
        U_stored = [sem(f"U_stored{i}") for i in range(2)]
        U_in = sem("U_in")
        mats_in = sem("mats_in")
        ust_in = [sem(f"ust_in{i}") for i in range(2)]
        wm2_in, m2_ps, m2_out = sem("wm2_in"), sem("m2_ps"), sem("m2_out")
        bias_in = sem("bias_in")
        s_ps, negm_done, exp_done = sem("s_ps"), sem("negm_done"), sem("exp_done")
        es_in, es_done, rden_done, P_done = sem("es_in"), sem("es_done"), sem("rden_done"), sem("P_done")
        pt_ps, pt_dve, pt_act = sem("pt_ps"), sem("pt_dve"), sem("pt_act")
        pv_ps, o_out = sem("pv_ps"), sem("o_out")
        xr_ps, xr_out, rotated, unit_done = sem("xr_ps"), sem("xr_out"), sem("rotated"), sem("unit_done")
        conv_done = sem("conv_done")
        y_ps, y_out, yt_ps, yt_out = sem("y_ps"), sem("y_out"), sem("yt_ps"), sem("yt_out")
        wglu_in, z_ps, z_out, glu_done = sem("wglu_in"), sem("z_ps"), sem("z_out"), sem("glu_done")
        w_out_in = sem("w_out_in")
        xo_in = [sem(f"xo_in{i}") for i in range(2)]
        o2_ps, o2_out, hm_done, h_stored = sem("o2_ps"), sem("o2_out"), sem("hm_done"), sem("h_stored")
        std2_done, x2_scaled, t2_ps, t2_out = sem("std2_done"), sem("x2_scaled"), sem("t2_ps"), sem("t2_out")
        lg_ps, lg_out, sig_done = sem("lg_ps"), sem("lg_out"), sem("sig_done")
        x2_stored, cst_in, wsh_in = sem("x2_stored"), sem("cst_in"), sem("wsh_in")
        consts_b, sel_done, pos_ps = sem("consts_b"), sem("sel_done"), sem("pos_ps")
        oh_t_done, tok_ps, idx_done = sem("oh_t_done"), sem("tok_ps"), sem("idx_done")
        reached_done = sem("reached_done")
        shg_ps, shu_ps, sh_act, prod_done = sem("shg_ps"), sem("shu_ps"), sem("sh_act"), sem("prod_done")
        shy_ps, ysh_out = sem("shy_ps"), sem("ysh_out")
        tok_cur_done, w_cur_done = sem("tok_cur_done"), sem("w_cur_done")
        xg_in = [sem(f"xg_in{i}") for i in range(3)]
        wx_in = [sem(f"wx_in{i}") for i in range(3)]
        xt_ps, xt_act, xt_dve = sem("xt_ps"), sem("xt_act"), sem("xt_dve")
        hg_ps, hu_ps, sl_out, h_done = (sem(n) for n in ("hg_ps", "hu_ps", "sl_out", "h_done"))
        yd_ps, yo_done = sem("yd_ps"), sem("yo_done")
        yo_stored = [sem(f"yo_stored{i}") for i in range(3)]
        hb_in, base_mul, base_done = sem("hb_in"), sem("base_mul"), sem("base_done")
        slot_cur_done, sum_step, out_stored = sem("slot_cur_done"), sem("sum_step"), sem("out_stored")
        gb_in = [sem(f"gb_in{i}") for i in range(SETS)]

        block = ctx.enter_context(nc.Block())

        def first(it):
            return type(it) is int and it == 0

        def turns(b):
            return 6 if b == 0 else 8

        def turns_before(b):
            return 0 if b == 0 else 6 + 8 * (b - 1)

        NGRP = 2 * NTILE
        NPP = NTILE // TPB

        def window(i):
            return list(range(max(0, i - 1), min(NTILE, i + 2)))

        def key_tiles(g):
            w = window(g // 2)
            return [(n * P, CTX // P + t) for n, t in enumerate(w)] + [(len(w) * P + c * P, c) for c in range(CTX // P)]

        def n_keys(g):
            return len(key_tiles(g)) * P

        def pt_before(g):
            return sum(len(key_tiles(x)) for x in range(g))

        def odd_before(g):
            return pt_before(g) // 2

        def even_before(g):
            return (pt_before(g) + 1) // 2

        @block.sync
        def _(sp):
            sp.dma_start(pack[:, :], a["pack"]).then_inc(pack_in, 16)
            sp.dma_start(raw, a["raw"]).then_inc(raw_in, 16)
            sp.dma_start(ident[:, :], a["ident"]).then_inc(ident_in, 16)
            sp.dma_start(mask_st, a["mask"]).then_inc(ident_in, 16)
            wm_src = a["w_mod"].rearrange("(k p) n -> p k n", p=P)

            def load_wmod(n):
                if n >= 2:
                    sp.wait_ge(wmod_used, n - 1)
                sp.dma_start(wmod[:, n % 2], wm_src[:, :, n * 512:(n + 1) * 512]).then_inc(wmod_in[n % 2], 16)

            def load_x(b):
                if b >= 2:
                    sp.wait_ge(xn_ps, 4 * (b - 1))
                src = a["ctx"] if b == 0 else a["x"][(b - 1) * BLK:b * BLK, :]
                sp.dma_start(xs[:, b % 2], src.rearrange("(t p) d -> p t d", p=P)).then_inc(x_in[b % 2], 16)

            load_wmod(0)
            load_wmod(1)
            load_x(0)
            for i, (lo, hi) in enumerate(((COL_U, COL_Q), (COL_Q, N_IN), (0, COL_U))):
                sp.dma_start(w_in[:, :, lo:hi], a["w_in"][:, :, lo:hi]).then_inc(w_in_in[i], 16)
            load_wmod(2)
            load_wmod(3)
            load_x(1)

            def store_U(b):
                sp.wait_ge(turn_out, turns_before(b + 1))
                sp.dma_start(U_d[:, :, b * CB:(b + 1) * CB], U_st[:, b % 2].rearrange("p (g c) -> p g c", c=CB)).then_inc(U_stored[b % 2], 16)

            for b in range(NBLK):
                if b >= 1:
                    if b >= 3:
                        sp.wait_ge(qk_done, TPB * (b - 1))
                    sp.dma_start(rope[:, b % 2], a["rope"][b - 1]).then_inc(rope_in[b % 2], 16)
                if b + 2 < NBLK:
                    load_x(b + 2)
                if b >= 1:
                    store_U(b - 1)
            store_U(NBLK - 1)

            sp.wait_ge(kv_ps, TPB * NBLK)
            sp.wait_ge(xn_ps, 4 * NBLK)
            sp.wait_ge(U_stored[0], 16 * 5)
            sp.wait_ge(U_stored[1], 16 * 4)
            sp.dma_start(U, U_d).then_inc(U_in, 16)

            def load_wm2(c):
                if c > 4:
                    sp.wait_ge(m2_ps, c - 4)
                sp.dma_start(wm2, wm_src[:, :, c * 512:(c + 1) * 512]).then_inc(wm2_in, 16)

            load_wm2(4)
            sp.wait_ge(turn_ps, turns_before(NBLK))
            sp.dma_start(g1bc, a["b_mod"][2:3, :].to_broadcast([P, D])).then_inc(bias_in, 16)
            sp.dma_start(g2bc, a["b_mod"][5:6, :].to_broadcast([P, D])).then_inc(bias_in, 16)
            load_wm2(5)
            sp.dma_start(R, R_d).then_inc(mats_in, 16)
            sp.dma_start(M, M_d).then_inc(mats_in, 16)
            for c in range(6, 12):
                load_wm2(c)
            sp.wait_ge(pv_ps, pt_before(NGRP))
            sp.dma_start(w_glu, a["w_glu"].rearrange("(k p) n -> p k n", p=P)).then_inc(wglu_in, 16)
            sp.wait_ge(unit_done, NU)
            sp.dma_start(w_out, a["w_out"]).then_inc(w_out_in, 16)
            sp.dma_start(r_w, a["router_w"]).then_inc(w_out_in, 16)

            def load_xo(pp):
                if pp < 2:
                    sp.wait_ge(yt_ps, 8)
                else:
                    sp.wait_ge(t2_ps, 4 * (pp - 1))
                sp.dma_start(xo[:, pp % 2], a["x"][pp * BLK:(pp + 1) * BLK, :].rearrange("(t p) d -> p t d", p=P))\
                    .then_inc(xo_in[pp % 2], 16)

            load_xo(0)
            load_xo(1)
            for pp in range(NPP):
                sp.wait_ge(hm_done, pp + 1)
                sp.dma_start(h_d[TPB * pp:TPB * (pp + 1)].rearrange("t p d -> p t d"), hm).then_inc(h_stored, 16)
                sp.wait_ge(x2_scaled, pp + 1)
                sp.dma_start(x2_d[pp * BLK:(pp + 1) * BLK, :].rearrange("(t p) d -> p t d", p=P), xo[:, pp % 2])\
                    .then_inc(x2_stored, 16)
                if pp + 2 < NPP:
                    sp.wait_ge(x2_stored, 16 * (pp + 1))
                    load_xo(pp + 2)
            sp.wait_ge(o2_ps, 4 * NPP)
            sp.dma_start(restart, a["restart"]).then_inc(cst_in, 16)
            sp.wait_ge(o2_out, 4 * NPP)
            sp.dma_start(cst, a["cst"][:, 0:384]).then_inc(cst_in, 16)
            sp.dma_start(earlier_st, a["cst"][:, 384:384 + P]).then_inc(cst_in, 16)
            sp.wait_ge(h_stored, 16 * NPP)
            sp.wait_ge(std2_done, NPP)
            sp.wait_ge(x2_scaled, NPP)
            sp.dma_start(wsh, a["w_sh"]).then_inc(wsh_in, 16)
            sp.wait_ge(shu_ps, TB)
            sp.wait_ge(prod_done, TB)

            def serve_turn(it):
                if not first(it):
                    sp.wait_ge(base_done, it)
                sp.dma_start(hb.unsqueeze(1), h_d[bass.ds(it, 1)].rearrange("n p d -> p n d")).then_inc(hb_in, 16)
                for s in range(STEPS):
                    sp.wait_ge(yo_done, it * (2 * STEPS) + 2 * (s + 1))
                    sp.dma_start(pair_t[bass.ds(it * STEPS + s, 1)].rearrange("n p d -> p n d"),
                                 yo[:, s % 3].unsqueeze(1)).then_inc(yo_stored[s % 3], 16)

            serve_turn(0)
            with sp.Fori(1, TURNS) as it:
                serve_turn(it)
            with sp.Fori(0, NTILE) as t:
                sp.wait_ge(sum_step, t * TOPK + TOPK)
                sp.dma_start(out_t[bass.ds(t, 1)].rearrange("n p d -> p n d"), y[:, bass.ds(t, 1), :])\
                    .then_inc(out_stored, 16)
            sp.wait_ge(out_stored, 16 * NTILE)

        @block.gpsimd
        def _(pool):
            steps = [0]

            def link(ins):
                steps[0] += 1
                ins.then_inc(pool_step, 1)
                pool.wait_ge(pool_step, steps[0])

            pool.wait_ge(ident_in, 32)
            pool.tensor_copy(identb[:, :], ident[:, :])
            pool.tensor_copy(maskb[:, :], mask_st).then_inc(mask_done, 1)
            pool.wait_ge(mask_done, 1)
            pool.wait_ge(trig_done, 2)
            pool.wait_ge(unit_cs, 1)
            cosm, sinm = SM[4], SM[3]
            for d in range(2):
                if d == 1:
                    pool.wait_ge(tab_stored, 16)
                us = slice(d * UP, (d + 1) * UP)
                pool.memset(tab[:, :, 0, 0:1], 1.0)
                pool.memset(tab[:, :, 1, 0:1], 0.0)
                pool.tensor_copy(tab[:, :, 0, 1:2], cosm[:, us, RISE + CH:RISE + CH + 1])
                link(pool.tensor_copy(tab[:, :, 1, 1:2], sinm[:, us, RISE + CH:RISE + CH + 1]))
                for j in range(1, DOUBLINGS + 1):
                    lo = 1 << j
                    n = min(lo, NCHUNK - lo)
                    co, si = tab[:, :, 0, 0:n], tab[:, :, 1, 0:n]
                    cm = cosm[:, us, DBL + j - 1:DBL + j].to_broadcast([P, UP, n])
                    sm = sinm[:, us, DBL + j - 1:DBL + j].to_broadcast([P, UP, n])
                    t0 = ptmp[:, 0, 0:UP * n].rearrange("p (u n) -> p u n", n=n)
                    t1 = ptmp[:, 1, 0:UP * n].rearrange("p (u n) -> p u n", n=n)
                    pool.tensor_tensor(t0, si, sm, ALU.mult)
                    link(pool.tensor_tensor(t1, si, cm, ALU.mult))
                    pool.tensor_tensor(tab[:, :, 0, lo:lo + n], co, cm, ALU.mult)
                    link(pool.tensor_tensor(tab[:, :, 1, lo:lo + n], co, sm, ALU.mult))
                    pool.tensor_tensor(tab[:, :, 0, lo:lo + n], tab[:, :, 0, lo:lo + n], t0, ALU.subtract)
                    link(pool.tensor_tensor(tab[:, :, 1, lo:lo + n], tab[:, :, 1, lo:lo + n], t1, ALU.add))
                pool.dma_start(tab_d[us].rearrange("u p c n -> p u c n"), tab).then_inc(tab_stored, 16)
            pool.wait_ge(mats_done, 2)
            for ri in range(2):
                pool.dma_start(R_d[:, 0:UP, ri, :], cA[:, ri, 0:UP, GH:(CH + 1) * GH]).then_inc(mats_stored, 16)
                pool.dma_start(R_d[:, UP:NU, ri, :], cA[:, ri, UP:NU, 0:CH * GH]).then_inc(mats_stored, 16)
            pool.wait_ge(K_done, 1)
            for s in range(CH):
                pool.dma_start(M_d[s * GH:(s + 1) * GH, :, :],
                               Kfull[:, :, (CH - 1 - s) * GH:(2 * CH - 1 - s) * GH]).then_inc(mats_stored, 16)
            pool.wait_ge(mats_stored, 16 * 12)

            pool.wait_ge(turn_ps, turns_before(NBLK))
            pool.wait_ge(qk_done, TPB * NBLK)
            pool.wait_ge(cc_out, 16)
            pool.wait_ge(cb_out, 16)

            def load_unit(u):
                if u >= 2:
                    pool.wait_ge(unit_done, u - 1)
                pool.dma_start(ust[:, u % 2, 0:2 * P].rearrange("p (c m) -> p c m", m=P), drvT_d[u])\
                    .then_inc(ust_in[u % 2], 16)
                pool.dma_start(ust[:, u % 2, 2 * P:].rearrange("p (c m) -> p c m", m=NCHUNK), tab_d[u])\
                    .then_inc(ust_in[u % 2], 16)

            def conv_piece(n):
                h, q = n // 4, n % 4
                lo, hi = q * 512, (q + 1) * 512
                v = mixT[:, 2 + h]
                acc, t = ctmp[:, 0], ctmp[:, 1]
                w = [pk("conv_w", 3 * h + j, 1) for j in range(3)]
                if n == 0:
                    pool.wait_ge(kv_ps, TPB * NBLK)
                lo1 = max(lo, 1)
                hi1 = min(hi, SEQ - 1)
                pool.tensor_scalar(acc, v[:, lo:hi], w[1], 1.0, ALU.mult, ALU.mult)
                link(pool.tensor_scalar(t[:, lo1 - lo:512], v[:, lo1 - 1:hi - 1], w[0], 1.0, ALU.mult, ALU.mult))
                link(pool.tensor_tensor(acc[:, lo1 - lo:512], acc[:, lo1 - lo:512], t[:, lo1 - lo:512], ALU.add))
                link(pool.tensor_scalar(t[:, 0:hi1 - lo], v[:, lo + 1:hi1 + 1], w[2], 1.0, ALU.mult, ALU.mult))
                link(pool.tensor_tensor(acc[:, 0:hi1 - lo], acc[:, 0:hi1 - lo], t[:, 0:hi1 - lo], ALU.add))
                pool.tensor_tensor(mixT[:, h, lo:hi], mixT[:, h, lo:hi], acc, ALU.mult).then_inc(conv_done, 1)
                pool.wait_ge(conv_done, n + 1)

            load_unit(0)
            load_unit(1)
            for g in range(NGRP):
                pool.wait_ge(rden_done, g + 1)
                n = n_keys(g)
                for j in range(QPK):
                    p = Pb[:, (g % 2) * QPK + j, 0:n]
                    ins = pool.tensor_scalar(p, p, rden[:, g % 2, j:j + 1], 1.0, ALU.mult, ALU.mult)
                ins.then_inc(P_done, 1)
                if g < 8:
                    conv_piece(g)
                if g % 2 == 1 and g // 2 >= 1 and g // 2 + 1 < NU:
                    load_unit(g // 2 + 1)
            pool.wait_ge(cst_in, 48)
            pool.wait_ge(std2_done, NPP)
            pool.memset(ones_b, 1.0)
            pool.tensor_copy(earlier, earlier_st).then_inc(consts_b, 1)
            pool.wait_ge(x2_stored, 16 * NPP)
            pool.wait_ge(t2_ps, 4 * NPP)

            def product(tb):
                pool.wait_ge(sh_act, tb + 1)
                pool.tensor_tensor(hsh[:, tb], hsh[:, tb], sl2[:, tb % 2], ALU.mult).then_inc(prod_done, 1)

            for tb in range(TB):
                product(tb)

            pool.wait_ge(idx_done, 1)
            pool.wait_ge(shg_ps, TB)
            pool.wait_ge(shu_ps, TB)

            def take_tok(it, s):
                if not (first(it) and s < 3):
                    pool.wait_ge(xt_ps, it * (2 * STEPS) + 2 * (s - 2))
                pool.tensor_copy(tok_cur[s % 3][:, :], tok_idx[:, bass.ds(it * STEPS + s, 1)]).then_inc(tok_cur_done, 1)

            def fetch(it, s):
                i, n = s % 3, it * STEPS + s
                pool.wait_ge(tok_cur_done, n + 1)
                if not (first(it) and s < 3):
                    pool.wait_ge(yd_ps, it * (2 * STEPS) + 2 * (s - 2))
                pool.tensor_copy(w_cur[i][:, :], w_idx[:, bass.ds(n, 1)]).then_inc(w_cur_done, 1)
                pool.indirect_dma_start(xg[:, i], None, x2_d, bass.IndirectOffsetOnAxis(ap=tok_cur[i][:, :], axis=0))\
                    .then_inc(xg_in[i], 16)
                pool.wait_ge(w_cur_done, n + 1)
                if not (type(n) is int and n == NT - 1):
                    take_tok(it, s + 1)
                pool.indirect_dma_start(wx[i].rearrange("p a b -> p (a b)"), None, a["w_exp"],
                                        bass.IndirectOffsetOnAxis(ap=w_cur[i][:, :], axis=0)).then_inc(wx_in[i], 16)

            def fetch_turn(it):
                for s in range(STEPS):
                    fetch(it, s)

            take_tok(0, 0)
            fetch_turn(0)
            with pool.Fori(1, TURNS - 1) as it:
                fetch_turn(it)
            fetch_turn(TURNS - 1)

            pool.wait_ge(yd_ps, 2 * NT)
            for i in range(3):
                pool.wait_ge(yo_stored[i], 16 * NT // 3)

            def take_slots(it, j):
                if not (type(it) is int and it * SETS + j < SETS):
                    pool.wait_ge(sum_step, it * (SETS * TOPK) + TOPK * (j + 1 - SETS))
                for k in range(TOPK):
                    ins = pool.tensor_copy(slot_cur[j % SETS][k][:, :], slot_idx[:, bass.ds(it * SETS + j, 1), k])
                ins.then_inc(slot_cur_done, 1)

            def gather_rows(it, j):
                t = it * SETS + j
                pool.wait_ge(slot_cur_done, t + 1)
                if not (type(t) is int and t == NTILE - 1):
                    take_slots(it, j + 1)
                for k in range(TOPK):
                    pool.indirect_dma_start(gb[:, TOPK * j + k], None, pair_d,
                                            bass.IndirectOffsetOnAxis(ap=slot_cur[j][k][:, :], axis=0))\
                        .then_inc(gb_in[j], 16)

            take_slots(0, 0)
            for j in range(SETS):
                gather_rows(0, j)
            with pool.Fori(1, NTILE // SETS - 1) as it:
                for j in range(SETS):
                    gather_rows(it, j)
            for j in range(SETS):
                gather_rows(NTILE // SETS - 1, j)

        @block.scalar
        def _(act):
            steps = [0]

            def link(ins):
                steps[0] += 1
                ins.then_inc(act_step, 1)
                act.wait_ge(act_step, steps[0])

            act.wait_ge(pack_in, 16)
            act.activation(silu_c[:, :, :], pk("c").rearrange("p (k j) -> p k j", j=2), ACT.Silu).then_inc(silu_done, 1)
            act.wait_ge(args_done, 1)
            act.activation(SM[3], SM[0], ACT.Sin).then_inc(trig_done, 1)
            act.activation(SM[5], SM[0], ACT.Sin, scale=0.5).then_inc(trig_done, 1)
            for q in range(8):
                act.wait_ge(drvT_ps, q + 1)
                if q >= 2:
                    act.wait_ge(drvT_stored[q % 2], 16 * (q // 2))
                act.activation(drvT_st[:, q % 2], PS[1 + q % 2][:, :], ACT.Copy).then_inc(drvT_out, 1)
                act.wait_ge(drvT_out, q + 1)
                ri, u0 = q // 4, 4 * (q % 4)
                act.dma_start(drvT_d[u0:u0 + 4, :, ri, :].rearrange("u p m -> p u m"),
                              drvT_st[:, q % 2].rearrange("p (u m) -> p u m", m=P)).then_inc(drvT_stored[q % 2], 16)

            act.wait_ge(unit_cs, 1)

            def norm(b):
                act.wait_ge(x_in[b % 2], 16 * (b // 2 + 1))
                if b >= 2:
                    act.wait_ge(x_scaled, b - 1)
                for t in range(TPB):
                    link(act.activation(junk, xs[:, b % 2, t], ACT.Square, accum_out=ss[:, b % 2, t:t + 1]))
                act.activation(ss[:, b % 2], ss[:, b % 2], ACT.Sqrt, scale=1.0 / D, bias=eps[:, :]).then_inc(std_done, 1)

            norm(0)
            for b in range(NBLK):
                if b + 1 < NBLK:
                    norm(b + 1)
                tok = slice((b - 1) * BLK, b * BLK)
                if b >= 1:
                    for h in range(2):
                        n = 2 * (b - 1) + h
                        act.wait_ge(cx_ps, n + 1)
                        if n >= 1:
                            act.wait_ge(cc_out, n)
                        act.activation(xtmp, PS[2][:, 0:BLK], ACT.Copy).then_inc(cx_out, 1)
                        act.wait_ge(cb_ps, n + 1)
                        act.activation(mixT[:, h, tok], PS[4][:, 0:BLK], ACT.Copy).then_inc(cb_out, 1)
                act.wait_ge(u_ps, b + 1)
                if b >= 1:
                    act.wait_ge(turn_ps, turns_before(b - 1) + 4)
                act.activation(uT, PS[4][:, :].rearrange("p (a b) -> p a b", b=BLK), ACT.Copy).then_inc(u_out, 1)
                for t in range(TPB):
                    m = TPB * b + t
                    if m >= 1:
                        act.wait_ge(qk_done, m)
                    if b >= 1:
                        act.wait_ge(q_out, m - TPB + 1)
                        act.activation(sq[:, 0:8], PS[5][:, :].rearrange("p (h d) -> p h d", d=HD),
                                       ACT.Square).then_inc(q_sq, 1)
                    act.wait_ge(k_out, m + 1)
                    act.activation(sq[:, 8:10], PS[6][:, 0:P].rearrange("p (h d) -> p h d", d=HD),
                                   ACT.Square).then_inc(k_sq, 1)
                    act.activation(V[:, m], PS[6][:, P:2 * P], ACT.Copy).then_inc(v_out, 1)
                    act.wait_ge(hs_done, m + 1)
                    act.activation(hstd[:, :], hs[:, :], ACT.Sqrt, scale=1.0 / HD, bias=eps[:, :]).then_inc(hstd_done, 1)

            for g in range(NGRP + 1):
                if g < NGRP:
                    half = n_keys(g) // 2
                    for j in range(QPK):
                        H = QPK * g + j
                        act.wait_ge(negm_done, H + 1)
                        if g >= 2:
                            act.wait_ge(pt_ps, pt_before(g - 1))
                        src = banks[:, 2 * (H % 2):2 * (H % 2) + 2, 0:half]
                        act.activation(Pb[:, (g % 2) * QPK + j, 0:2 * half].rearrange("p (a b) -> p a b", b=half), src,
                                       ACT.Exp, bias=negm[:, g % 2, j:j + 1], scale=SCALE,
                                       accum_out=rs[:, g % 2, j:j + 1]).then_inc(exp_done, 1)
                    act.wait_ge(es_in, g + 1)
                    act.activation(esink[:, g % 2], esink[:, g % 2], ACT.Exp).then_inc(es_done, 1)
                if g >= 1:
                    for J in range(pt_before(g - 1), pt_before(g)):
                        if J % 2 == 1:
                            act.wait_ge(pt_ps, J + 1)
                            if J >= 2:
                                act.wait_ge(pv_ps, J - 1)
                            act.activation(PT[:, 1], PS[5], ACT.Copy).then_inc(pt_act, 1)
                if g < 2 * NU:
                    u, ri = g // 2, g % 2
                    act.wait_ge(xr_ps, g + 1)
                    if u >= 1:
                        act.wait_ge(rotated, u)
                    if u < UP:
                        act.activation(rot[:, ri], PS[7][:, 0:NCHUNK], ACT.Copy).then_inc(xr_out, 1)
                    else:
                        act.activation(rot[:, ri, 0:CCTX], PS[7][:, 0:CCTX][:, ::-1], ACT.Copy)
                        act.activation(rot[:, ri, CCTX:NCHUNK], PS[7][:, CCTX:NCHUNK][:, ::-1], ACT.Copy)\
                            .then_inc(xr_out, 1)
            for r in range(8):
                act.wait_ge(y_ps, r + 1)
                dst = Yc[:, r // 4].rearrange("p t (a s q h) -> p a q s t h", a=2, q=2, h=GH)
                src = PS[r].rearrange("p (s t h) -> p s t h", t=CH, h=GH)
                act.activation(dst[:, (r // 2) % 2, r % 2], src, ACT.Gelu_apprx_tanh).then_inc(y_out, 1)
            for w in range(8):
                act.wait_ge(z_ps, w + 1)
                if w >= 2:
                    act.wait_ge(glu_done, w - 1)
                act.activation(th[:, w % 2], PS[w], ACT.Tanh, scale=0.5, bias=hbglu[:, w % 2:w % 2 + 1]).then_inc(z_out, 1)
            for pp in range(NPP):
                act.wait_ge(hm_done, pp + 1)
                if pp >= 2:
                    act.wait_ge(x2_scaled, pp - 1)
                for t in range(TPB):
                    link(act.activation(junk2, hm[:, t], ACT.Square, accum_out=ss[:, pp % 2, t:t + 1]))
                act.activation(ss[:, pp % 2], ss[:, pp % 2], ACT.Sqrt, scale=1.0 / D, bias=eps[:, :]).then_inc(std2_done, 1)
            act.wait_ge(lg_out, NPP)
            act.activation(lgt, lgt, ACT.Sigmoid).then_inc(sig_done, 1)

            act.wait_ge(o2_ps, 4 * NPP)
            act.wait_ge(x2_stored, 16 * NPP)
            for tb in range(TB):
                act.wait_ge(shg_ps, tb + 1)
                if tb >= 2:
                    act.wait_ge(prod_done, tb - 1)
                act.activation(sl2[:, tb % 2], PS[tb % 2], ACT.Silu)
                act.wait_ge(shu_ps, tb + 1)
                act.activation(hsh[:, tb], PS[2 + tb % 2], ACT.Copy).then_inc(sh_act, 1)
            act.wait_ge(reached_done, 1)
            act.wait_ge(prod_done, TB)
            for d in range(2 * NTILE):
                act.wait_ge(shy_ps, d + 1)
                act.activation(y[:, d // 2, (d % 2) * 512:(d % 2 + 1) * 512], PS[d % 4], ACT.Copy).then_inc(ysh_out, 1)

            def turned(it, s):
                n = it * STEPS + s
                act.wait_ge(xt_ps, it * (2 * STEPS) + 2 * s + 1)
                if not (first(it) and s < 2):
                    act.wait_ge(hu_ps, it * STEPS + (s - 1))
                for k in range(4):
                    ins = act.activation(xT[:, s % 2, k], PS[0][:, k * P:(k + 1) * P], ACT.Identity,
                                         scale=scale2[:, k:k + 1], bias=mod2[:, k:k + 1])
                ins.then_inc(xt_act, 1)

            def silu(it, s):
                act.wait_ge(hg_ps, it * STEPS + (s + 1))
                if not (first(it) and s < 2):
                    act.wait_ge(h_done, it * STEPS + (s - 1))
                act.activation(slx[:, s % 2], PS[4 + s % 2][:, 0:P], ACT.Silu).then_inc(sl_out, 1)

            turned(0, 0)
            for s in range(1, STEPS):
                turned(0, s)
                silu(0, s - 1)
            with act.Fori(1, TURNS) as it:
                for s in range(STEPS):
                    turned(it, s)
                    silu(it, s - 1)
            silu(TURNS - 1, STEPS - 1)

        @block.vector
        def _(dve):
            steps = [0]

            def link(ins):
                steps[0] += 1
                ins.then_inc(dve_step, 1)
                dve.wait_ge(dve_step, steps[0])

            def tt(o, x, z, op):
                return dve.tensor_tensor(o, x, z, op)

            dve.memset(eps[:, :], EPS)
            dve.wait_ge(pack_in, 16)
            dve.tensor_scalar(nsink[:, :], pk("sink"), -1.0, None, ALU.mult)
            dve.tensor_scalar(hbglu[:, :], pk("b_glu"), 0.5, None, ALU.mult)
            rr, am, e_, sn, cs, sh = SM[0], SM[1], SM[2], SM[3], SM[4], SM[5]
            w = SM[6].rearrange("p a b -> p (a b)")
            dt, la, lo_, t0, t1, nr, ni, rd, kr, ki = (w[:, NU * i:NU * (i + 1)] for i in range(10))

            def exact_exp(o, x, n, bits):
                link(dve.tensor_scalar(n, x, 1.0 / math.log(2.0), ROUND, ALU.mult, ALU.add))
                link(dve.tensor_scalar(n, n, ROUND, None, ALU.subtract))
                for part in (LN2_A, LN2_B):
                    link(dve.scalar_tensor_tensor(out=x, in0=n, scalar=-part, in1=x, op0=ALU.mult, op1=ALU.add))
                link(dve.tensor_scalar(o, x, 1.0 / math.factorial(8), None, ALU.mult))
                for j in range(7, 0, -1):
                    link(dve.scalar_tensor_tensor(out=o, in0=o, scalar=1.0 / math.factorial(j), in1=x,
                                                  op0=ALU.add, op1=ALU.mult))
                dve.tensor_scalar(o, o, 1.0, None, ALU.add)
                link(dve.tensor_scalar(n, n, -127.0, 128.0, ALU.max, ALU.min))
                link(dve.tensor_scalar(n, n, 127.0, 2.0 ** 23, ALU.add, ALU.mult))
                link(dve.tensor_copy(bits, n))
                link(tt(o, o, bits.bitcast(F32), ALU.mult))

            link(dve.tensor_copy(t0, pk("log_dt")))
            exact_exp(dt, t0, t1, nr.bitcast(mybir.dt.int32))
            tt(la, pk("lam_re"), dt, ALU.mult)
            link(tt(lo_, pk("lam_im"), dt, ALU.mult))

            def reduce_angle(x, n):
                link(dve.tensor_scalar(n, x, INV_2PI, ROUND, ALU.mult, ALU.add))
                link(dve.tensor_scalar(n, n, ROUND, None, ALU.subtract))
                for part in (PI_A, PI_B):
                    link(dve.scalar_tensor_tensor(out=x, in0=n, scalar=-part, in1=x, op0=ALU.mult, op1=ALU.add))
                return dve.scalar_tensor_tensor(out=x, in0=n, scalar=-PI_C, in1=x, op0=ALU.mult, op1=ALU.add)

            link(reduce_angle(lo_, t0))
            mult = pk("mults").unsqueeze(1).to_broadcast([P, NU, NM])
            tt(rr, lo_.unsqueeze(2).to_broadcast([P, NU, NM]), mult, ALU.mult)
            link(tt(am, la.unsqueeze(2).to_broadcast([P, NU, NM]), mult, ALU.mult))
            flat = [s.rearrange("p a b -> p (a b)") for s in (rr, cs)]
            reduce_angle(flat[0], flat[1]).then_inc(args_done, 1)
            link(tt(t0, pk("lam_re"), pk("lam_re"), ALU.mult))
            link(tt(t1, pk("lam_im"), pk("lam_im"), ALU.mult))
            link(tt(t0, t0, t1, ALU.add))
            link(dve.reciprocal(rd, t0))
            three = "p (u n) -> p u n"
            exact_exp(e_[:, :, 0:NPOW], am[:, :, 0:NPOW], tmpA[:, 0:NU * NPOW].rearrange(three, n=NPOW),
                      tmpB[:, 0:NU * NPOW].rearrange(three, n=NPOW).bitcast(mybir.dt.int32))
            dve.wait_ge(trig_done, 2)
            link(tt(cs, sh, sh, ALU.mult))
            dve.tensor_scalar(cs, cs, -2.0, 1.0, ALU.mult, ALU.add).then_inc(unit_cs, 1)
            dve.wait_ge(unit_cs, 1)
            dve.tensor_copy(r8[:, :], e_[:, :, RISE + CH])
            pr, pi_ = am, sh
            tt(pr[:, :, 0:NPOW], e_[:, :, 0:NPOW], cs[:, :, 0:NPOW], ALU.mult)
            link(tt(pi_[:, :, 0:NPOW], e_[:, :, 0:NPOW], sn[:, :, 0:NPOW], ALU.mult))
            dve.tensor_copy(ni, pi_[:, :, RISE + 1])
            link(dve.tensor_scalar(nr, pr[:, :, RISE + 1], -1.0, None, ALU.add))
            lr, li = pk("lam_re"), pk("lam_im")
            tt(t0, nr, lr, ALU.mult)
            link(tt(t1, ni, li, ALU.mult))
            link(tt(kr, t0, t1, ALU.add))
            tt(t0, ni, lr, ALU.mult)
            link(tt(t1, nr, li, ALU.mult))
            link(tt(ki, t0, t1, ALU.subtract))
            tt(kr, kr, rd, ALU.mult)
            link(tt(ki, ki, rd, ALU.mult))

            def b3(v, n):
                return v.unsqueeze(2).to_broadcast([P, v.shape[1], n])

            dve.wait_ge(raw_in, 16)
            v0 = tmpA[:, 0:256].rearrange("p (u h) -> p u h", h=GH)
            v1 = tmpB[:, 0:256].rearrange("p (u h) -> p u h", h=GH)
            for ri, (x, z, op) in enumerate(((0, 1, ALU.subtract), (1, 0, ALU.add))):
                tt(v0, raw[:, x], b3(kr, GH), ALU.mult)
                link(tt(v1, raw[:, z], b3(ki, GH), ALU.mult))
                link(tt(bbar[:, ri], v0, v1, op))

            def cmul(o_re, o_im, x_re, x_im, z_re, z_im, n, negate):
                tA = tmpA[:, 0:UP * n * GH].rearrange("p (u n h) -> p u n h", n=n, h=GH)
                tB = tmpB[:, 0:UP * n * GH].rearrange("p (u n h) -> p u n h", n=n, h=GH)

                def pw(v):
                    return v.unsqueeze(3).to_broadcast([P, UP, n, GH])

                def vec(v):
                    return v.unsqueeze(2).to_broadcast([P, UP, n, GH])

                tt(tA, pw(x_re), vec(z_re), ALU.mult)
                link(tt(tB, pw(x_im), vec(z_im), ALU.mult))
                link(tt(o_re, tA, tB, ALU.subtract))
                tt(tA, pw(x_re), vec(z_im), ALU.mult)
                link(tt(tB, pw(x_im), vec(z_re), ALU.mult))
                if negate:
                    link(dve.tensor_scalar(tA, tA, -1.0, None, ALU.mult))
                    return tt(o_im, tA, tB, ALU.subtract)
                return tt(o_im, tA, tB, ALU.add)

            for d in range(2):
                us = slice(d * UP, (d + 1) * UP)
                lo = 1 if d == 0 else RISE
                o = [drv[:, ri, us].rearrange("p u (s h) -> p u s h", h=GH) for ri in range(2)]
                cmul(o[0], o[1], pr[:, us, lo:lo + CH], pi_[:, us, lo:lo + CH], bbar[:, 0, us], bbar[:, 1, us], CH,
                     False).then_inc(drv_done, 1)
                dve.wait_ge(drv_done, d + 1)
            for d in range(2):
                us = slice(d * UP, (d + 1) * UP)
                lo = RISE if d == 0 else 0
                o = [cA[:, ri, us].rearrange("p u (s h) -> p u s h", h=GH) for ri in range(2)]
                cmul(o[0], o[1], pr[:, us, lo:lo + CH + 1], pi_[:, us, lo:lo + CH + 1], raw[:, 2, us], raw[:, 3, us],
                     CH + 1, True).then_inc(mats_done, 1)
                dve.wait_ge(mats_done, d + 1)
            dve.wait_ge(wmod_used, 4)
            mp = PS[0][:, 0:4 * KD].rearrange("p (m j) -> p m j", j=2)
            tt(shift1[:, :, :], mp[:, 0:KD], b3(pk("b_mod", 0, KD), 2), ALU.add)
            link(tt(scale1[:, :, :], mp[:, KD:2 * KD], b3(pk("b_mod", KD, KD), 2), ALU.add))
            link(dve.tensor_scalar(scale1[:, :, :], scale1[:, :, :], 1.0, None, ALU.add))
            tt(scale1[:, :, :], scale1[:, :, :], b3(pk("norm1"), 2), ALU.mult).then_inc(mod1_done, 1)
            dve.wait_ge(mod1_done, 1)
            dve.wait_ge(drvT_ps, 8)
            for q in range(8):
                dve.wait_ge(K_ps, q + 1)
                for gi in range(2):
                    bank = PS[3 + 2 * (q % 2) + gi][0:GH, :]
                    g = 2 * q + gi
                    dve.tensor_copy(Kfull[:, g, P:KW], bank[:, GH:P])
                    link(dve.tensor_copy(Kfull[:, g, 0:P], bank[:, P:2 * P]))
                    ins = tt(Kfull[:, g, P - GH:P], Kfull[:, g, P - GH:P], bank[:, 0:GH], ALU.add)
                ins.then_inc(K_out, 1)
            dve.wait_ge(K_out, 8)
            dve.wait_ge(ident_in, 32)
            skip = tmpA[0:GH, 0:NG * GH].rearrange("p (g h) -> p g h", h=GH)
            link(tt(skip, ident[0:GH, 0:GH].unsqueeze(1).to_broadcast([GH, NG, GH]),
                    pk("d_skip")[0:GH, :].unsqueeze(2).to_broadcast([GH, NG, GH]), ALU.mult))
            tt(Kfull[:, :, P - GH:P], Kfull[:, :, P - GH:P], skip, ALU.add).then_inc(K_done, 1)
            dve.wait_ge(mats_stored, 16 * 12)
            dve.wait_ge(tab_stored, 32)
            for i in range(2):
                dve.wait_ge(drvT_stored[i], 16 * 4)

            def scale_x(b):
                dve.wait_ge(std_done, b + 1)
                link(dve.reciprocal(rstd[:, :], ss[:, b % 2]))
                for t in range(TPB):
                    ins = dve.tensor_scalar(xs[:, b % 2, t], xs[:, b % 2, t], rstd[:, t:t + 1], None, ALU.mult)
                ins.then_inc(x_scaled, 1)
                dve.wait_ge(x_scaled, b + 1)

            def modulate_xT(b):
                if b >= 2:
                    dve.wait_ge(kv_ps, TPB * (b - 1))
                j = 1 if b == 0 else 0
                for q in range(4):
                    dve.wait_ge(xn_ps, 4 * b + q + 1)
                    for i in range(2):
                        k = 2 * q + i
                        ins = dve.tensor_scalar(xnT[:, b % 2, k], PS[q % 2][:, i * BLK:(i + 1) * BLK],
                                                scale1[:, k, j:j + 1], shift1[:, k, j:j + 1], ALU.mult, ALU.add)
                    ins.then_inc(xn_out, 1)

            def take_turns(b):
                base = turns_before(b)

                for i in range(4):
                    dve.wait_ge(turn_ps, base + i + 1)
                    if i == 0 and b >= 1:
                        dve.wait_ge(turn_out, base)
                    src = PS[7 - i % 2][0:CB, :].rearrange("p (s g h) -> p s g h", s=2, h=GH)
                    dst = Uc[:, :, 2 * i:2 * i + 2, :].rearrange("p g s h -> p s g h")
                    dve.tensor_copy(dst, src).then_inc(turn_out, 1)
                i = 4
                if b >= 1:
                    for t in range(TPB):
                        tile = TPB * (b - 1) + t
                        dve.wait_ge(turn_ps, base + i + 1)
                        dst = mixT[:, 4:8, tile * P:(tile + 1) * P]
                        dve.tensor_copy(dst, PS[7 - i % 2][:, :].rearrange("p (j q) -> p j q", q=P)).then_inc(turn_out, 1)
                        i += 1
                dve.wait_ge(turn_ps, base + i + 1)
                dve.tensor_copy(kT[:, b * BLK:(b + 1) * BLK], PS[7 - i % 2][:, 0:BLK]).then_inc(turn_out, 1)
                i += 1
                dve.wait_ge(turn_ps, base + i + 1)
                if b >= 2:
                    dve.wait_ge(U_stored[b % 2], 16 * (b // 2))
                dve.tensor_copy(U_st[:, b % 2], PS[7 - i % 2][:, :]).then_inc(turn_out, 1)

            def head_norm(b, t):
                m = TPB * b + t
                h0 = 8 if b == 0 else 0
                if b >= 1:
                    dve.wait_ge(q_ps, m - TPB + 1)
                    tt(qg[:, 0:8], PS[5][:, :].rearrange("p (h d) -> p h d", d=HD),
                       pk("q_g").unsqueeze(1).to_broadcast([P, 8, HD]), ALU.mult).then_inc(q_out, 1)
                dve.wait_ge(kv_ps, m + 1)
                tt(qg[:, 8:10], PS[6][:, 0:P].rearrange("p (h d) -> p h d", d=HD),
                   pk("k_g").unsqueeze(1).to_broadcast([P, 2, HD]), ALU.mult).then_inc(k_out, 1)
                dve.wait_ge(k_sq, m + 1)
                if b == 0:
                    dve.memset(hs[:, 0:8], 1.0)
                dve.tensor_reduce(hs[:, h0:10], sq[:, h0:10], AX.X, ALU.add).then_inc(hs_done, 1)
                dve.wait_ge(hstd_done, m + 1)
                link(dve.reciprocal(hrs[:, :], hstd[:, :]))
                rs3 = hrs[:, h0:10].unsqueeze(2).to_broadcast([P, 10 - h0, HD])
                if b == 0:
                    tt(qkr[:, t, 512:640].rearrange("p (h d) -> p h d", d=HD), qg[:, 8:10], rs3,
                       ALU.mult).then_inc(qk_done, 1)
                    dve.wait_ge(qk_done, m + 1)
                    return
                if t == 0:
                    dve.wait_ge(turn_ps, turns_before(b))
                    dve.wait_ge(rope_in[b % 2], 16 * ((b + 1) // 2))
                link(tt(qg, qg, rs3, ALU.mult))
                cosv = rope[:, b % 2, t, 0:HD].unsqueeze(1).to_broadcast([P, 10, HD])
                tt(rc, qg, cosv, ALU.mult)
                halves = "p h (a f i) -> p h a f i"
                sv = sq.rearrange(halves, a=2, f=2)
                qv = qg.rearrange(halves, a=2, f=2)
                nv = rope[:, b % 2, t, HD:2 * HD].rearrange("p (a f i) -> p a f i", a=2, f=2)
                for f in range(2):
                    last = tt(sv[:, :, :, f], qv[:, :, :, 1 - f], nv[:, :, f].unsqueeze(1).to_broadcast([P, 10, 2, 16]),
                              ALU.mult)
                link(last)
                tt(qkr[:, t].rearrange("p (h d) -> p h d", d=HD), rc, sq, ALU.add).then_inc(qk_done, 1)
                dve.wait_ge(qk_done, m + 1)

            scale_x(0)
            modulate_xT(0)
            for b in range(NBLK):
                if b + 1 < NBLK:
                    scale_x(b + 1)
                    modulate_xT(b + 1)
                if b >= 1:
                    tok = slice((b - 1) * BLK, b * BLK)
                    for h in range(2):
                        n = 2 * (b - 1) + h
                        dve.wait_ge(cc_ps, n + 1)
                        dve.wait_ge(cx_out, n + 1)
                        tt(mixT[:, 2 + h, tok], PS[3][:, 0:BLK], xtmp, ALU.mult).then_inc(cc_out, 1)
                    take_turns(b - 1)
                for t in range(TPB):
                    head_norm(b, t)
            take_turns(NBLK - 1)

            def rotate(u):
                dve.wait_ge(xr_out, 2 * u + 2)
                dve.wait_ge(ust_in[u % 2], 32 * (u // 2 + 1))
                x = [rot[:, i] for i in range(6)]
                c, s_ = ust[:, u % 2, 256:256 + NCHUNK], ust[:, u % 2, 256 + NCHUNK:]
                tt(x[2], c, x[0], ALU.mult)
                link(tt(x[3], s_, x[1], ALU.mult))
                tt(x[4], x[2], x[3], ALU.add)
                link(tt(x[5], c, x[1], ALU.mult))
                link(tt(x[3], s_, x[0], ALU.mult))
                tt(x[5], x[5], x[3], ALU.subtract).then_inc(rotated, 1)
                dve.wait_ge(rotated, u + 1)
                decay = r8[:, u:u + 1].to_broadcast([P, NCHUNK])
                dve.tensor_tensor_scan(x[2], decay, x[4], 0.0, ALU.mult, ALU.add)
                link(dve.tensor_tensor_scan(x[3], decay, x[5], 0.0, ALU.mult, ALU.add))

            def unrotate(u):
                x = [rot[:, i, CCTX - 1:NCHUNK - 1] for i in range(6)]
                c, s_ = (ust[:, u % 2, 256 + i * NCHUNK + CCTX - 1:256 + (i + 1) * NCHUNK - 1] for i in range(2))
                if u == 6:
                    dve.wait_ge(conv_done, 8)
                if u == 7:
                    dve.wait_ge(m2_ps, 8)
                st = [S[:, u, ri] if u < UP else S[:, u, ri][:, ::-1] for ri in range(2)]
                tt(x[4], c, x[2], ALU.mult)
                link(tt(x[5], s_, x[3], ALU.mult))
                link(tt(st[0], x[4], x[5], ALU.subtract))
                tt(x[4], c, x[3], ALU.mult)
                link(tt(x[5], s_, x[2], ALU.mult))
                tt(st[1], x[4], x[5], ALU.add).then_inc(unit_done, 1)
                dve.wait_ge(unit_done, u + 1)

            for g in range(NGRP + 1):
                if g < NGRP:
                    half = n_keys(g) // 2
                    for j in range(QPK):
                        H = QPK * g + j
                        dve.wait_ge(s_ps, H + 1)
                        src = banks[:, 2 * (H % 2):2 * (H % 2) + 2, 0:half]
                        if g >= 2:
                            dve.wait_ge(es_done, g - 1)
                        link(dve.tensor_reduce(mx[:, g % 2, j:j + 1], src, AX.XY, ALU.max))
                        head = QPK * (g % 2) + j
                        dve.tensor_scalar(negm[:, g % 2, j:j + 1], mx[:, g % 2, j:j + 1], -SCALE,
                                          nsink[:, head:head + 1], ALU.mult, ALU.min).then_inc(negm_done, 1)
                    dve.wait_ge(negm_done, QPK * (g + 1))
                    tt(esink[:, g % 2], pk("sink", QPK * (g % 2), QPK), negm[:, g % 2], ALU.add).then_inc(es_in, 1)
                if g >= 1:
                    for J in range(pt_before(g - 1), pt_before(g)):
                        if J % 2 == 0:
                            dve.wait_ge(pt_ps, J + 1)
                            if J >= 2:
                                dve.wait_ge(pv_ps, J - 1)
                            dve.tensor_copy(PT[:, 0], PS[4]).then_inc(pt_dve, 1)
                    if g % 2 == 0:
                        i = g // 2 - 1
                        dve.wait_ge(pv_ps, pt_before(g))
                        dve.tensor_copy(mixT[:, 4:8, i * P:(i + 1) * P],
                                        PS[6].rearrange("p (j q) -> p j q", q=P)).then_inc(o_out, 1)
                if g < NGRP:
                    dve.wait_ge(es_done, g + 1)
                    if g >= 2:
                        dve.wait_ge(P_done, g - 1)
                    link(tt(rden[:, g % 2], rs[:, g % 2], esink[:, g % 2], ALU.add))
                    dve.reciprocal(rden[:, g % 2], rden[:, g % 2]).then_inc(rden_done, 1)
                if g >= 2:
                    (rotate if g % 2 == 0 else unrotate)(g // 2 - 1)
                if g % 2 == 0 and g // 2 < 8:
                    i = g // 2
                    dve.wait_ge(m2_ps, i + 1)
                    dve.wait_ge(bias_in, 32)
                    if i in (0, 1, 6, 7):
                        dst = (g1bc if i < 2 else g2bc)[:, (i % 2) * 512:(i % 2 + 1) * 512]
                        tt(dst, PS[7], dst, ALU.add).then_inc(m2_out, 1)
                    else:
                        src = PS[7][:, 0:8].rearrange("p (c j) -> p c j", j=2)[:, :, 0]
                        tt(mod2[:, 4 * (i - 2):4 * (i - 1)], src, pk("b_mod", 4 * (i + 4), 4), ALU.add).then_inc(m2_out, 1)
            unrotate(NU - 1)
            dve.wait_ge(conv_done, 8)
            for z in range(8):
                ct, half, tq = z // 4, (z // 2) % 2, z % 2
                dve.wait_ge(yt_ps, z + 1)
                dst = mixT[:, 2 + half, ct * 1024:(ct + 1) * 1024].rearrange("p (c t) -> p t c", t=CH)
                dve.tensor_copy(dst[:, 4 * tq:4 * tq + 4], PS[z].rearrange("p (t c) -> p t c", c=P)).then_inc(yt_out, 1)
            for w in range(8):
                tb, half = w // 2, w % 2
                dve.wait_ge(z_out, w + 1)
                link(dve.tensor_scalar(th[:, half], th[:, half], 0.5, 0.5, ALU.mult, ALU.add))
                dve.wait_ge(z_ps, 2 * tb + 2)
                v = mixT[:, 2 + half, tb * 512:(tb + 1) * 512]
                tt(v, v, th[:, half], ALU.mult).then_inc(glu_done, 1)
            link(dve.tensor_scalar(scale2[:, :], mod2[:, KD:2 * KD], 1.0, None, ALU.add))
            link(tt(scale2[:, :], scale2[:, :], pk("norm2"), ALU.mult))

            def add_mix(pp):
                if pp >= 1:
                    dve.wait_ge(h_stored, 16 * pp)
                for r in range(4):
                    t, half = r // 2, slice((r % 2) * 512, (r % 2 + 1) * 512)
                    dve.wait_ge(o2_ps, 4 * pp + r + 1)
                    tt(hm[:, t, half], PS[r], g1bc[:, half], ALU.mult).then_inc(o2_out, 1)
                dve.wait_ge(o2_out, 4 * (pp + 1))
                dve.wait_ge(xo_in[pp % 2], 16 * (pp // 2 + 1))
                tt(hm, hm, xo[:, pp % 2], ALU.add).then_inc(hm_done, 1)
                dve.wait_ge(std2_done, pp + 1)
                link(dve.reciprocal(rstd[:, :], ss[:, pp % 2]))
                for t in range(TPB):
                    ins = dve.tensor_scalar(xo[:, pp % 2, t], hm[:, t], rstd[:, t:t + 1], None, ALU.mult)
                ins.then_inc(x2_scaled, 1)
                dve.wait_ge(x2_scaled, pp + 1)

            add_mix(0)
            for pp in range(NPP):
                if pp + 1 < NPP:
                    add_mix(pp + 1)
                for q in range(4):
                    dve.wait_ge(t2_ps, 4 * pp + q + 1)
                    for i in range(2):
                        k = 2 * q + i
                        ins = dve.tensor_scalar(tT[:, k, pp * BLK:(pp + 1) * BLK], PS[4 + q % 2][:, i * BLK:(i + 1) * BLK],
                                                scale2[:, k:k + 1], mod2[:, k:k + 1], ALU.mult, ALU.add)
                    ins.then_inc(t2_out, 1)
                dve.wait_ge(lg_ps, pp + 1)
                dve.tensor_copy(lgt[:, TPB * pp:TPB * (pp + 1)], PS[6 + pp % 2][:, 0:TPB * NR]
                                .rearrange("p (t r) -> p t r", r=NR)).then_inc(lg_out, 1)
            biased, above, equal, rank, sel, gates, where, pick, pick2 = rt
            one = "p t r -> p (t r)"
            dve.wait_ge(sig_done, 1)
            dve.wait_ge(o2_ps, 4 * NPP)
            dve.wait_ge(x2_stored, 16 * NPP)
            link(tt(biased, lgt, pk("r_bias").unsqueeze(1).to_broadcast([P, NTILE, NR]), ALU.add))
            for t in range(NTILE):
                last = dve.max(top8[:, t], biased[:, t])
            link(last)
            fourth = top8[:, :, TOPK - 1:TOPK].to_broadcast([P, NTILE, NR])
            tt(above, biased, fourth, ALU.is_gt)
            link(tt(equal, biased, fourth, ALU.is_equal))
            link(dve.tensor_reduce(rsm[:, 0], above, AX.X, ALU.add))
            link(dve.tensor_scalar(rsm[:, 1], rsm[:, 0], -1.0, float(TOPK), ALU.mult, ALU.add))
            dve.wait_ge(cst_in, 48)
            link(dve.tensor_tensor_scan(rank.rearrange(one), restart, equal.rearrange(one), 0.0, ALU.mult, ALU.add))
            link(tt(rank, rank, rsm[:, 1].unsqueeze(2).to_broadcast([P, NTILE, NR]), ALU.is_le))
            link(tt(sel, equal, rank, ALU.mult))
            link(tt(sel, sel, above, ALU.add))
            dve.tensor_copy(selb, sel.rearrange(one)).then_inc(sel_done, 1)
            link(tt(gates, sel, lgt, ALU.mult))
            link(dve.tensor_reduce(rsm[:, 2], gates, AX.X, ALU.add))
            link(dve.reciprocal(rsm[:, 3], rsm[:, 2]))
            link(tt(gates, gates, rsm[:, 3].unsqueeze(2).to_broadcast([P, NTILE, NR]), ALU.mult))
            link(dve.tensor_scalar(gates, gates, ROUTED, None, ALU.mult))
            link(dve.tensor_tensor_scan(rank.rearrange(one), restart, sel.rearrange(one), 0.0, ALU.mult, ALU.add))
            link(tt(rank, rank, sel, ALU.mult))

            def whole(o, x):
                link(dve.tensor_scalar(o, x, ROUND, None, ALU.add))
                link(dve.tensor_scalar(o, o, ROUND, None, ALU.subtract))

            count, tiles, upto, start = (counts[:, i] for i in range(4))
            dve.wait_ge(pos_ps, 1)
            dve.wait_ge(cst_in, 48)
            link(dve.tensor_scalar(count, PS[5][:, 0:NR], 1.0 / P, (P - 1) / (2.0 * P), ALU.mult, ALU.add))
            whole(tiles, count)
            link(dve.tensor_tensor_scan(upto, ones, tiles, 0.0, ALU.mult, ALU.add))
            link(tt(start, upto, tiles, ALU.subtract))
            link(dve.tensor_scalar(start, start, float(P), None, ALU.mult))
            link(tt(where, PS[4].rearrange("p (t r) -> p t r", r=NR), start.unsqueeze(1).to_broadcast([P, NTILE, NR]),
                    ALU.add))
            for k in range(TOPK):
                dve.scalar_tensor_tensor(out=pick, in0=rank, scalar=k + 1.0, in1=where, op0=ALU.is_equal, op1=ALU.mult)
                link(dve.scalar_tensor_tensor(out=pick2, in0=rank, scalar=k + 1.0, in1=gates, op0=ALU.is_equal,
                                              op1=ALU.mult))
                dve.tensor_reduce(slot_f[:, :, k], pick, AX.X, ALU.add)
                link(dve.tensor_reduce(gate_k[:, :, k], pick2, AX.X, ALU.add))
            link(dve.tensor_scalar(slot_p, slot_f, 1.0 / P, -(P - 1) / (2.0 * P), ALU.mult, ALU.add))
            whole(slot_t, slot_p)
            link(dve.scalar_tensor_tensor(out=slot_p, in0=slot_t, scalar=-float(P), in1=slot_f, op0=ALU.mult,
                                          op1=ALU.add))
            dve.tensor_copy(slot_idx, slot_f)
            oh = oh_t.rearrange("p (t c n) -> p t c n", c=2, n=NT)
            for k in range(TOPK):
                if k >= 1:
                    dve.wait_ge(tok_ps, k)
                tt(oh_p.rearrange("p (t m) -> p t m", m=P), iota_p.unsqueeze(1).to_broadcast([P, NTILE, P]),
                   slot_p[:, :, k:k + 1].to_broadcast([P, NTILE, P]), ALU.is_equal)
                link(tt(oh[:, :, 1], iota_t.unsqueeze(1).to_broadcast([P, NTILE, NT]),
                        slot_t[:, :, k:k + 1].to_broadcast([P, NTILE, NT]), ALU.is_equal))
                link(tt(oh[:, :, 0], oh[:, :, 1], tile_no.unsqueeze(2).to_broadcast([P, NTILE, NT]), ALU.mult))
                dve.tensor_scalar(oh[:, :, 1], oh[:, :, 1], row_no, None, ALU.mult).then_inc(oh_t_done, 1)
                if k == 0:
                    link(tt(reached, iota_t.unsqueeze(2).to_broadcast([P, NT, NR]),
                            upto.unsqueeze(1).to_broadcast([P, NT, NR]), ALU.is_ge))
                    tile_e = pick.rearrange(one)[:, 0:NT]
                    dve.tensor_reduce(tile_e, reached, AX.X, ALU.add).then_inc(reached_done, 1)
                    dve.wait_ge(reached_done, 1)
                    link(dve.tensor_scalar(tile_e, tile_e, NR - 1.0, float(P), ALU.min, ALU.mult))
                    link(dve.tensor_scalar(tile_e, tile_e, row_no, None, ALU.add))
                    dve.tensor_copy(w_idx, tile_e)
            dve.wait_ge(tok_ps, TOPK)
            tok_f = pick2.rearrange(one)[:, 0:2 * NT]
            link(dve.tensor_copy(tok_f, PS[6][:, 0:2 * NT]))
            link(dve.scalar_tensor_tensor(out=tok_f[:, 0:NT], in0=tok_f[:, 0:NT], scalar=float(P), in1=tok_f[:, NT:2 * NT],
                                          op0=ALU.mult, op1=ALU.add))
            dve.tensor_copy(tok_idx, tok_f[:, 0:NT]).then_inc(idx_done, 1)

            def turned(it, s):
                dve.wait_ge(xt_ps, it * (2 * STEPS) + 2 * (s + 1))
                if not (first(it) and s < 2):
                    dve.wait_ge(hu_ps, it * STEPS + (s - 1))
                for k in range(4):
                    ins = dve.tensor_scalar(xT[:, s % 2, 4 + k], PS[1][:, k * P:(k + 1) * P], scale2[:, 4 + k:5 + k],
                                            mod2[:, 4 + k:5 + k], ALU.mult, ALU.add)
                ins.then_inc(xt_dve, 1)

            def send(it, s):
                if not (first(it) and s < 3):
                    dve.wait_ge(yo_stored[s % 3], it * 32 + 16 * (s // 3))
                for h in range(2):
                    half = slice(h * 512, (h + 1) * 512)
                    dve.wait_ge(yd_ps, it * (2 * STEPS) + (2 * s + h + 1))
                    tt(yo[:, s % 3, half], PS[2 + h], g2bc[:, half], ALU.mult).then_inc(yo_done, 1)

            def product(it, s):
                dve.wait_ge(sl_out, it * STEPS + (s + 1))
                dve.wait_ge(hu_ps, it * STEPS + (s + 1))
                if not (first(it) and s < 2):
                    dve.wait_ge(yd_ps, it * (2 * STEPS) + 2 * (s - 1))
                tt(hx[:, s % 2], slx[:, s % 2], PS[6 + s % 2][:, 0:P], ALU.mult).then_inc(h_done, 1)

            def experts_step(it, s):
                turned(it, s)
                if not (first(it) and s < 2):
                    send(it, s - 2)
                if not (first(it) and s < 1):
                    product(it, s - 1)

            def add_base(it):
                base = y[:, bass.ds(it, 1), :]
                tt(base, base, g2bc.unsqueeze(1), ALU.mult).then_inc(base_mul, 1)
                dve.wait_ge(base_mul, it + 1)
                dve.wait_ge(hb_in, it * 16 + 16)
                tt(base, base, hb.unsqueeze(1), ALU.add).then_inc(base_done, 1)

            def experts_turn(it):
                for s in range(STEPS):
                    experts_step(it, s)
                    if s == 3:
                        add_base(it)

            dve.wait_ge(ysh_out, 2 * NTILE)
            experts_turn(0)
            with dve.Fori(1, TURNS) as it:
                experts_turn(it)
            send(TURNS - 1, STEPS - 2)
            product(TURNS - 1, STEPS - 1)
            send(TURNS - 1, STEPS - 1)

            dve.wait_ge(base_done, NTILE)
            with dve.Fori(0, NTILE // SETS) as it:
                for j in range(SETS):
                    t = it * SETS + j
                    dve.wait_ge(gb_in[j], it * (16 * TOPK) + 16 * TOPK)
                    for k in range(TOPK):
                        dve.scalar_tensor_tensor(out=y[:, bass.ds(t, 1), :], in0=gb[:, TOPK * j + k].unsqueeze(1),
                                                 scalar=gate_k[:, bass.ds(t, 1), k], in1=y[:, bass.ds(t, 1), :],
                                                 op0=ALU.mult, op1=ALU.add).then_inc(sum_step, 1)
                        dve.wait_ge(sum_step, t * TOPK + (k + 1))

        @block.tensor
        def _(pe):
            pe.wait_ge(silu_done, 1)
            for n in range(4):
                pe.wait_ge(wmod_in[n % 2], 16 * (n // 2 + 1))
                for cb in range(4):
                    col = 2 * (4 * n + cb)
                    for k in range(KD):
                        mm = pe.matmul(PS[0][:, col:col + 2], wmod[:, n % 2, k, cb * P:(cb + 1) * P], silu_c[:, k, :],
                                       start=(k == 0), stop=(k == KD - 1))
                mm.then_inc(wmod_used, 1)
            pe.wait_ge(ident_in, 32)
            pe.wait_ge(drv_done, 2)
            for q in range(8):
                if q >= 2:
                    pe.wait_ge(drvT_out, q - 1)
                for i in range(4):
                    ri, u = (4 * q + i) // NU, (4 * q + i) % NU
                    mm = pe.transpose(PS[1 + q % 2][:, i * P:(i + 1) * P], drv[:, ri, u], ident[:, :])
                mm.then_inc(drvT_ps, 1)
            pe.wait_ge(mats_done, 2)
            for q in range(8):
                if q >= 2:
                    pe.wait_ge(K_out, q - 1)
                for gi in range(2):
                    rows = slice(NS * gi, NS * gi + NS)
                    for d in range(2):
                        u = d * UP + q
                        cols = slice(d * P, (d + 1) * P)
                        lo = 0 if d == 0 else GH
                        for ri in range(2):
                            mm = pe.matmul(PS[3 + 2 * (q % 2) + gi][0:GH, cols], bbar[rows, ri, u], cA[rows, ri, u, lo:lo + P],
                                           start=(ri == 0), stop=(ri == 1))
                mm.then_inc(K_ps, 1)

            def turn_x(b):
                pe.wait_ge(x_scaled, b + 1)
                if b == 0:
                    pe.wait_ge(mod1_done, 1)
                    pe.wait_ge(drvT_out, 8)
                for q in range(4):
                    job = 4 * b + q
                    if job >= 2:
                        pe.wait_ge(xn_out, job - 1)
                    for i in range(2):
                        k = 2 * q + i
                        for t in range(TPB):
                            mm = pe.transpose(PS[q % 2][:, i * BLK + t * P:i * BLK + (t + 1) * P],
                                              xs[:, b % 2, t, k * P:(k + 1) * P], ident[:, :])
                    mm.then_inc(xn_ps, 1)

            def columns(bank, b, col):
                for k in range(KD):
                    mm = pe.matmul(bank, w_in[:, k, col:col + P], xnT[:, b % 2, k], start=(k == 0), stop=(k == KD - 1))
                return mm

            def turn(b):
                base = turns_before(b)
                pe.wait_ge(u_out, b + 1)
                if b == 0:
                    pe.wait_ge(K_out, 8)
                pe.wait_ge(k_out, TPB * (b + 1))
                pe.wait_ge(v_out, TPB * (b + 1))
                i = 0

                def bank():
                    if base + i >= 2:
                        pe.wait_ge(turn_out, base + i - 1)
                    return PS[7 - i % 2]

                for i in range(4):
                    o = bank()
                    for sl_ in range(2):
                        for h in range(2):
                            s = 2 * i + sl_
                            col = (2 * sl_ + h) * P
                            mm = pe.transpose(o[0:CB, col:col + P], uT[:, h, s:BLK:CH], ident[:, :])
                    mm.then_inc(turn_ps, 1)
                i = 4
                if b >= 1:
                    for t in range(TPB):
                        pe.wait_ge(qk_done, TPB * b + t + 1)
                        o = bank()
                        for j in range(QPK):
                            mm = pe.transpose(o[:, j * P:(j + 1) * P], qkr[:, t, j * P:(j + 1) * P], ident[:, :])
                        mm.then_inc(turn_ps, 1)
                        i += 1
                pe.wait_ge(qk_done, TPB * (b + 1))
                o = bank()
                for t in range(TPB):
                    mm = pe.transpose(o[:, t * P:(t + 1) * P], qkr[:, t, 512:640], ident[:, :])
                mm.then_inc(turn_ps, 1)
                i += 1
                pe.wait_ge(turn_out, base + 4)
                o = bank()
                for g in range(NG):
                    mm = pe.transpose(o[:, g * CB:(g + 1) * CB], Uc[:, g].rearrange("p s h -> p (s h)"),
                                      ident[0:CB, 0:CB])
                mm.then_inc(turn_ps, 1)

            turn_x(0)
            for b in range(NBLK):
                if b + 1 < NBLK:
                    turn_x(b + 1)
                pe.wait_ge(xn_out, 4 * (b + 1))
                if b >= 1:
                    if b == 1:
                        pe.wait_ge(w_in_in[2], 16)
                        pe.wait_ge(K_out, 8)
                    for h in range(2):
                        n = 2 * (b - 1) + h
                        if n >= 1:
                            pe.wait_ge(cx_out, n)
                        columns(PS[2][:, 0:BLK], b, h * P).then_inc(cx_ps, 1)
                        if n >= 1:
                            pe.wait_ge(cc_out, n)
                        columns(PS[3][:, 0:BLK], b, COL_C + h * P).then_inc(cc_ps, 1)
                        if n >= 1:
                            pe.wait_ge(cb_out, n)
                        if h == 0:
                            pe.wait_ge(u_out, b)
                        columns(PS[4][:, 0:BLK], b, COL_B + h * P).then_inc(cb_ps, 1)
                    turn(b - 1)
                if b == 0:
                    pe.wait_ge(w_in_in[0], 16)
                    pe.wait_ge(K_out, 8)
                else:
                    pe.wait_ge(cb_out, 2 * b)
                for h in range(2):
                    mm = columns(PS[4][:, h * BLK:(h + 1) * BLK], b, COL_U + h * P)
                mm.then_inc(u_ps, 1)
                if b == 0:
                    pe.wait_ge(w_in_in[1], 16)
                else:
                    pe.wait_ge(turn_out, turns_before(b))
                for t in range(TPB):
                    m = TPB * b + t
                    if b >= 1:
                        if m > TPB:
                            pe.wait_ge(q_sq, m - TPB)
                            pe.wait_ge(q_out, m - TPB)
                        for k in range(KD):
                            mm = pe.matmul(PS[5][:, :], xnT[:, b % 2, k, t * P:(t + 1) * P],
                                           w_in[:, k, COL_Q:COL_Q + 512], start=(k == 0), stop=(k == KD - 1))
                        mm.then_inc(q_ps, 1)
                    if m >= 1:
                        pe.wait_ge(k_out, m)
                        pe.wait_ge(v_out, m)
                    for k in range(KD):
                        mm = pe.matmul(PS[6][:, 0:2 * P], xnT[:, b % 2, k, t * P:(t + 1) * P],
                                       w_in[:, k, COL_K:N_IN], start=(k == 0), stop=(k == KD - 1))
                    mm.then_inc(kv_ps, 1)
            turn(NBLK - 1)

            pe.wait_ge(xn_out, 4 * NBLK)
            pe.wait_ge(cx_out, 16)
            pe.wait_ge(cc_out, 16)
            pe.wait_ge(u_out, NBLK)
            pe.wait_ge(q_sq, NTILE)
            pe.wait_ge(v_out, TPB * NBLK)
            pe.wait_ge(turn_out, turns_before(NBLK))
            pe.wait_ge(mask_done, 1)

            def scores(g):
                i, kv = g // 2, g % 2
                rows = slice(HD * kv, HD * (kv + 1))
                w = window(i)
                W, half = len(w) * P, n_keys(g) // 2
                k0 = CTX + w[0] * P
                lo = min(W, half)
                masks = []
                if i > 0:
                    masks.append((0, 0, P, 0))
                if i < NTILE - 1:
                    at = (len(w) - 1) * P
                    m = max(0, min(P, half - at))
                    if m:
                        masks.append((0, at, m, P))
                    if m < P:
                        masks.append((1, at + m - half, P - m, P + m))
                for j in range(QPK):
                    H = QPK * g + j
                    if H >= 2:
                        pe.wait_ge(exp_done, H - 1)
                    b = [PS[2 * (H % 2)], PS[2 * (H % 2) + 1]]
                    q = mixT[rows, 4 + j, i * P:(i + 1) * P]
                    mm = pe.matmul(b[1][:, W - half:W - half + CTX], q, kT[rows, 0:CTX], start=True, stop=True)
                    if W > half:
                        mm = pe.matmul(b[1][:, 0:W - half], q, kT[rows, k0 + half:k0 + W], start=True, stop=False)
                    in1 = [m for m in masks if m[0] == 1]
                    for n, (_, at, m, mc) in enumerate(in1):
                        mm = pe.matmul(b[1][:, at:at + m], identb[:, :], maskb[:, mc:mc + m], start=False,
                                       stop=(n == len(in1) - 1))
                    in0 = [m for m in masks if m[0] == 0]
                    mm = pe.matmul(b[0][:, 0:lo], q, kT[rows, k0:k0 + lo], start=True, stop=not in0)
                    for n, (_, at, m, mc) in enumerate(in0):
                        mm = pe.matmul(b[0][:, at:at + m], identb[:, :], maskb[:, mc:mc + m], start=False,
                                       stop=(n == len(in0) - 1))
                    mm.then_inc(s_ps, 1)

            def outputs(g):
                i, kv = g // 2, g % 2
                rows = slice(HD * kv, HD * (kv + 1))
                tiles = key_tiles(g)
                base = pt_before(g)
                pe.wait_ge(P_done, g + 1)
                if kv == 0 and i >= 1:
                    pe.wait_ge(o_out, i)

                def turn_p(n):
                    J = base + n
                    if J >= 2:
                        pe.wait_ge(pt_act if J % 2 else pt_dve, J // 2)
                    for j in range(QPK):
                        mm = pe.transpose(PS[4 + J % 2][:, j * P:(j + 1) * P],
                                          Pb[:, (g % 2) * QPK + j, tiles[n][0]:tiles[n][0] + P], ident[:, :])
                    mm.then_inc(pt_ps, 1)

                def times_v(n):
                    J = base + n
                    pe.wait_ge(pt_act if J % 2 else pt_dve, J // 2 + 1)
                    pe.matmul(PS[6][rows, :], V[:, tiles[n][1], HD * kv:HD * (kv + 1)], PT[:, J % 2],
                              start=(n == 0), stop=(n == len(tiles) - 1)).then_inc(pv_ps, 1)

                turn_p(0)
                for n in range(1, len(tiles)):
                    turn_p(n)
                    times_v(n - 1)
                times_v(len(tiles) - 1)

            def drive(u, ri):
                pe.wait_ge(ust_in[u % 2], 32 * (u // 2 + 1))
                if u + ri >= 1:
                    pe.wait_ge(xr_out, 2 * u + ri)
                if u == 0:
                    pe.wait_ge(U_in, 16)
                if ri == 1 and u < 8:
                    pe.wait_ge(m2_out, u + 1)
                for gi in range(2):
                    mm = pe.matmul(PS[7][NS * gi:NS * (gi + 1), 0:NCHUNK],
                                   ust[:, u % 2, ri * P + NS * gi:ri * P + NS * (gi + 1)], U[:, 2 * (u % UP) + gi, :],
                                   start=True, stop=True)
                mm.then_inc(xr_ps, 1)

            def modulation(i):
                pe.wait_ge(wm2_in, 16 * (i + 1))
                pe.wait_ge(xr_out, 2 * i + 1)
                if i in (0, 1, 6, 7):
                    for k in range(KD):
                        mm = pe.matmul(PS[7], silu_c[:, k, 0:1].to_broadcast([P, P]), wm2[:, k], start=(k == 0),
                                       stop=(k == KD - 1))
                else:
                    for cb in range(4):
                        for k in range(KD):
                            mm = pe.matmul(PS[7][:, 2 * cb:2 * cb + 2], wm2[:, k, cb * P:(cb + 1) * P], silu_c[:, k, :],
                                           start=(k == 0), stop=(k == KD - 1))
                mm.then_inc(m2_ps, 1)

            for g in range(NGRP + 1):
                if g < NGRP:
                    scores(g)
                    drive(g // 2, g % 2)
                if g >= 1:
                    outputs(g - 1)
                if g % 2 == 0 and g // 2 < 8:
                    modulation(g // 2)

            pe.wait_ge(mats_in, 32)
            pe.wait_ge(unit_done, NU)
            pe.wait_ge(exp_done, QPK * NGRP)
            pe.wait_ge(pt_dve, even_before(NGRP))
            pe.wait_ge(pt_act, odd_before(NGRP))
            pe.wait_ge(o_out, NTILE)
            pe.wait_ge(xr_out, 2 * NU)
            for r in range(8):
                ct, a8, par = r // 4, (r // 2) % 2, r % 2
                rows = slice(NS * par, NS * (par + 1))
                for sl_ in range(4):
                    g = 8 * a8 + 2 * sl_ + par
                    o = PS[r][:, sl_ * P:(sl_ + 1) * P]
                    pe.matmul(o, U[:, g, CCTX + ct * P:CCTX + (ct + 1) * P], M[:, g], start=True, stop=False)
                    for d in range(2):
                        for ri in range(2):
                            u = d * UP + g // 2
                            mm = pe.matmul(o, S[rows, u, ri, ct * P:(ct + 1) * P], R[rows, u, ri], start=False,
                                           stop=(d == 1 and ri == 1))
                mm.then_inc(y_ps, 1)
            for z in range(8):
                ct, half, tq = z // 4, (z // 2) % 2, z % 2
                pe.wait_ge(y_out, 4 * (ct + 1))
                for t in range(4):
                    mm = pe.transpose(PS[z][:, t * P:(t + 1) * P], Yc[:, ct, 4 * tq + t, half * P:(half + 1) * P], ident[:, :])
                mm.then_inc(yt_ps, 1)
            pe.wait_ge(wglu_in, 16)
            for w in range(8):
                tb, half = w // 2, w % 2
                pe.wait_ge(yt_out, 4 if tb < 2 else 8)
                for k in range(2):
                    mm = pe.matmul(PS[w], w_glu[:, k, half * P:(half + 1) * P], mixT[:, 2 + k, tb * 512:(tb + 1) * 512],
                                   start=(k == 0), stop=(k == 1))
                mm.then_inc(z_ps, 1)

            def project_out(pp):
                for r in range(4):
                    t, half = r // 2, slice((r % 2) * 512, (r % 2 + 1) * 512)
                    if pp >= 1:
                        pe.wait_ge(o2_out, 4 * (pp - 1) + r + 1)
                    for k in range(KD):
                        mm = pe.matmul(PS[r], mixT[:, k, (TPB * pp + t) * P:(TPB * pp + t + 1) * P], w_out[:, k, half],
                                       start=(k == 0), stop=(k == KD - 1))
                    mm.then_inc(o2_ps, 1)

            pe.wait_ge(z_out, 8)
            pe.wait_ge(glu_done, 8)
            pe.wait_ge(w_out_in, 32)
            project_out(0)
            for pp in range(NPP):
                if pp + 1 < NPP:
                    project_out(pp + 1)
                pe.wait_ge(x2_scaled, pp + 1)
                for q in range(4):
                    job = 4 * pp + q
                    if job >= 2:
                        pe.wait_ge(t2_out, job - 1)
                    for i in range(2):
                        k = 2 * q + i
                        for t in range(TPB):
                            mm = pe.transpose(PS[4 + q % 2][:, i * BLK + t * P:i * BLK + (t + 1) * P],
                                              xo[:, pp % 2, t, k * P:(k + 1) * P], ident[:, :])
                    mm.then_inc(t2_ps, 1)
                pe.wait_ge(t2_out, 4 * (pp + 1))
                if pp >= 2:
                    pe.wait_ge(lg_out, pp - 1)
                for t in range(TPB):
                    for k in range(KD):
                        mm = pe.matmul(PS[6 + pp % 2][:, t * NR:(t + 1) * NR],
                                       tT[:, k, (TPB * pp + t) * P:(TPB * pp + t + 1) * P], r_w[:, k, :],
                                       start=(k == 0), stop=(k == KD - 1))
                mm.then_inc(lg_ps, 1)

            def shared_in(tb):
                for m, ps in enumerate((shg_ps, shu_ps)):
                    if tb >= 2:
                        pe.wait_ge(sh_act, tb - 1)
                    for k in range(KD):
                        mm = pe.matmul(PS[2 * m + tb % 2], wsh[:, m, k * EF:(k + 1) * EF], tT[:, k, tb * TW:(tb + 1) * TW],
                                       start=(k == 0), stop=(k == KD - 1))
                    mm.then_inc(ps, 1)

            def shared_down(tb):
                pe.wait_ge(prod_done, tb + 1)
                for r in range(8):
                    d = 8 * tb + r
                    t, half = r // 2, slice((r % 2) * 512, (r % 2 + 1) * 512)
                    if d >= 4:
                        pe.wait_ge(ysh_out, d - 3)
                    pe.matmul(PS[d % 4], hsh[:, tb, t * P:(t + 1) * P], wsh[:, 2, half], start=True, stop=True)\
                        .then_inc(shy_ps, 1)

            def tokens(k):
                pe.wait_ge(oh_t_done, k + 1)
                for t in range(NTILE):
                    mm = pe.matmul(PS[6][:, 0:2 * NT], oh_p[:, t * P:(t + 1) * P], oh_t[:, t * 2 * NT:(t + 1) * 2 * NT],
                                   start=(k == 0 and t == 0), stop=(k == TOPK - 1 and t == NTILE - 1))
                mm.then_inc(tok_ps, 1)

            pe.wait_ge(wsh_in, 16)
            pe.wait_ge(o2_out, 4 * NPP)
            pe.wait_ge(t2_out, 4 * NPP)
            pe.wait_ge(lg_out, NPP)
            shared_in(0)
            shared_in(1)
            pe.wait_ge(sel_done, 1)
            pe.wait_ge(consts_b, 1)
            pe.matmul(PS[4], earlier, selb, start=True, stop=False)
            for j in range(1, NTILE):
                pe.matmul(PS[4][:, j * NR:NTILE * NR], ones_b, selb[:, 0:(NTILE - j) * NR], start=False,
                          stop=(j == NTILE - 1))
            for t in range(NTILE):
                mm = pe.matmul(PS[5][:, 0:NR], ones_b, selb[:, t * NR:(t + 1) * NR], start=(t == 0), stop=(t == NTILE - 1))
            mm.then_inc(pos_ps, 1)
            shared_in(2)
            shared_in(3)
            pe.wait_ge(sh_act, TB)
            for i in range(TB):
                tokens(i)
                shared_down(i)

            def turn_rows(it, s):
                n = it * STEPS + s
                pe.wait_ge(xg_in[s % 3], it * 32 + 16 * (s // 3 + 1))
                for h, used in enumerate((xt_act, xt_dve)):
                    if not (first(it) and s < 1):
                        pe.wait_ge(used, it * STEPS + s)
                    for i in range(4):
                        mm = pe.transpose(PS[h][:, i * P:(i + 1) * P], xg[:, s % 3, (4 * h + i) * P:(4 * h + i + 1) * P],
                                          ident[:, :])
                    mm.then_inc(xt_ps, 1)

            def down(it, s):
                pe.wait_ge(h_done, it * STEPS + (s + 1))
                for h in range(2):
                    if not (first(it) and s < 1):
                        pe.wait_ge(yo_done, it * (2 * STEPS) + (2 * s + h - 1))
                    pe.matmul(PS[2 + h], hx[:, s % 2], wx[s % 3][:, 2, h * 512:(h + 1) * 512], start=True, stop=True)\
                        .then_inc(yd_ps, 1)

            def gate_and_up(it, s):
                pe.wait_ge(xt_act, it * STEPS + (s + 1))
                pe.wait_ge(xt_dve, it * STEPS + (s + 1))
                pe.wait_ge(wx_in[s % 3], it * 32 + 16 * (s // 3 + 1))
                for m, ps in enumerate((hg_ps, hu_ps)):
                    if not (first(it) and s < 2):
                        pe.wait_ge((sl_out, h_done)[m], it * STEPS + (s - 1))
                    for k in range(KD):
                        mm = pe.matmul(PS[4 + 2 * m + s % 2][:, 0:P], wx[s % 3][:, m, k * EF:(k + 1) * EF], xT[:, s % 2, k],
                                       start=(k == 0), stop=(k == KD - 1))
                    mm.then_inc(ps, 1)

            def experts_step(it, s):
                turn_rows(it, s)
                if not (first(it) and s < 2):
                    down(it, s - 2)
                if not (first(it) and s < 1):
                    gate_and_up(it, s - 1)

            pe.wait_ge(ysh_out, 2 * NTILE)
            pe.wait_ge(idx_done, 1)
            for s in range(STEPS):
                experts_step(0, s)
            with pe.Fori(1, TURNS) as it:
                for s in range(STEPS):
                    experts_step(it, s)
            down(TURNS - 1, STEPS - 2)
            gate_and_up(TURNS - 1, STEPS - 1)
            down(TURNS - 1, STEPS - 1)


def lay_out(inputs):
    import numpy as np

    f = {k: np.asarray(v) for k, v in inputs.items()}
    f = {k: (v[0] if v.ndim and v.shape[0] == 1 and k not in ("x", "c") else v) for k, v in f.items()}

    def rows(v):
        return v.reshape(-1, P).T

    def same(v):
        return np.broadcast_to(v, (P, v.shape[-1]))

    def by_state(v):
        v = v.reshape((2, UP, 2, NS) + v.shape[3:])
        return np.ascontiguousarray(np.moveaxis(v, (2, 3), (0, 1))).reshape((P, NU) + v.shape[4:])

    cc = np.stack([f["c"][0], f["c_ctx"]])
    parts = {
        "c": np.ascontiguousarray(cc.reshape(2, KD, P).transpose(2, 1, 0)).reshape(P, 2 * KD),
        "b_mod": rows(f["b_mod"]), "norm1": rows(f["norm1_g"]), "norm2": rows(f["norm2_g"]),
        "lam_re": by_state(f["ssm_lam_re"]), "lam_im": by_state(f["ssm_lam_im"]),
        "log_dt": by_state(np.broadcast_to(f["ssm_log_dt"][:, :, None], (2, NG, NS))),
        "q_g": same(f["q_norm_g"]), "k_g": same(f["k_norm_g"]), "sink": same(f["attn_sink"]),
        "b_glu": rows(f["b_glu"]),
        "conv_w": np.ascontiguousarray(f["conv_w"].reshape(3, 2, P).transpose(2, 1, 0)).reshape(P, 6),
        "r_bias": same(f["router_bias"]),
        "mults": same(np.array(MULTS, np.float32)),
        "d_skip": np.concatenate([f["ssm_d"].reshape(NG, GH).T, np.zeros((P - GH, NG), np.float32)]),
    }
    pack = np.concatenate([parts[k] for k in PACK], axis=1)
    assert pack.shape == (P, N_PACK)
    raw = np.stack([by_state(f["ssm_b_re"]), by_state(f["ssm_b_im"]),
                    by_state(f["ssm_c_re"].transpose(0, 1, 3, 2)), by_state(f["ssm_c_im"].transpose(0, 1, 3, 2))], axis=1)
    w = f["w_in"]
    wq = w[:, 1024:1536].reshape(D, NKV, QPK, HD).transpose(0, 2, 1, 3).reshape(D, 512)
    w_in = np.concatenate([w[:, 0:COL_Q], wq, w[:, 1536:N_IN]], axis=1).reshape(KD, P, N_IN).transpose(1, 0, 2)
    wo = f["w_out"]
    wo_att = wo[512:1024].reshape(NKV, QPK, HD, D).transpose(1, 0, 2, 3).reshape(512, D)
    w_out = np.concatenate([wo[0:512], wo_att]).reshape(KD, P, D).transpose(1, 0, 2)
    pairs = HD // 4
    pos = np.arange(SEQ)
    freq = (np.float32(10000.0) ** (-np.arange(pairs, dtype=np.float32) / pairs)).astype(np.float32)
    ang = np.stack([(pos // 64).astype(np.float32)[:, None] * freq, (pos % 64).astype(np.float32)[:, None] * freq], axis=1)
    co, si = np.cos(ang), np.sin(ang)
    table = np.concatenate([np.stack([co, co], 2).reshape(SEQ, HD), np.stack([-si, si], 2).reshape(SEQ, HD)], axis=1)
    rope = table.reshape(NBLK - 1, TPB, P, 2 * HD).transpose(0, 2, 1, 3)
    q_, k_ = np.arange(P)[:, None], np.arange(P)[None, :]
    mask = np.concatenate([np.where(k_ >= q_, 0.0, -1e30), np.where(k_ <= q_, 0.0, -1e30)], axis=1)

    def by_row(w):
        return np.moveaxis(w.reshape((KD, P) + w.shape[1:]), (0, 1), (-2, -3)).reshape(w.shape[1:-1] + (P, D))

    w_exp = np.stack([by_row(f["w_exp_gate"]), by_row(f["w_exp_up"]), f["w_exp_down"]], axis=2)
    w_sh = np.stack([by_row(f["w_sh_gate"]), by_row(f["w_sh_up"]), f["w_sh_down"]], axis=1)
    cst = np.zeros((P, 384 + P), np.float32)
    cst[:, 0:P] = np.arange(P)
    cst[:, P:P + NT] = np.arange(NT)
    cst[:, 224:240] = np.arange(NTILE)
    cst[:, 240] = np.arange(P)
    cst[:, 256:256 + NR] = 1.0
    cst[:, 384:] = q_ < k_
    arrays = {
        "pack": pack, "raw": raw.reshape(P, 4, NU, GH), "w_mod": f["w_mod"], "b_mod": f["b_mod"].reshape(6, D),
        "x": f["x"][0], "ctx": f["ctx"], "w_in": w_in, "w_glu": f["w_glu"], "w_out": w_out,
        "router_w": f["router_w"].reshape(KD, P, NR).transpose(1, 0, 2), "w_exp": w_exp.reshape(NR * P, 3 * D),
        "w_sh": w_sh, "cst": cst, "rope": rope,
        "ident": np.eye(P, dtype=np.float32), 
        "mask": mask.astype(np.float32),
        "restart": same((np.arange(NTILE * NR) % NR != 0).astype(np.float32)),
    }
    return {k: np.ascontiguousarray(v) for k, v in arrays.items()}


def kernel(**inputs):
    import numpy as np
    import concourse.bacc as bacc
    from concourse.bass_utils import run_bass_kernel_spmd

    nc = bacc.Bacc("TRN2", target_bir_lowering=False, num_devices=1)
    arrays = lay_out(inputs)
    a = {k: nc.dram_tensor(f"in_{k}", v.shape, mybir.dt.from_np(v.dtype), kind="ExternalInput").ap()
         for k, v in arrays.items()}
    out = nc.dram_tensor("out", (SEQ, D), F32, kind="ExternalOutput").ap()
    block_kernel(nc, a, out)
    r = run_bass_kernel_spmd(nc, [{f"in_{k}": v for k, v in arrays.items()}], core_ids=[0])
    return r.results[0]["out"].reshape(1, SEQ, D)
```

```python
import math
from contextlib import ExitStack

import concourse.bass as bass
from concourse import mybir

F32 = mybir.dt.float32
BF16 = mybir.dt.bfloat16
U32 = mybir.dt.uint32
ALU = mybir.AluOpType
ACT = mybir.ActivationFunctionType
AX = mybir.AxisListType

P = 128
D = 1024
KD = D // P
SEQ, CTX = 2048, 256
BLK = 256
TPB = BLK // P
NBLK = (SEQ + CTX) // BLK
NTILE = SEQ // P
N_IN = 1792
COL_B, COL_C, COL_U, COL_Q, COL_K = 256, 512, 768, 1024, 1536
HD = 64
NHEAD, NKV, QPK = 8, 2, 4
SCALE = HD ** -0.5
EPS = 1e-6

CH = 8
NG, GH, NS = 16, 16, 64
UP = NG // 2
NU = 2 * UP
CCTX, CLAT = CTX // CH, SEQ // CH
NCHUNK = CCTX + CLAT
CB = BLK // CH
DOUBLINGS = 8
MULTS = list(range(CH, -1, -1)) + list(range(0, CH + 1)) + [CH << j for j in range(1, DOUBLINGS + 1)]
RISE, DBL = CH + 1, 2 * (CH + 1)
NPOW, NM = 2 * (CH + 1), len(MULTS)
KW = (2 * CH - 1) * GH
INV_2PI = 1.0 / (2.0 * math.pi)
PI_A = 6.28125
PI_B = 0.0019350051879882812
PI_C = 2.0 * math.pi - PI_A - PI_B
LN2_A = 0.693359375
LN2_B = math.log(2.0) - LN2_A
ROUND = 1.5 * 2.0 ** 23

NR, TOPK, ROUTED = 32, 4, 2.5
EF = 128
TB = 4
TW = SEQ // TB
STEPS = 6
NT = (SEQ * TOPK - NR) // P + NR
TURNS = -(-NT // STEPS)
LAST = NT - (TURNS - 1) * STEPS
assert TURNS == SEQ // P
SETS = 4

PACK = {}
_at = 0
for _name, _n in (("c", 2 * KD), ("b_mod", 48), ("norm1", KD), ("norm2", KD), ("lam_re", NU), ("lam_im", NU),
                  ("log_dt", NU), ("q_g", HD), ("k_g", HD), ("sink", NHEAD), ("b_glu", 2), ("conv_w", 6),
                  ("r_bias", NR), ("mults", NM), ("d_skip", NG)):
    PACK[_name] = (_at, _n)
    _at += _n
N_PACK = _at


def block_kernel(nc, a, out):
    ctx = ExitStack()
    with ctx:
        def sb(name, shape, dt=F32):
            return ctx.enter_context(nc.sbuf_tensor(name, shape, dt))

        def sem(name):
            return ctx.enter_context(nc.semaphore(name))

        arena = sb("arena", [P, 51584])

        def cut(at, *shape, rows=P):
            n = math.prod(shape)
            assert at + n <= 51584
            v = arena[0:rows, at:at + n]
            if len(shape) == 2:
                v = v.rearrange("p (a b) -> p a b", b=shape[1])
            if len(shape) == 3:
                v = v.rearrange("p (a b c) -> p a b c", b=shape[1], c=shape[2])
            return v

        mixT = cut(0, 8, SEQ)
        kT = cut(16384, SEQ + CTX)
        V = cut(18688, (SEQ + CTX) // P, P)
        tab = cut(0, UP, 2, NCHUNK)
        tab2 = cut(41472, UP, 2, NCHUNK)
        drv = cut(4608, 2, NU, P)
        Kfull = cut(4608, NG, KW, rows=GH)
        cA = cut(8704, 2, NU, (CH + 1) * GH)
        bbar = cut(13312, 2, NU, GH)
        raw = cut(13824, 4, NU, GH)
        tmpA = cut(14848, 1152)
        tmpB = cut(16000, 1152)
        drvT_st = cut(17152, 2, 512)
        ptmp = cut(18176, 2, UP * 128)
        mask_st = cut(18176, 2 * P)
        mrows = cut(37376, 4, 512, rows=2)
        wmod = cut(39424, 2, KD, 512)
        SM = [cut(47616 + i * NU * NM, NU, NM) for i in range(7)]
        w_in = cut(20992, KD, N_IN)
        xs = cut(35328, 2, TPB, D)
        xnT = cut(39424, 2, KD, BLK)
        U_st = cut(43520, 2, NG * CB)
        Uc = cut(44544, NG, CH, GH, rows=CB)
        uT = cut(46592, 2, BLK)
        qg = cut(47104, 10, HD)
        sq = cut(47744, 10, HD)
        rc = cut(48384, 10, HD)
        qkr = cut(49024, TPB, 640)
        rope = cut(50304, 2, TPB, 2 * HD)
        junk = cut(50816, 512).bitcast(BF16)
        xtmp = cut(51328, BLK)
        wm2 = cut(29696, KD, 512)
        U = cut(20992, NG, NCHUNK)
        S = cut(25600, NU, 2, CLAT)
        mrow = cut(29184, 512, rows=2)
        ctmp = cut(28672, 2, 512)
        R = cut(33792, NU, 2, P)
        M = cut(37888, NG, P)
        Pb = cut(39936, 8, 640)
        PT = cut(45056, 2, 512)
        ust = cut(46080, 2, 832)
        rot = cut(47744, 6, NCHUNK)
        g1bc = cut(49472, D)
        g2bc = cut(50496, D)
        Yc = cut(16384, 2, CH, 256)
        w_glu = cut(20480, 2, 256)
        th = cut(20992, 2, 512)
        w_out = cut(39936, KD, D)
        tT = cut(20992, KD, SEQ)
        xo = cut(16384, 2, TPB, D)
        hm = cut(37376, TPB, D)
        lgt = cut(48128, NTILE, NR)
        r_w = cut(48640, KD, NR)
        junk2 = cut(48896, 512).bitcast(BF16)
        wsh = cut(37376, 3, D)
        hsh = cut(40448, TB, TW)
        rt = [cut(42496 + 512 * i, NTILE, NR) for i in range(9)]
        rsm = cut(47104, 4, NTILE)
        top8 = cut(47168, NTILE, 8)
        restart = cut(47296, NTILE * NR)
        counts = cut(47808, 4, NR)
        selb = cut(48896, NTILE * NR // 2).bitcast(BF16)
        earlier = cut(49152, P // 2).bitcast(BF16)
        ones_b = cut(49216, P // 2).bitcast(BF16)
        cst = cut(49472, 384)
        iota_p, iota_t, tile_no = cst[:, 0:P], cst[:, P:P + NT], cst[:, 224:240]
        row_no, ones, earlier_st = cst[:, 240:241], cst[:, 256:256 + NR], cut(49856, P)
        w_idx = cut(49984, NT).bitcast(U32)
        tok_idx = cut(50080, NT).bitcast(U32)
        slot_idx = cut(50176, NTILE, TOPK).bitcast(U32)
        gate_k = cut(50240, NTILE, TOPK)
        slot_f = cut(50304, NTILE, TOPK)
        slot_t = cut(50368, NTILE, TOPK)
        slot_p = cut(50432, NTILE, TOPK)
        reached = cut(0, NT, NR)
        oh_p = cut(16384, NTILE * P // 2).bitcast(BF16)
        oh_t = cut(18432, NTILE * 2 * NT // 2).bitcast(BF16)
        sl2 = cut(15360, 2, TW)
        y = cut(0, NTILE, D)
        wx = [cut(20992 + 3 * D * i, 3, D) for i in range(3)]
        xg = cut(30208, 3, D)
        xT = cut(33280, 2, KD, P)
        hb = cut(35328, D)
        slx = cut(16384, 2, P)
        hx = cut(16640, 2, P)
        yo = cut(42496, 3, D)
        gb = cut(20992, SETS * TOPK, D)

        ident = sb("ident", [P, P])
        identb = sb("identb", [P, P], BF16)
        maskb = sb("maskb", [P, 2 * P], BF16)
        pack = sb("pack", [P, N_PACK])

        def pk(name, lo=0, n=None):
            at, size = PACK[name]
            return pack[:, at + lo:at + lo + (n or size)]

        silu_c = sb("silu_c", [P, KD, 2])
        scale1 = sb("scale1", [P, KD, 2])
        shift1 = sb("shift1", [P, KD, 2])
        mod2 = sb("mod2", [P, 2 * KD])
        scale2 = sb("scale2", [P, KD])
        nsink = sb("nsink", [P, NHEAD])
        hbglu = sb("hbglu", [P, 2])
        eps = sb("eps", [P, 1])
        r8 = sb("r8", [P, NU])
        ss = sb("ss", [P, 2, TPB])
        rstd = sb("rstd", [P, TPB])
        hs = sb("hs", [P, 10])
        hstd = sb("hstd", [P, 10])
        hrs = sb("hrs", [P, 10])
        mx = sb("mx", [P, 2, QPK])
        negm = sb("negm", [P, 2, QPK])
        rs = sb("rs", [P, 2, QPK])
        esink = sb("esink", [P, 2, QPK])
        rden = sb("rden", [P, 2, QPK])
        tok_cur = [sb(f"tok_cur{i}", [P, 1], U32) for i in range(3)]
        w_cur = [sb(f"w_cur{i}", [P, 1], U32) for i in range(3)]
        slot_cur = [[sb(f"slot_cur{i}_{k}", [P, 1], U32) for k in range(TOPK)] for i in range(SETS)]

        banks = ctx.enter_context(nc.psum_tensor("banks", [P, 8, 512], F32))
        PS = [banks[:, i, :] for i in range(8)]

        drvT_d = nc.dram_tensor("drvT_d", [NU, P, 2, P], F32).ap()
        tab_d = nc.dram_tensor("tab_d", [NU, P, 2, NCHUNK], F32).ap()
        R_d = nc.dram_tensor("R_d", [P, NU, 2, P], F32).ap()
        M_d = nc.dram_tensor("M_d", [P, NG, P], F32).ap()
        U_d = nc.dram_tensor("U_d", [P, NG, NCHUNK], F32).ap()
        h_d = nc.dram_tensor("h_d", [NTILE, P, D], F32).ap()
        x2_d = nc.dram_tensor("x2_d", [SEQ, D], F32).ap()
        pair_d = nc.dram_tensor("pair_d", [NT * P, D], F32).ap()
        pair_t = pair_d.rearrange("(n p) d -> n p d", p=P)
        out_t = out.rearrange("(t p) d -> t p d", p=P)

        pack_in = sem("pack_in")
        ident_in = sem("ident_in")
        raw_in = sem("raw_in")
        consts_b, tab2_done, tab2_stored = sem("consts_b"), sem("tab2_done"), sem("tab2_stored")
        wmod_in = [sem(f"wmod_in{i}") for i in range(2)]
        wmod_used = sem("wmod_used")
        w_in_in = [sem(f"w_in_in{i}") for i in range(3)]
        x_in = [sem(f"x_in{i}") for i in range(2)]
        rope_in = [sem(f"rope_in{i}") for i in range(2)]
        silu_done = sem("silu_done")
        args_done = sem("args_done")
        trig_done = sem("trig_done")
        dve_step = sem("dve_step")
        act_step = sem("act_step")
        pool_step = sem("pool_step")
        unit_cs = sem("unit_cs")
        drv_done = sem("drv_done")
        drvT_ps = sem("drvT_ps")
        drvT_out = sem("drvT_out")
        drvT_stored = [sem(f"drvT_stored{i}") for i in range(2)]
        tab_stored = sem("tab_stored")
        mats_done = sem("mats_done")
        K_ps = sem("K_ps")
        K_out = sem("K_out")
        K_done = sem("K_done")
        mats_stored = sem("mats_stored")
        mrow_out, mcol_ps, mod_done = sem("mrow_out"), sem("mcol_ps"), sem("mod_done")
        std_done = sem("std_done")
        x_scaled = sem("x_scaled")
        xn_ps = sem("xn_ps")
        xn_out = sem("xn_out")
        cx_ps, cx_out = sem("cx_ps"), sem("cx_out")
        cc_ps, cc_out = sem("cc_ps"), sem("cc_out")
        cb_ps, cb_out = sem("cb_ps"), sem("cb_out")
        u_ps, u_out = sem("u_ps"), sem("u_out")
        q_ps, q_sq, q_out = sem("q_ps"), sem("q_sq"), sem("q_out")
        kv_ps, k_sq, v_out, k_out = sem("kv_ps"), sem("k_sq"), sem("v_out"), sem("k_out")
        hs_done = sem("hs_done")
        hstd_done = sem("hstd_done")
        qk_done = sem("qk_done")
        turn_ps, turn_out = sem("turn_ps"), sem("turn_out")
        U_stored = [sem(f"U_stored{i}") for i in range(2)]
        U_in = sem("U_in")
        mats_in = sem("mats_in")
        drv_in = [sem(f"drv_in{i}") for i in range(2)]
        phase_in = [sem(f"phase_in{i}") for i in range(2)]
        wm2_in, m2_ps, m2_out = sem("wm2_in"), sem("m2_ps"), sem("m2_out")
        s_ps, negm_done, exp_done = sem("s_ps"), sem("negm_done"), sem("exp_done")
        es_in, es_done, rden_done, P_done = sem("es_in"), sem("es_done"), sem("rden_done"), sem("P_done")
        pt_ps, pt_dve, pt_act = sem("pt_ps"), sem("pt_dve"), sem("pt_act")
        pv_ps, o_out = sem("pv_ps"), sem("o_out")
        xr_ps, xr_out, rotated, unit_done = sem("xr_ps"), sem("xr_out"), sem("rotated"), sem("unit_done")
        conv_done = sem("conv_done")
        y_ps, y_out, yt_ps, yt_out = sem("y_ps"), sem("y_out"), sem("yt_ps"), sem("yt_out")
        wglu_in, z_ps, z_out, glu_done = sem("wglu_in"), sem("z_ps"), sem("z_out"), sem("glu_done")
        w_out_in = sem("w_out_in")
        xo_in = [sem(f"xo_in{i}") for i in range(2)]
        o2_ps, o2_out, hm_done, h_stored = sem("o2_ps"), sem("o2_out"), sem("hm_done"), sem("h_stored")
        std2_done, x2_scaled, t2_ps, t2_out = sem("std2_done"), sem("x2_scaled"), sem("t2_ps"), sem("t2_out")
        lg_ps, lg_out, sig_done = sem("lg_ps"), sem("lg_out"), sem("sig_done")
        x2_stored, cst_in, wsh_in = sem("x2_stored"), sem("cst_in"), sem("wsh_in")
        mod2_done = sem("mod2_done")
        sel_done, pos_ps = sem("sel_done"), sem("pos_ps")
        oh_t_done, tok_ps, idx_done = sem("oh_t_done"), sem("tok_ps"), sem("idx_done")
        reached_done = sem("reached_done")
        shg_ps, shu_ps, sh_act, prod_done = sem("shg_ps"), sem("shu_ps"), sem("sh_act"), sem("prod_done")
        shy_ps, ysh_out = sem("shy_ps"), sem("ysh_out")
        tok_cur_done, w_cur_done = sem("tok_cur_done"), sem("w_cur_done")
        xg_in = [sem(f"xg_in{i}") for i in range(3)]
        wx_in = [sem(f"wx_in{i}") for i in range(3)]
        xt_ps, xt_act, xt_dve = sem("xt_ps"), sem("xt_act"), sem("xt_dve")
        hg_ps, hu_ps, sl_out, h_done = (sem(n) for n in ("hg_ps", "hu_ps", "sl_out", "h_done"))
        yd_ps, yo_done = sem("yd_ps"), sem("yo_done")
        yo_stored = [sem(f"yo_stored{i}") for i in range(3)]
        hb_in, base_mul, base_done = sem("hb_in"), sem("base_mul"), sem("base_done")
        slot_cur_done, sum_step, out_stored = sem("slot_cur_done"), sem("sum_step"), sem("out_stored")
        gb_in = [sem(f"gb_in{i}") for i in range(SETS)]

        block = ctx.enter_context(nc.Block())

        def first(it):
            return type(it) is int and it == 0

        def tiles_in(it):
            return LAST if type(it) is int and it == TURNS - 1 else STEPS

        def turns(b):
            return 6 if b == 0 else 8

        def turns_before(b):
            return 0 if b == 0 else 6 + 8 * (b - 1)

        TAB_STEPS = 1 + 3 * DOUBLINGS
        MOD2 = (4, 5, 10, 11, 6, 7, 8, 9)
        NGRP = 2 * NTILE
        NPP = NTILE // TPB

        def window(i):
            return list(range(max(0, i - 1), min(NTILE, i + 2)))

        def key_tiles(g):
            w = window(g // 2)
            return [(n * P, CTX // P + t) for n, t in enumerate(w)] + [(len(w) * P + c * P, c) for c in range(CTX // P)]

        def n_keys(g):
            return len(key_tiles(g)) * P

        def pt_before(g):
            return sum(len(key_tiles(x)) for x in range(g))

        def turn_steps(g):
            tiles = [("tile", n) for n in range(len(key_tiles(g - 1)))] if g >= 1 else []
            if g == NGRP:
                return tiles
            return [("head", 0), *tiles[0:1], ("head", 1), *tiles[1:2], ("head", 2), ("head", 3),
                    *tiles[2:3], ("sums", 0), ("drive", 0), *tiles[3:]]

        def odd_before(g):
            return pt_before(g) // 2

        def even_before(g):
            return (pt_before(g) + 1) // 2

        @block.sync
        def _(sp):
            sp.dma_start(pack[:, :], a["pack"]).then_inc(pack_in, 16)
            sp.dma_start(raw, a["raw"]).then_inc(raw_in, 16)
            sp.dma_start(ident[:, :], a["ident"]).then_inc(ident_in, 16)
            sp.dma_start(mask_st, a["mask"]).then_inc(ident_in, 16)
            wm_src = a["w_mod"].rearrange("(k p) n -> p k n", p=P)

            def load_wmod(n):
                if n >= 2:
                    sp.wait_ge(wmod_used, n - 1)
                sp.dma_start(wmod[:, n % 2], wm_src[:, :, n * 512:(n + 1) * 512]).then_inc(wmod_in[n % 2], 16)

            def load_x(b):
                if b >= 2:
                    sp.wait_ge(xn_ps, 4 * (b - 1))
                src = a["ctx"] if b == 0 else a["x"][(b - 1) * BLK:b * BLK, :]
                sp.dma_start(xs[:, b % 2], src.rearrange("(t p) d -> p t d", p=P)).then_inc(x_in[b % 2], 16)

            load_wmod(0)
            load_wmod(1)
            load_x(0)
            load_wmod(2)
            load_wmod(3)

            def load_w_in(i):
                lo, hi = ((COL_U, COL_Q), (COL_Q, N_IN), (0, COL_U))[i]
                sp.dma_start(w_in[:, :, lo:hi], a["w_in"][:, :, lo:hi]).then_inc(w_in_in[i], 16)

            load_w_in(0)
            load_w_in(1)
            sp.wait_ge(mcol_ps, 1)
            load_x(1)

            sp.wait_ge(mats_done, 2)
            for ri in range(2):
                sp.dma_start(R_d[:, 0:UP, ri, :], cA[:, ri, 0:UP, GH:(CH + 1) * GH]).then_inc(mats_stored, 16)
                sp.dma_start(R_d[:, UP:NU, ri, :], cA[:, ri, UP:NU, 0:CH * GH]).then_inc(mats_stored, 16)
            load_w_in(2)
            load_x(2)
            sp.wait_ge(tab2_done, 1)
            sp.dma_start(tab_d[UP:NU].rearrange("u p c n -> p u c n"), tab2).then_inc(tab2_stored, 16)
            sp.wait_ge(K_done, 1)
            for s in range(CH):
                sp.dma_start(M_d[s * GH:(s + 1) * GH, :, :],
                             Kfull[:, :, (CH - 1 - s) * GH:(2 * CH - 1 - s) * GH]).then_inc(mats_stored, 16)
            def store_U(b):
                sp.wait_ge(turn_out, turns_before(b + 1))
                sp.dma_start(U_d[:, :, b * CB:(b + 1) * CB], U_st[:, b % 2].rearrange("p (g c) -> p g c", c=CB)).then_inc(U_stored[b % 2], 16)

            for b in range(NBLK):
                if b >= 1:
                    if b >= 3:
                        sp.wait_ge(qk_done, TPB * (b - 1))
                    sp.dma_start(rope[:, b % 2], a["rope"][b - 1]).then_inc(rope_in[b % 2], 16)
                if 1 <= b < NBLK - 2:
                    load_x(b + 2)
                if b >= 1:
                    store_U(b - 1)

            sp.wait_ge(kv_ps, TPB * NBLK)
            sp.wait_ge(xn_ps, 4 * NBLK)

            def load_wm2(i):
                c = MOD2[i]
                if i >= 1:
                    sp.wait_ge(m2_ps, i)
                sp.dma_start(wm2, wm_src[:, :, c * 512:(c + 1) * 512]).then_inc(wm2_in, 16)

            load_wm2(0)
            sp.wait_ge(xn_out, 4 * NBLK)
            sp.dma_start(R, R_d).then_inc(mats_in, 16)
            sp.dma_start(M, M_d).then_inc(mats_in, 16)
            store_U(NBLK - 1)
            sp.wait_ge(U_stored[0], 16 * 5)
            sp.wait_ge(U_stored[1], 16 * 4)
            sp.dma_start(U, U_d).then_inc(U_in, 16)
            sp.wait_ge(turn_ps, turns_before(NBLK))
            sp.dma_start(g1bc, a["b_mod"][2:3, :].to_broadcast([P, D])).then_inc(mats_in, 16)
            sp.dma_start(g2bc, a["b_mod"][5:6, :].to_broadcast([P, D])).then_inc(mats_in, 16)
            load_wm2(1)
            for i in range(2, 8):
                load_wm2(i)
            sp.wait_ge(pv_ps, pt_before(NGRP))
            sp.dma_start(w_glu, a["w_glu"].rearrange("(k p) n -> p k n", p=P)).then_inc(wglu_in, 16)
            sp.wait_ge(unit_done, NU)
            sp.dma_start(w_out, a["w_out"]).then_inc(w_out_in, 16)
            sp.dma_start(r_w, a["router_w"]).then_inc(w_out_in, 16)

            def load_xo(pp):
                if pp < 2:
                    sp.wait_ge(yt_ps, 8)
                else:
                    sp.wait_ge(t2_ps, 4 * (pp - 1))
                sp.dma_start(xo[:, pp % 2], a["x"][pp * BLK:(pp + 1) * BLK, :].rearrange("(t p) d -> p t d", p=P))\
                    .then_inc(xo_in[pp % 2], 16)

            load_xo(0)
            load_xo(1)
            for pp in range(NPP):
                sp.wait_ge(hm_done, pp + 1)
                sp.dma_start(h_d[TPB * pp:TPB * (pp + 1)].rearrange("t p d -> p t d"), hm).then_inc(h_stored, 16)
                sp.wait_ge(x2_scaled, pp + 1)
                sp.dma_start(x2_d[pp * BLK:(pp + 1) * BLK, :].rearrange("(t p) d -> p t d", p=P), xo[:, pp % 2])\
                    .then_inc(x2_stored, 16)
                if pp + 2 < NPP:
                    sp.wait_ge(x2_stored, 16 * (pp + 1))
                    load_xo(pp + 2)
            sp.wait_ge(o2_ps, 4 * NPP)
            sp.dma_start(restart, a["restart"]).then_inc(cst_in, 16)
            sp.wait_ge(o2_out, 4 * NPP)
            sp.dma_start(cst, a["cst"][:, 0:384]).then_inc(cst_in, 16)
            sp.dma_start(earlier_st, a["cst"][:, 384:384 + P]).then_inc(cst_in, 16)
            sp.wait_ge(h_stored, 16 * NPP)
            sp.wait_ge(std2_done, NPP)
            sp.wait_ge(x2_scaled, NPP)
            sp.dma_start(wsh, a["w_sh"]).then_inc(wsh_in, 16)
            sp.wait_ge(shu_ps, TB)
            sp.wait_ge(prod_done, TB)

            def serve_turn(it):
                if not first(it):
                    sp.wait_ge(base_done, it)
                sp.dma_start(hb.unsqueeze(1), h_d[bass.ds(it, 1)].rearrange("n p d -> p n d")).then_inc(hb_in, 16)
                for s in range(tiles_in(it)):
                    sp.wait_ge(yo_done, it * (2 * STEPS) + 2 * (s + 1))
                    sp.dma_start(pair_t[bass.ds(it * STEPS + s, 1)].rearrange("n p d -> p n d"),
                                 yo[:, s % 3].unsqueeze(1)).then_inc(yo_stored[s % 3], 16)

            serve_turn(0)
            with sp.Fori(1, TURNS - 1) as it:
                serve_turn(it)
            serve_turn(TURNS - 1)
            with sp.Fori(0, NTILE) as t:
                sp.wait_ge(sum_step, t * TOPK + TOPK)
                sp.dma_start(out_t[bass.ds(t, 1)].rearrange("n p d -> p n d"), y[:, bass.ds(t, 1), :])\
                    .then_inc(out_stored, 16)
            sp.wait_ge(out_stored, 16 * NTILE)

        @block.gpsimd
        def _(pool):
            steps = [0]

            def link(ins):
                steps[0] += 1
                ins.then_inc(pool_step, 1)
                pool.wait_ge(pool_step, steps[0])

            pool.wait_ge(ident_in, 32)
            pool.tensor_copy(identb[:, :], ident[:, :])
            pool.tensor_copy(maskb[:, :], mask_st).then_inc(consts_b, 1)
            pool.wait_ge(consts_b, 1)
            pool.wait_ge(trig_done, 2)
            pool.wait_ge(unit_cs, 1)
            cosm, sinm = SM[4], SM[3]
            us = slice(0, UP)
            pool.memset(tab[:, :, 0, 0:1], 1.0)
            pool.memset(tab[:, :, 1, 0:1], 0.0)
            pool.tensor_copy(tab[:, :, 0, 1:2], cosm[:, us, RISE + CH:RISE + CH + 1])
            link(pool.tensor_copy(tab[:, :, 1, 1:2], sinm[:, us, RISE + CH:RISE + CH + 1]))
            for j in range(1, DOUBLINGS + 1):
                lo = 1 << j
                n = min(lo, NCHUNK - lo)
                co, si = tab[:, :, 0, 0:n], tab[:, :, 1, 0:n]
                cm = cosm[:, us, DBL + j - 1:DBL + j].to_broadcast([P, UP, n])
                sm = sinm[:, us, DBL + j - 1:DBL + j].to_broadcast([P, UP, n])
                t0 = ptmp[:, 0, 0:UP * n].rearrange("p (u n) -> p u n", n=n)
                t1 = ptmp[:, 1, 0:UP * n].rearrange("p (u n) -> p u n", n=n)
                pool.tensor_tensor(t0, si, sm, ALU.mult)
                link(pool.tensor_tensor(t1, si, cm, ALU.mult))
                pool.tensor_tensor(tab[:, :, 0, lo:lo + n], co, cm, ALU.mult)
                link(pool.tensor_tensor(tab[:, :, 1, lo:lo + n], co, sm, ALU.mult))
                pool.tensor_tensor(tab[:, :, 0, lo:lo + n], tab[:, :, 0, lo:lo + n], t0, ALU.subtract)
                link(pool.tensor_tensor(tab[:, :, 1, lo:lo + n], tab[:, :, 1, lo:lo + n], t1, ALU.add))
            pool.dma_start(tab_d[us].rearrange("u p c n -> p u c n"), tab).then_inc(tab_stored, 16)
            pool.wait_ge(turn_ps, turns_before(NBLK))
            pool.wait_ge(qk_done, TPB * NBLK)
            pool.wait_ge(cc_out, 16)
            pool.wait_ge(cb_out, 16)

            def load_drive(u):
                if u >= 2:
                    pool.wait_ge(xr_ps, 2 * (u - 1))
                pool.dma_start(ust[:, u % 2, 0:2 * P].rearrange("p (c m) -> p c m", m=P), drvT_d[u])\
                    .then_inc(drv_in[u % 2], 16)

            def load_phases(u):
                if u >= 2:
                    pool.wait_ge(unit_done, u - 1)
                pool.dma_start(ust[:, u % 2, 2 * P:].rearrange("p (c m) -> p c m", m=NCHUNK), tab_d[u])\
                    .then_inc(phase_in[u % 2], 16)

            def conv_piece(n):
                h, q = n // 4, n % 4
                lo, hi = q * 512, (q + 1) * 512
                v = mixT[:, 2 + h]
                acc, t = ctmp[:, 0], ctmp[:, 1]
                w = [pk("conv_w", 3 * h + j, 1) for j in range(3)]
                if n == 0:
                    pool.wait_ge(kv_ps, TPB * NBLK)
                lo1 = max(lo, 1)
                hi1 = min(hi, SEQ - 1)
                pool.tensor_scalar(acc, v[:, lo:hi], w[1], 1.0, ALU.mult, ALU.mult)
                link(pool.tensor_scalar(t[:, lo1 - lo:512], v[:, lo1 - 1:hi - 1], w[0], 1.0, ALU.mult, ALU.mult))
                link(pool.tensor_tensor(acc[:, lo1 - lo:512], acc[:, lo1 - lo:512], t[:, lo1 - lo:512], ALU.add))
                link(pool.tensor_scalar(t[:, 0:hi1 - lo], v[:, lo + 1:hi1 + 1], w[2], 1.0, ALU.mult, ALU.mult))
                link(pool.tensor_tensor(acc[:, 0:hi1 - lo], acc[:, 0:hi1 - lo], t[:, 0:hi1 - lo], ALU.add))
                pool.tensor_tensor(mixT[:, h, lo:hi], mixT[:, h, lo:hi], acc, ALU.mult).then_inc(conv_done, 1)
                pool.wait_ge(conv_done, n + 1)

            for u in range(2):
                load_drive(u)
                load_phases(u)
            for g in range(NGRP):
                u = g // 2
                if g % 2 == 0 and 1 <= u < NU - 1:
                    load_drive(u + 1)
                if g % 2 == 0 and u >= 2:
                    load_phases(u)
                pool.wait_ge(rden_done, g + 1)
                n = n_keys(g)
                for j in range(QPK):
                    p = Pb[:, (g % 2) * QPK + j, 0:n]
                    ins = pool.tensor_scalar(p, p, rden[:, g % 2, j:j + 1], 1.0, ALU.mult, ALU.mult)
                ins.then_inc(P_done, 1)
                if g < 8:
                    conv_piece(g)
            pool.wait_ge(cst_in, 48)
            pool.wait_ge(std2_done, NPP)
            pool.memset(ones_b, 1.0)
            pool.tensor_copy(earlier, earlier_st).then_inc(consts_b, 1)
            pool.wait_ge(x2_stored, 16 * NPP)
            pool.wait_ge(t2_ps, 4 * NPP)

            def product(tb):
                pool.wait_ge(sh_act, tb + 1)
                pool.tensor_tensor(hsh[:, tb], hsh[:, tb], sl2[:, tb % 2], ALU.mult).then_inc(prod_done, 1)

            for tb in range(TB):
                product(tb)

            pool.wait_ge(shg_ps, TB)
            pool.wait_ge(shu_ps, TB)

            def take_tok(it, s):
                if not (first(it) and s < 3):
                    pool.wait_ge(xt_ps, it * (2 * STEPS) + 2 * (s - 2))
                pool.tensor_copy(tok_cur[s % 3][:, :], tok_idx[:, bass.ds(it * STEPS + s, 1)]).then_inc(tok_cur_done, 1)

            def fetch(it, s):
                i, n = s % 3, it * STEPS + s
                pool.wait_ge(tok_cur_done, n + 1)
                if first(it) and s < 3:
                    take_tok(it, s + 1)
                    pool.indirect_dma_start(xg[:, i], None, x2_d,
                                            bass.IndirectOffsetOnAxis(ap=tok_cur[i][:, :], axis=0)).then_inc(xg_in[i], 16)
                    return
                pool.wait_ge(yd_ps, it * (2 * STEPS) + 2 * (s - 2))
                pool.tensor_copy(w_cur[i][:, :], w_idx[:, bass.ds(n, 1)]).then_inc(w_cur_done, 1)
                pool.indirect_dma_start(xg[:, i], None, x2_d, bass.IndirectOffsetOnAxis(ap=tok_cur[i][:, :], axis=0))\
                    .then_inc(xg_in[i], 16)
                pool.wait_ge(w_cur_done, n + 1)
                if not (type(n) is int and n == NT - 1):
                    take_tok(it, s + 1)
                pool.indirect_dma_start(wx[i].rearrange("p a b -> p (a b)"), None, a["w_exp"],
                                        bass.IndirectOffsetOnAxis(ap=w_cur[i][:, :], axis=0)).then_inc(wx_in[i], 16)

            def fetch_turn(it):
                for s in range(tiles_in(it)):
                    fetch(it, s)

            pool.wait_ge(reached_done, 2)
            for i in range(3):
                pool.tensor_copy(w_cur[i][:, :], w_idx[:, i:i + 1]).then_inc(w_cur_done, 1)
                pool.wait_ge(w_cur_done, i + 1)
                pool.indirect_dma_start(wx[i].rearrange("p a b -> p (a b)"), None, a["w_exp"],
                                        bass.IndirectOffsetOnAxis(ap=w_cur[i][:, :], axis=0)).then_inc(wx_in[i], 16)
            pool.wait_ge(idx_done, 1)
            take_tok(0, 0)
            fetch_turn(0)
            with pool.Fori(1, TURNS - 1) as it:
                fetch_turn(it)
            fetch_turn(TURNS - 1)

            pool.wait_ge(yd_ps, 2 * NT)
            for i in range(3):
                pool.wait_ge(yo_stored[i], 16 * len(range(i, NT, 3)))

            def take_slots(it, j):
                if not (type(it) is int and it * SETS + j < SETS):
                    pool.wait_ge(sum_step, it * (SETS * TOPK) + TOPK * (j + 1 - SETS))
                for k in range(TOPK):
                    ins = pool.tensor_copy(slot_cur[j % SETS][k][:, :], slot_idx[:, bass.ds(it * SETS + j, 1), k])
                ins.then_inc(slot_cur_done, 1)

            def gather_rows(it, j):
                t = it * SETS + j
                pool.wait_ge(slot_cur_done, t + 1)
                if not (type(t) is int and t == NTILE - 1):
                    take_slots(it, j + 1)
                for k in range(TOPK):
                    pool.indirect_dma_start(gb[:, TOPK * j + k], None, pair_d,
                                            bass.IndirectOffsetOnAxis(ap=slot_cur[j][k][:, :], axis=0))\
                        .then_inc(gb_in[j], 16)

            take_slots(0, 0)
            for j in range(SETS):
                gather_rows(0, j)
            with pool.Fori(1, NTILE // SETS - 1) as it:
                for j in range(SETS):
                    gather_rows(it, j)
            for j in range(SETS):
                gather_rows(NTILE // SETS - 1, j)

        @block.scalar
        def _(act):
            steps = [0]

            def link(ins):
                steps[0] += 1
                ins.then_inc(act_step, 1)
                act.wait_ge(act_step, steps[0])

            act.wait_ge(pack_in, 16)
            act.activation(silu_c[:, :, :], pk("c").rearrange("p (k j) -> p k j", j=2), ACT.Silu).then_inc(silu_done, 1)
            act.wait_ge(args_done, 1)
            act.activation(SM[3], SM[0], ACT.Sin).then_inc(trig_done, 1)
            act.activation(SM[5], SM[0], ACT.Sin, scale=0.5).then_inc(trig_done, 1)
            for n in range(4):
                act.wait_ge(wmod_used, n + 1)
                act.activation(mrows[:, n], PS[7 * (n % 2)][0:2, :], ACT.Copy).then_inc(mrow_out, 1)
            act.wait_ge(unit_cs, 1)

            def norm(b):
                act.wait_ge(x_in[b % 2], 16 * (b // 2 + 1))
                if b >= 2:
                    act.wait_ge(x_scaled, b - 1)
                for t in range(TPB):
                    link(act.activation(junk, xs[:, b % 2, t], ACT.Square, accum_out=ss[:, b % 2, t:t + 1]))
                act.activation(ss[:, b % 2], ss[:, b % 2], ACT.Sqrt, scale=1.0 / D, bias=eps[:, :]).then_inc(std_done, 1)

            norm(0)
            for q in range(8):
                act.wait_ge(drvT_ps, q + 1)
                if q >= 2:
                    act.wait_ge(drvT_stored[q % 2], 16 * (q // 2))
                act.activation(drvT_st[:, q % 2], PS[1 + q % 2][:, :], ACT.Copy).then_inc(drvT_out, 1)
                act.wait_ge(drvT_out, q + 1)
                ri, u0 = q // 4, 4 * (q % 4)
                act.dma_start(drvT_d[u0:u0 + 4, :, ri, :].rearrange("u p m -> p u m"),
                              drvT_st[:, q % 2].rearrange("p (u m) -> p u m", m=P)).then_inc(drvT_stored[q % 2], 16)

            norm(1)
            for b in range(NBLK):
                tok = slice((b - 1) * BLK, b * BLK)
                if b >= 1:
                    for h in range(2):
                        n = 2 * (b - 1) + h
                        act.wait_ge(cx_ps, n + 1)
                        if n >= 1:
                            act.wait_ge(cc_out, n)
                        act.activation(xtmp, PS[2][:, 0:BLK], ACT.Copy).then_inc(cx_out, 1)
                        act.wait_ge(cb_ps, n + 1)
                        act.wait_ge(tab_stored, 16)
                        act.activation(mixT[:, h, tok], PS[4][:, 0:BLK], ACT.Copy).then_inc(cb_out, 1)
                act.wait_ge(u_ps, b + 1)
                if b >= 1:
                    act.wait_ge(turn_ps, turns_before(b - 1) + 4)
                act.activation(uT, PS[4][:, :].rearrange("p (a b) -> p a b", b=BLK), ACT.Copy).then_inc(u_out, 1)
                if 1 <= b < NBLK - 2:
                    norm(b + 2)
                if b == 0:
                    act.wait_ge(pool_step, TAB_STEPS)
                for t in range(TPB):
                    m = TPB * b + t
                    if m >= 1:
                        act.wait_ge(qk_done, m)
                    if b >= 1:
                        act.wait_ge(q_out, m - TPB + 1)
                        act.activation(sq[:, 0:8], PS[5][:, :].rearrange("p (h d) -> p h d", d=HD),
                                       ACT.Square).then_inc(q_sq, 1)
                    act.wait_ge(k_out, m + 1)
                    act.activation(sq[:, 8:10], PS[6][:, 0:P].rearrange("p (h d) -> p h d", d=HD),
                                   ACT.Square).then_inc(k_sq, 1)
                    act.activation(V[:, m], PS[6][:, P:2 * P], ACT.Copy).then_inc(v_out, 1)
                    act.wait_ge(hs_done, m + 1)
                    act.activation(hstd[:, :], hs[:, :], ACT.Sqrt, scale=1.0 / HD, bias=eps[:, :]).then_inc(hstd_done, 1)
                if b == 0:
                    norm(2)

            def exponentials(g, j):
                H, half = QPK * g + j, n_keys(g) // 2
                act.wait_ge(negm_done, H + 1)
                if g >= 2:
                    act.wait_ge(pt_ps, pt_before(g - 1))
                src = banks[:, 2 * (H % 2):2 * (H % 2) + 2, 0:half]
                act.activation(Pb[:, (g % 2) * QPK + j, 0:2 * half].rearrange("p (a b) -> p a b", b=half), src,
                               ACT.Exp, bias=negm[:, g % 2, j:j + 1], scale=SCALE,
                               accum_out=rs[:, g % 2, j:j + 1]).then_inc(exp_done, 1)
                if j == QPK - 1:
                    act.wait_ge(es_in, g + 1)
                    act.activation(esink[:, g % 2], esink[:, g % 2], ACT.Exp).then_inc(es_done, 1)

            for g in range(NGRP + 1):
                for step, n in turn_steps(g):
                    if step == "head":
                        exponentials(g, n)
                    J = pt_before(g - 1) + n if step == "tile" else 0
                    if J % 2 == 1:
                        act.wait_ge(pt_ps, J + 1)
                        if J >= 2:
                            act.wait_ge(pv_ps, J - 1)
                        act.activation(PT[:, 1], PS[5], ACT.Copy).then_inc(pt_act, 1)
                if g < 2 * NU:
                    u, ri = g // 2, g % 2
                    act.wait_ge(xr_ps, g + 1)
                    if u >= 1:
                        act.wait_ge(rotated, u)
                    if u < UP:
                        act.activation(rot[:, ri], PS[7][:, 0:NCHUNK], ACT.Copy).then_inc(xr_out, 1)
                    else:
                        act.activation(rot[:, ri, 0:CCTX], PS[7][:, 0:CCTX][:, ::-1], ACT.Copy)
                        act.activation(rot[:, ri, CCTX:NCHUNK], PS[7][:, CCTX:NCHUNK][:, ::-1], ACT.Copy)\
                            .then_inc(xr_out, 1)
            for r in range(8):
                act.wait_ge(y_ps, r + 1)
                dst = Yc[:, r // 4].rearrange("p t (a s q h) -> p a q s t h", a=2, q=2, h=GH)
                src = PS[r].rearrange("p (s t h) -> p s t h", t=CH, h=GH)
                act.activation(dst[:, (r // 2) % 2, r % 2], src, ACT.Gelu_apprx_tanh).then_inc(y_out, 1)
            for w in range(8):
                act.wait_ge(z_ps, w + 1)
                if w >= 2:
                    act.wait_ge(glu_done, w - 1)
                act.activation(th[:, w % 2], PS[w], ACT.Tanh, scale=0.5, bias=hbglu[:, w % 2:w % 2 + 1]).then_inc(z_out, 1)
            def statistics(pp):
                act.wait_ge(hm_done, pp + 1)
                if pp >= 2:
                    act.wait_ge(x2_scaled, pp - 1)
                for t in range(TPB):
                    link(act.activation(junk2, hm[:, t], ACT.Square, accum_out=ss[:, pp % 2, t:t + 1]))
                act.activation(ss[:, pp % 2], ss[:, pp % 2], ACT.Sqrt, scale=1.0 / D, bias=eps[:, :]).then_inc(std2_done, 1)

            statistics(0)
            act.wait_ge(mod2_done, 1)
            for pp in range(NPP):
                for q in range(4):
                    act.wait_ge(t2_ps, 4 * pp + q + 1)
                    for i in range(2):
                        k = 2 * q + i
                        ins = act.activation(tT[:, k, pp * BLK:(pp + 1) * BLK], PS[4 + q % 2][:, i * BLK:(i + 1) * BLK],
                                             ACT.Identity, scale=scale2[:, k:k + 1], bias=mod2[:, k:k + 1])
                    ins.then_inc(t2_out, 1)
                if pp + 1 < NPP:
                    statistics(pp + 1)
                act.wait_ge(lg_ps, pp + 1)
                act.activation(lgt[:, TPB * pp:TPB * (pp + 1)], PS[6 + pp % 2][:, 0:TPB * NR]
                               .rearrange("p (t r) -> p t r", r=NR), ACT.Copy).then_inc(lg_out, 1)
            act.wait_ge(lg_out, NPP)
            act.activation(lgt, lgt, ACT.Sigmoid).then_inc(sig_done, 1)

            act.wait_ge(o2_ps, 4 * NPP)
            act.wait_ge(x2_stored, 16 * NPP)
            for tb in range(TB):
                act.wait_ge(shg_ps, tb + 1)
                if tb >= 2:
                    act.wait_ge(prod_done, tb - 1)
                act.activation(sl2[:, tb % 2], PS[tb % 2], ACT.Silu)
                act.wait_ge(shu_ps, tb + 1)
                act.activation(hsh[:, tb], PS[2 + tb % 2], ACT.Copy).then_inc(sh_act, 1)
            act.wait_ge(reached_done, 1)
            act.wait_ge(prod_done, TB)
            for d in range(2 * NTILE):
                act.wait_ge(shy_ps, d + 1)
                act.activation(y[:, d // 2, (d % 2) * 512:(d % 2 + 1) * 512], PS[d % 4], ACT.Copy).then_inc(ysh_out, 1)

            def turned(it, s):
                n = it * STEPS + s
                act.wait_ge(xt_ps, it * (2 * STEPS) + 2 * s + 1)
                if not (first(it) and s < 2):
                    act.wait_ge(hu_ps, it * STEPS + (s - 1))
                for k in range(4):
                    ins = act.activation(xT[:, s % 2, k], PS[0][:, k * P:(k + 1) * P], ACT.Identity,
                                         scale=scale2[:, k:k + 1], bias=mod2[:, k:k + 1])
                ins.then_inc(xt_act, 1)

            def silu(it, s):
                act.wait_ge(hg_ps, it * STEPS + (s + 1))
                if not (first(it) and s < 2):
                    act.wait_ge(h_done, it * STEPS + (s - 1))
                act.activation(slx[:, s % 2], PS[4 + s % 2][:, 0:P], ACT.Silu).then_inc(sl_out, 1)

            turned(0, 0)
            for s in range(1, STEPS):
                turned(0, s)
                silu(0, s - 1)
            with act.Fori(1, TURNS - 1) as it:
                for s in range(STEPS):
                    turned(it, s)
                    silu(it, s - 1)
            for s in range(LAST):
                turned(TURNS - 1, s)
                silu(TURNS - 1, s - 1)
            silu(TURNS - 1, LAST - 1)

        @block.vector
        def _(dve):
            steps = [0]

            def link(ins):
                steps[0] += 1
                ins.then_inc(dve_step, 1)
                dve.wait_ge(dve_step, steps[0])

            def tt(o, x, z, op):
                return dve.tensor_tensor(o, x, z, op)

            dve.memset(eps[:, :], EPS)
            dve.wait_ge(pack_in, 16)
            dve.tensor_scalar(nsink[:, :], pk("sink"), -1.0, None, ALU.mult)
            dve.tensor_scalar(hbglu[:, :], pk("b_glu"), 0.5, None, ALU.mult)
            rr, am, e_, sn, cs, sh = SM[0], SM[1], SM[2], SM[3], SM[4], SM[5]
            w = SM[6].rearrange("p a b -> p (a b)")
            dt, la, lo_, t0, t1, nr, ni, rd, kr, ki = (w[:, NU * i:NU * (i + 1)] for i in range(10))

            def exact_exp(o, x, n, bits):
                link(dve.tensor_scalar(n, x, 1.0 / math.log(2.0), ROUND, ALU.mult, ALU.add))
                link(dve.tensor_scalar(n, n, ROUND, None, ALU.subtract))
                for part in (LN2_A, LN2_B):
                    link(dve.scalar_tensor_tensor(out=x, in0=n, scalar=-part, in1=x, op0=ALU.mult, op1=ALU.add))
                link(dve.tensor_scalar(o, x, 1.0 / math.factorial(8), None, ALU.mult))
                for j in range(7, 0, -1):
                    link(dve.scalar_tensor_tensor(out=o, in0=o, scalar=1.0 / math.factorial(j), in1=x,
                                                  op0=ALU.add, op1=ALU.mult))
                dve.tensor_scalar(o, o, 1.0, None, ALU.add)
                link(dve.tensor_scalar(n, n, -127.0, 128.0, ALU.max, ALU.min))
                link(dve.tensor_scalar(n, n, 127.0, 2.0 ** 23, ALU.add, ALU.mult))
                link(dve.tensor_copy(bits, n))
                link(tt(o, o, bits.bitcast(F32), ALU.mult))

            link(dve.tensor_copy(t0, pk("log_dt")))
            exact_exp(dt, t0, t1, nr.bitcast(mybir.dt.int32))
            tt(la, pk("lam_re"), dt, ALU.mult)
            link(tt(lo_, pk("lam_im"), dt, ALU.mult))

            def reduce_angle(x, n):
                link(dve.tensor_scalar(n, x, INV_2PI, ROUND, ALU.mult, ALU.add))
                link(dve.tensor_scalar(n, n, ROUND, None, ALU.subtract))
                for part in (PI_A, PI_B):
                    link(dve.scalar_tensor_tensor(out=x, in0=n, scalar=-part, in1=x, op0=ALU.mult, op1=ALU.add))
                return dve.scalar_tensor_tensor(out=x, in0=n, scalar=-PI_C, in1=x, op0=ALU.mult, op1=ALU.add)

            link(reduce_angle(lo_, t0))
            mult = pk("mults").unsqueeze(1).to_broadcast([P, NU, NM])
            tt(rr, lo_.unsqueeze(2).to_broadcast([P, NU, NM]), mult, ALU.mult)
            link(tt(am, la.unsqueeze(2).to_broadcast([P, NU, NM]), mult, ALU.mult))
            flat = [s.rearrange("p a b -> p (a b)") for s in (rr, cs)]
            reduce_angle(flat[0], flat[1]).then_inc(args_done, 1)
            link(tt(t0, pk("lam_re"), pk("lam_re"), ALU.mult))
            link(tt(t1, pk("lam_im"), pk("lam_im"), ALU.mult))
            link(tt(t0, t0, t1, ALU.add))
            link(dve.reciprocal(rd, t0))
            three = "p (u n) -> p u n"
            exact_exp(e_[:, :, 0:NPOW], am[:, :, 0:NPOW], tmpA[:, 0:NU * NPOW].rearrange(three, n=NPOW),
                      tmpB[:, 0:NU * NPOW].rearrange(three, n=NPOW).bitcast(mybir.dt.int32))
            dve.wait_ge(trig_done, 2)
            link(tt(cs, sh, sh, ALU.mult))
            dve.tensor_scalar(cs, cs, -2.0, 1.0, ALU.mult, ALU.add).then_inc(unit_cs, 1)
            dve.wait_ge(unit_cs, 1)
            dve.tensor_copy(r8[:, :], e_[:, :, RISE + CH])
            pr, pi_ = am, sh
            tt(pr[:, :, 0:NPOW], e_[:, :, 0:NPOW], cs[:, :, 0:NPOW], ALU.mult)
            link(tt(pi_[:, :, 0:NPOW], e_[:, :, 0:NPOW], sn[:, :, 0:NPOW], ALU.mult))
            dve.tensor_copy(ni, pi_[:, :, RISE + 1])
            link(dve.tensor_scalar(nr, pr[:, :, RISE + 1], -1.0, None, ALU.add))
            lr, li = pk("lam_re"), pk("lam_im")
            tt(t0, nr, lr, ALU.mult)
            link(tt(t1, ni, li, ALU.mult))
            link(tt(kr, t0, t1, ALU.add))
            tt(t0, ni, lr, ALU.mult)
            link(tt(t1, nr, li, ALU.mult))
            link(tt(ki, t0, t1, ALU.subtract))
            tt(kr, kr, rd, ALU.mult)
            link(tt(ki, ki, rd, ALU.mult))

            def b3(v, n):
                return v.unsqueeze(2).to_broadcast([P, v.shape[1], n])

            dve.wait_ge(raw_in, 16)
            v0 = tmpA[:, 0:256].rearrange("p (u h) -> p u h", h=GH)
            v1 = tmpB[:, 0:256].rearrange("p (u h) -> p u h", h=GH)
            for ri, (x, z, op) in enumerate(((0, 1, ALU.subtract), (1, 0, ALU.add))):
                tt(v0, raw[:, x], b3(kr, GH), ALU.mult)
                link(tt(v1, raw[:, z], b3(ki, GH), ALU.mult))
                link(tt(bbar[:, ri], v0, v1, op))

            def cmul(o_re, o_im, x_re, x_im, z_re, z_im, n, negate):
                tA = tmpA[:, 0:UP * n * GH].rearrange("p (u n h) -> p u n h", n=n, h=GH)
                tB = tmpB[:, 0:UP * n * GH].rearrange("p (u n h) -> p u n h", n=n, h=GH)

                def pw(v):
                    return v.unsqueeze(3).to_broadcast([P, UP, n, GH])

                def vec(v):
                    return v.unsqueeze(2).to_broadcast([P, UP, n, GH])

                tt(tA, pw(x_re), vec(z_re), ALU.mult)
                link(tt(tB, pw(x_im), vec(z_im), ALU.mult))
                link(tt(o_re, tA, tB, ALU.subtract))
                tt(tA, pw(x_re), vec(z_im), ALU.mult)
                link(tt(tB, pw(x_im), vec(z_re), ALU.mult))
                if negate:
                    link(dve.tensor_scalar(tA, tA, -1.0, None, ALU.mult))
                    return tt(o_im, tA, tB, ALU.subtract)
                return tt(o_im, tA, tB, ALU.add)

            for d in range(2):
                us = slice(d * UP, (d + 1) * UP)
                lo = 1 if d == 0 else RISE
                o = [drv[:, ri, us].rearrange("p u (s h) -> p u s h", h=GH) for ri in range(2)]
                cmul(o[0], o[1], pr[:, us, lo:lo + CH], pi_[:, us, lo:lo + CH], bbar[:, 0, us], bbar[:, 1, us], CH,
                     False).then_inc(drv_done, 1)
                dve.wait_ge(drv_done, d + 1)
            for d in range(2):
                us = slice(d * UP, (d + 1) * UP)
                lo = RISE if d == 0 else 0
                o = [cA[:, ri, us].rearrange("p u (s h) -> p u s h", h=GH) for ri in range(2)]
                cmul(o[0], o[1], pr[:, us, lo:lo + CH + 1], pi_[:, us, lo:lo + CH + 1], raw[:, 2, us], raw[:, 3, us],
                     CH + 1, True).then_inc(mats_done, 1)
                dve.wait_ge(mats_done, d + 1)
            dve.wait_ge(mcol_ps, 1)
            mp = PS[0][:, 0:4 * KD].rearrange("p (m j) -> p m j", j=2)
            tt(shift1[:, :, :], mp[:, 0:KD], b3(pk("b_mod", 0, KD), 2), ALU.add)
            link(tt(scale1[:, :, :], mp[:, KD:2 * KD], b3(pk("b_mod", KD, KD), 2), ALU.add))
            link(dve.tensor_scalar(scale1[:, :, :], scale1[:, :, :], 1.0, None, ALU.add))
            tt(scale1[:, :, :], scale1[:, :, :], b3(pk("norm1"), 2), ALU.mult).then_inc(mod_done, 1)
            dve.wait_ge(mod_done, 1)
            def phase_table():
                cosm, sinm, us = SM[4], SM[3], slice(UP, NU)
                dve.memset(tab2[:, :, 0, 0:1], 1.0)
                dve.memset(tab2[:, :, 1, 0:1], 0.0)
                dve.tensor_copy(tab2[:, :, 0, 1:2], cosm[:, us, RISE + CH:RISE + CH + 1])
                link(dve.tensor_copy(tab2[:, :, 1, 1:2], sinm[:, us, RISE + CH:RISE + CH + 1]))
                for j in range(1, DOUBLINGS + 1):
                    lo = 1 << j
                    n = min(lo, NCHUNK - lo)
                    co, si = tab2[:, :, 0, 0:n], tab2[:, :, 1, 0:n]
                    cm = cosm[:, us, DBL + j - 1:DBL + j].to_broadcast([P, UP, n])
                    sm = sinm[:, us, DBL + j - 1:DBL + j].to_broadcast([P, UP, n])
                    t0 = tmpA[:, 0:UP * n].rearrange("p (u n) -> p u n", n=n)
                    t1 = tmpB[:, 0:UP * n].rearrange("p (u n) -> p u n", n=n)
                    tt(t0, si, sm, ALU.mult)
                    link(tt(t1, si, cm, ALU.mult))
                    tt(tab2[:, :, 0, lo:lo + n], co, cm, ALU.mult)
                    link(tt(tab2[:, :, 1, lo:lo + n], co, sm, ALU.mult))
                    tt(tab2[:, :, 0, lo:lo + n], tab2[:, :, 0, lo:lo + n], t0, ALU.subtract)
                    last = tt(tab2[:, :, 1, lo:lo + n], tab2[:, :, 1, lo:lo + n], t1, ALU.add)
                    if j < DOUBLINGS:
                        link(last)
                last.then_inc(tab2_done, 1)

            def scale_x(b):
                dve.wait_ge(std_done, b + 1)
                link(dve.reciprocal(rstd[:, :], ss[:, b % 2]))
                for t in range(TPB):
                    ins = dve.tensor_scalar(xs[:, b % 2, t], xs[:, b % 2, t], rstd[:, t:t + 1], None, ALU.mult)
                ins.then_inc(x_scaled, 1)
                dve.wait_ge(x_scaled, b + 1)

            def modulate_xT(b):
                if b >= 2:
                    dve.wait_ge(kv_ps, TPB * (b - 1))
                j = 1 if b == 0 else 0
                for q in range(4):
                    dve.wait_ge(xn_ps, 4 * b + q + 1)
                    for i in range(2):
                        k = 2 * q + i
                        ins = dve.tensor_scalar(xnT[:, b % 2, k], PS[q % 2][:, i * BLK:(i + 1) * BLK],
                                                scale1[:, k, j:j + 1], shift1[:, k, j:j + 1], ALU.mult, ALU.add)
                    ins.then_inc(xn_out, 1)

            def take_turns(b):
                base = turns_before(b)

                for i in range(4):
                    dve.wait_ge(turn_ps, base + i + 1)
                    if i == 0 and b >= 1:
                        dve.wait_ge(turn_out, base)
                    src = PS[7 - i % 2][0:CB, :].rearrange("p (s g h) -> p s g h", s=2, h=GH)
                    dst = Uc[:, :, 2 * i:2 * i + 2, :].rearrange("p g s h -> p s g h")
                    dve.tensor_copy(dst, src).then_inc(turn_out, 1)
                i = 4
                if b >= 1:
                    for t in range(TPB):
                        tile = TPB * (b - 1) + t
                        dve.wait_ge(turn_ps, base + i + 1)
                        dst = mixT[:, 4:8, tile * P:(tile + 1) * P]
                        dve.tensor_copy(dst, PS[7 - i % 2][:, :].rearrange("p (j q) -> p j q", q=P)).then_inc(turn_out, 1)
                        i += 1
                dve.wait_ge(turn_ps, base + i + 1)
                dve.tensor_copy(kT[:, b * BLK:(b + 1) * BLK], PS[7 - i % 2][:, 0:BLK]).then_inc(turn_out, 1)
                i += 1
                dve.wait_ge(turn_ps, base + i + 1)
                if b >= 2:
                    dve.wait_ge(U_stored[b % 2], 16 * (b // 2))
                dve.tensor_copy(U_st[:, b % 2], PS[7 - i % 2][:, :]).then_inc(turn_out, 1)

            def head_norm(b, t):
                m = TPB * b + t
                h0 = 8 if b == 0 else 0
                if b >= 1:
                    dve.wait_ge(q_ps, m - TPB + 1)
                    tt(qg[:, 0:8], PS[5][:, :].rearrange("p (h d) -> p h d", d=HD),
                       pk("q_g").unsqueeze(1).to_broadcast([P, 8, HD]), ALU.mult).then_inc(q_out, 1)
                dve.wait_ge(kv_ps, m + 1)
                tt(qg[:, 8:10], PS[6][:, 0:P].rearrange("p (h d) -> p h d", d=HD),
                   pk("k_g").unsqueeze(1).to_broadcast([P, 2, HD]), ALU.mult).then_inc(k_out, 1)
                dve.wait_ge(k_sq, m + 1)
                if b == 0:
                    dve.memset(hs[:, 0:8], 1.0)
                dve.tensor_reduce(hs[:, h0:10], sq[:, h0:10], AX.X, ALU.add).then_inc(hs_done, 1)
                dve.wait_ge(hstd_done, m + 1)
                link(dve.reciprocal(hrs[:, :], hstd[:, :]))
                rs3 = hrs[:, h0:10].unsqueeze(2).to_broadcast([P, 10 - h0, HD])
                if b == 0:
                    tt(qkr[:, t, 512:640].rearrange("p (h d) -> p h d", d=HD), qg[:, 8:10], rs3,
                       ALU.mult).then_inc(qk_done, 1)
                    dve.wait_ge(qk_done, m + 1)
                    return
                if t == 0:
                    dve.wait_ge(turn_ps, turns_before(b))
                    dve.wait_ge(rope_in[b % 2], 16 * ((b + 1) // 2))
                link(tt(qg, qg, rs3, ALU.mult))
                cosv = rope[:, b % 2, t, 0:HD].unsqueeze(1).to_broadcast([P, 10, HD])
                tt(rc, qg, cosv, ALU.mult)
                halves = "p h (a f i) -> p h a f i"
                sv = sq.rearrange(halves, a=2, f=2)
                qv = qg.rearrange(halves, a=2, f=2)
                nv = rope[:, b % 2, t, HD:2 * HD].rearrange("p (a f i) -> p a f i", a=2, f=2)
                for f in range(2):
                    last = tt(sv[:, :, :, f], qv[:, :, :, 1 - f], nv[:, :, f].unsqueeze(1).to_broadcast([P, 10, 2, 16]),
                              ALU.mult)
                link(last)
                tt(qkr[:, t].rearrange("p (h d) -> p h d", d=HD), rc, sq, ALU.add).then_inc(qk_done, 1)
                dve.wait_ge(qk_done, m + 1)

            scale_x(0)
            modulate_xT(0)
            phase_table()
            dve.wait_ge(tab2_done, 1)
            dve.wait_ge(pool_step, TAB_STEPS)
            for t in range(TPB):
                head_norm(0, t)
            dve.wait_ge(drvT_ps, 8)
            for q in range(8):
                dve.wait_ge(K_ps, q + 1)
                for gi in range(2):
                    bank = PS[3 + 2 * (q % 2) + gi][0:GH, :]
                    g = 2 * q + gi
                    dve.tensor_copy(Kfull[:, g, P:KW], bank[:, GH:P])
                    link(dve.tensor_copy(Kfull[:, g, 0:P], bank[:, P:2 * P]))
                    ins = tt(Kfull[:, g, P - GH:P], Kfull[:, g, P - GH:P], bank[:, 0:GH], ALU.add)
                ins.then_inc(K_out, 1)
            dve.wait_ge(K_out, 8)
            dve.wait_ge(ident_in, 32)
            skip = tmpA[0:GH, 0:NG * GH].rearrange("p (g h) -> p g h", h=GH)
            link(tt(skip, ident[0:GH, 0:GH].unsqueeze(1).to_broadcast([GH, NG, GH]),
                    pk("d_skip")[0:GH, :].unsqueeze(2).to_broadcast([GH, NG, GH]), ALU.mult))
            tt(Kfull[:, :, P - GH:P], Kfull[:, :, P - GH:P], skip, ALU.add).then_inc(K_done, 1)
            for i in range(2):
                dve.wait_ge(drvT_stored[i], 16 * 4)
            dve.wait_ge(tab2_stored, 16)
            scale_x(1)
            modulate_xT(1)
            scale_x(2)
            for b in range(1, NBLK):
                if b >= 1:
                    tok = slice((b - 1) * BLK, b * BLK)
                    if b == 1:
                        dve.wait_ge(mats_stored, 16 * 12)
                        dve.wait_ge(tab_stored, 16)
                    for h in range(2):
                        n = 2 * (b - 1) + h
                        dve.wait_ge(cc_ps, n + 1)
                        dve.wait_ge(cx_out, n + 1)
                        tt(mixT[:, 2 + h, tok], PS[3][:, 0:BLK], xtmp, ALU.mult).then_inc(cc_out, 1)
                    if b + 1 < NBLK:
                        modulate_xT(b + 1)
                    take_turns(b - 1)
                head_norm(b, 0)
                if b + 2 < NBLK:
                    scale_x(b + 2)
                head_norm(b, 1)
            take_turns(NBLK - 1)

            def rotate(u, part):
                x = [rot[:, i] for i in range(6)]
                c, s_ = ust[:, u % 2, 256:256 + NCHUNK], ust[:, u % 2, 256 + NCHUNK:]
                if part == 0:
                    dve.wait_ge(xr_out, 2 * u + 2)
                    dve.wait_ge(phase_in[u % 2], 16 * (u // 2 + 1))
                    tt(x[2], c, x[0], ALU.mult)
                    link(tt(x[3], s_, x[1], ALU.mult))
                    link(tt(x[4], x[2], x[3], ALU.add))
                else:
                    tt(x[5], c, x[1], ALU.mult)
                    link(tt(x[3], s_, x[0], ALU.mult))
                    tt(x[5], x[5], x[3], ALU.subtract).then_inc(rotated, 1)
                    dve.wait_ge(rotated, u + 1)

            def scan(u):
                x = [rot[:, i] for i in range(6)]
                decay = r8[:, u:u + 1].to_broadcast([P, NCHUNK])
                dve.tensor_tensor_scan(x[2], decay, x[4], 0.0, ALU.mult, ALU.add)
                link(dve.tensor_tensor_scan(x[3], decay, x[5], 0.0, ALU.mult, ALU.add))

            def unrotate(u, part):
                x = [rot[:, i, CCTX - 1:NCHUNK - 1] for i in range(6)]
                c, s_ = (ust[:, u % 2, 256 + i * NCHUNK + CCTX - 1:256 + (i + 1) * NCHUNK - 1] for i in range(2))
                if u == 6:
                    dve.wait_ge(conv_done, 8)
                if u == 7:
                    dve.wait_ge(m2_ps, 8)
                st = [S[:, u, ri] if u < UP else S[:, u, ri][:, ::-1] for ri in range(2)]
                if part == 0:
                    tt(x[4], c, x[2], ALU.mult)
                    link(tt(x[5], s_, x[3], ALU.mult))
                    link(tt(st[0], x[4], x[5], ALU.subtract))
                else:
                    tt(x[4], c, x[3], ALU.mult)
                    link(tt(x[5], s_, x[2], ALU.mult))
                    tt(st[1], x[4], x[5], ALU.add).then_inc(unit_done, 1)
                    dve.wait_ge(unit_done, u + 1)

            def denominators(g):
                dve.wait_ge(es_done, g + 1)
                if g >= 2:
                    dve.wait_ge(P_done, g - 1)
                link(tt(rden[:, g % 2], rs[:, g % 2], esink[:, g % 2], ALU.add))
                dve.reciprocal(rden[:, g % 2], rden[:, g % 2]).then_inc(rden_done, 1)

            def maximum(g, j):
                H, half = QPK * g + j, n_keys(g) // 2
                dve.wait_ge(s_ps, H + 1)
                src = banks[:, 2 * (H % 2):2 * (H % 2) + 2, 0:half]
                if g >= 2:
                    dve.wait_ge(es_done, g - 1)
                link(dve.tensor_reduce(mx[:, g % 2, j:j + 1], src, AX.XY, ALU.max))
                head = QPK * (g % 2) + j
                dve.tensor_scalar(negm[:, g % 2, j:j + 1], mx[:, g % 2, j:j + 1], -SCALE,
                                  nsink[:, head:head + 1], ALU.mult, ALU.min).then_inc(negm_done, 1)
                if j == QPK - 1:
                    dve.wait_ge(negm_done, QPK * (g + 1))
                    tt(esink[:, g % 2], pk("sink", QPK * (g % 2), QPK), negm[:, g % 2], ALU.add).then_inc(es_in, 1)

            for g in range(NGRP + 1):
                for step, n in turn_steps(g):
                    if step == "head":
                        maximum(g, n)
                    if step == "sums":
                        denominators(g)
                    J = pt_before(g - 1) + n if step == "tile" else 1
                    if J % 2 == 0:
                        dve.wait_ge(pt_ps, J + 1)
                        if J >= 2:
                            dve.wait_ge(pv_ps, J - 1)
                        dve.tensor_copy(PT[:, 0], PS[4]).then_inc(pt_dve, 1)
                        part = J // 2 - even_before(g - 1)
                        if g >= 2 and part < 2:
                            (rotate if g % 2 == 0 else unrotate)(g // 2 - 1, part)
                if g >= 1:
                    if g % 2 == 0:
                        i = g // 2 - 1
                        dve.wait_ge(pv_ps, pt_before(g))
                        dve.tensor_copy(mixT[:, 4:8, i * P:(i + 1) * P],
                                        PS[6].rearrange("p (j q) -> p j q", q=P)).then_inc(o_out, 1)
                if g >= 2 and g % 2 == 0:
                    scan(g // 2 - 1)
                if g % 2 == 0 and g // 2 < 8:
                    i = g // 2
                    dve.wait_ge(m2_ps, i + 1)
                    dve.wait_ge(mats_in, 64)
                    if i < 4:
                        dst = (g1bc if i < 2 else g2bc)[:, (i % 2) * 512:(i % 2 + 1) * 512]
                        tt(dst, PS[7], dst, ALU.add).then_inc(m2_out, 1)
                    else:
                        dve.wait_ge(conv_done, 8)
                        dve.wait_ge(mcol_ps, i - 3)
                        dve.tensor_copy(mrow, PS[7][0:2, :]).then_inc(mrow_out, 1)
                if g % 2 == 1 and 4 <= g // 2 < 8:
                    i = g // 2
                    dve.wait_ge(mcol_ps, i - 2)
                    src = PS[7][:, 0:8].rearrange("p (c j) -> p c j", j=2)[:, :, 0]
                    tt(mod2[:, 4 * (i - 4):4 * (i - 3)], src, pk("b_mod", 4 * MOD2[i], 4), ALU.add).then_inc(mod_done, 1)
            unrotate(NU - 1, 0)
            unrotate(NU - 1, 1)
            dve.wait_ge(conv_done, 8)
            for z in range(8):
                ct, half, tq = z // 4, (z // 2) % 2, z % 2
                dve.wait_ge(yt_ps, z + 1)
                dst = mixT[:, 2 + half, ct * 1024:(ct + 1) * 1024].rearrange("p (c t) -> p t c", t=CH)
                dve.tensor_copy(dst[:, 4 * tq:4 * tq + 4], PS[z].rearrange("p (t c) -> p t c", c=P)).then_inc(yt_out, 1)
            for w in range(8):
                tb, half = w // 2, w % 2
                dve.wait_ge(z_out, w + 1)
                link(dve.tensor_scalar(th[:, half], th[:, half], 0.5, 0.5, ALU.mult, ALU.add))
                dve.wait_ge(z_ps, 2 * tb + 2)
                v = mixT[:, 2 + half, tb * 512:(tb + 1) * 512]
                tt(v, v, th[:, half], ALU.mult).then_inc(glu_done, 1)
            link(dve.tensor_scalar(scale2[:, :], mod2[:, KD:2 * KD], 1.0, None, ALU.add))
            tt(scale2[:, :], scale2[:, :], pk("norm2"), ALU.mult).then_inc(mod2_done, 1)

            def add_mix(pp):
                if pp >= 1:
                    dve.wait_ge(h_stored, 16 * pp)
                for r in range(4):
                    t, half = r // 2, slice((r % 2) * 512, (r % 2 + 1) * 512)
                    dve.wait_ge(o2_ps, 4 * pp + r + 1)
                    tt(hm[:, t, half], PS[r], g1bc[:, half], ALU.mult).then_inc(o2_out, 1)
                dve.wait_ge(o2_out, 4 * (pp + 1))
                dve.wait_ge(xo_in[pp % 2], 16 * (pp // 2 + 1))
                tt(hm, hm, xo[:, pp % 2], ALU.add).then_inc(hm_done, 1)
                dve.wait_ge(std2_done, pp + 1)
                link(dve.reciprocal(rstd[:, :], ss[:, pp % 2]))
                for t in range(TPB):
                    ins = dve.tensor_scalar(xo[:, pp % 2, t], hm[:, t], rstd[:, t:t + 1], None, ALU.mult)
                ins.then_inc(x2_scaled, 1)
                dve.wait_ge(x2_scaled, pp + 1)

            for pp in range(NPP):
                add_mix(pp)
            biased, above, equal, rank, sel, gates, where, pick, pick2 = rt
            one = "p t r -> p (t r)"
            dve.wait_ge(sig_done, 1)
            dve.wait_ge(o2_ps, 4 * NPP)
            dve.wait_ge(x2_stored, 16 * NPP)
            link(tt(biased, lgt, pk("r_bias").unsqueeze(1).to_broadcast([P, NTILE, NR]), ALU.add))
            for t in range(NTILE):
                last = dve.max(top8[:, t], biased[:, t])
            link(last)
            fourth = top8[:, :, TOPK - 1:TOPK].to_broadcast([P, NTILE, NR])
            tt(above, biased, fourth, ALU.is_gt)
            link(tt(equal, biased, fourth, ALU.is_equal))
            link(dve.tensor_reduce(rsm[:, 0], above, AX.X, ALU.add))
            link(dve.tensor_scalar(rsm[:, 1], rsm[:, 0], -1.0, float(TOPK), ALU.mult, ALU.add))
            dve.wait_ge(cst_in, 48)
            link(dve.tensor_tensor_scan(rank.rearrange(one), restart, equal.rearrange(one), 0.0, ALU.mult, ALU.add))
            link(tt(rank, rank, rsm[:, 1].unsqueeze(2).to_broadcast([P, NTILE, NR]), ALU.is_le))
            link(tt(sel, equal, rank, ALU.mult))
            link(tt(sel, sel, above, ALU.add))
            dve.tensor_copy(selb, sel.rearrange(one)).then_inc(sel_done, 1)
            link(tt(gates, sel, lgt, ALU.mult))
            link(dve.tensor_reduce(rsm[:, 2], gates, AX.X, ALU.add))
            link(dve.reciprocal(rsm[:, 3], rsm[:, 2]))
            link(tt(gates, gates, rsm[:, 3].unsqueeze(2).to_broadcast([P, NTILE, NR]), ALU.mult))
            link(dve.tensor_scalar(gates, gates, ROUTED, None, ALU.mult))
            link(dve.tensor_tensor_scan(rank.rearrange(one), restart, sel.rearrange(one), 0.0, ALU.mult, ALU.add))
            link(tt(rank, rank, sel, ALU.mult))

            def whole(o, x):
                link(dve.tensor_scalar(o, x, ROUND, None, ALU.add))
                link(dve.tensor_scalar(o, o, ROUND, None, ALU.subtract))

            count, tiles, upto, start = (counts[:, i] for i in range(4))
            dve.wait_ge(pos_ps, 1)
            dve.wait_ge(cst_in, 48)
            link(dve.tensor_scalar(count, PS[5][:, 0:NR], 1.0 / P, (P - 1) / (2.0 * P), ALU.mult, ALU.add))
            whole(tiles, count)
            link(dve.tensor_tensor_scan(upto, ones, tiles, 0.0, ALU.mult, ALU.add))
            link(tt(start, upto, tiles, ALU.subtract))
            link(dve.tensor_scalar(start, start, float(P), None, ALU.mult))
            link(tt(where, PS[4].rearrange("p (t r) -> p t r", r=NR), start.unsqueeze(1).to_broadcast([P, NTILE, NR]),
                    ALU.add))
            for k in range(TOPK):
                dve.scalar_tensor_tensor(out=pick, in0=rank, scalar=k + 1.0, in1=where, op0=ALU.is_equal, op1=ALU.mult)
                link(dve.scalar_tensor_tensor(out=pick2, in0=rank, scalar=k + 1.0, in1=gates, op0=ALU.is_equal,
                                              op1=ALU.mult))
                dve.tensor_reduce(slot_f[:, :, k], pick, AX.X, ALU.add)
                link(dve.tensor_reduce(gate_k[:, :, k], pick2, AX.X, ALU.add))
            link(dve.tensor_scalar(slot_p, slot_f, 1.0 / P, -(P - 1) / (2.0 * P), ALU.mult, ALU.add))
            whole(slot_t, slot_p)
            link(dve.scalar_tensor_tensor(out=slot_p, in0=slot_t, scalar=-float(P), in1=slot_f, op0=ALU.mult,
                                          op1=ALU.add))
            dve.tensor_copy(slot_idx, slot_f)
            oh = oh_t.rearrange("p (t c n) -> p t c n", c=2, n=NT)
            for k in range(TOPK):
                if k >= 1:
                    dve.wait_ge(tok_ps, k)
                tt(oh_p.rearrange("p (t m) -> p t m", m=P), iota_p.unsqueeze(1).to_broadcast([P, NTILE, P]),
                   slot_p[:, :, k:k + 1].to_broadcast([P, NTILE, P]), ALU.is_equal)
                link(tt(oh[:, :, 1], iota_t.unsqueeze(1).to_broadcast([P, NTILE, NT]),
                        slot_t[:, :, k:k + 1].to_broadcast([P, NTILE, NT]), ALU.is_equal))
                link(tt(oh[:, :, 0], oh[:, :, 1], tile_no.unsqueeze(2).to_broadcast([P, NTILE, NT]), ALU.mult))
                dve.tensor_scalar(oh[:, :, 1], oh[:, :, 1], row_no, None, ALU.mult).then_inc(oh_t_done, 1)
                if k == 0:
                    link(tt(reached, iota_t.unsqueeze(2).to_broadcast([P, NT, NR]),
                            upto.unsqueeze(1).to_broadcast([P, NT, NR]), ALU.is_ge))
                    tile_e = pick.rearrange(one)[:, 0:NT]
                    dve.tensor_reduce(tile_e, reached, AX.X, ALU.add).then_inc(reached_done, 1)
                    dve.wait_ge(reached_done, 1)
                    link(dve.tensor_scalar(tile_e, tile_e, NR - 1.0, float(P), ALU.min, ALU.mult))
                    link(dve.tensor_scalar(tile_e, tile_e, row_no, None, ALU.add))
                    dve.tensor_copy(w_idx, tile_e).then_inc(reached_done, 1)
            dve.wait_ge(tok_ps, TOPK)
            tok_f = pick2.rearrange(one)[:, 0:2 * NT]
            link(dve.tensor_copy(tok_f, PS[6][:, 0:2 * NT]))
            link(dve.scalar_tensor_tensor(out=tok_f[:, 0:NT], in0=tok_f[:, 0:NT], scalar=float(P), in1=tok_f[:, NT:2 * NT],
                                          op0=ALU.mult, op1=ALU.add))
            dve.tensor_copy(tok_idx, tok_f[:, 0:NT]).then_inc(idx_done, 1)

            def turned(it, s):
                dve.wait_ge(xt_ps, it * (2 * STEPS) + 2 * (s + 1))
                if not (first(it) and s < 2):
                    dve.wait_ge(hu_ps, it * STEPS + (s - 1))
                for k in range(4):
                    ins = dve.tensor_scalar(xT[:, s % 2, 4 + k], PS[1][:, k * P:(k + 1) * P], scale2[:, 4 + k:5 + k],
                                            mod2[:, 4 + k:5 + k], ALU.mult, ALU.add)
                ins.then_inc(xt_dve, 1)

            def send(it, s):
                if not (first(it) and s < 3):
                    dve.wait_ge(yo_stored[s % 3], it * 32 + 16 * (s // 3))
                for h in range(2):
                    half = slice(h * 512, (h + 1) * 512)
                    dve.wait_ge(yd_ps, it * (2 * STEPS) + (2 * s + h + 1))
                    tt(yo[:, s % 3, half], PS[2 + h], g2bc[:, half], ALU.mult).then_inc(yo_done, 1)

            def product(it, s):
                dve.wait_ge(sl_out, it * STEPS + (s + 1))
                dve.wait_ge(hu_ps, it * STEPS + (s + 1))
                if not (first(it) and s < 2):
                    dve.wait_ge(yd_ps, it * (2 * STEPS) + 2 * (s - 1))
                tt(hx[:, s % 2], slx[:, s % 2], PS[6 + s % 2][:, 0:P], ALU.mult).then_inc(h_done, 1)

            def experts_step(it, s):
                turned(it, s)
                if not (first(it) and s < 2):
                    send(it, s - 2)
                if not (first(it) and s < 1):
                    product(it, s - 1)

            def add_base(it):
                base = y[:, bass.ds(it, 1), :]
                tt(base, base, g2bc.unsqueeze(1), ALU.mult).then_inc(base_mul, 1)
                dve.wait_ge(base_mul, it + 1)
                dve.wait_ge(hb_in, it * 16 + 16)
                tt(base, base, hb.unsqueeze(1), ALU.add).then_inc(base_done, 1)

            def experts_turn(it):
                for s in range(tiles_in(it)):
                    experts_step(it, s)
                    if s == 3:
                        add_base(it)

            dve.wait_ge(ysh_out, 2 * NTILE)
            experts_turn(0)
            with dve.Fori(1, TURNS - 1) as it:
                experts_turn(it)
            experts_turn(TURNS - 1)
            send(TURNS - 1, LAST - 2)
            product(TURNS - 1, LAST - 1)
            send(TURNS - 1, LAST - 1)

            dve.wait_ge(base_done, NTILE)
            with dve.Fori(0, NTILE // SETS) as it:
                for j in range(SETS):
                    t = it * SETS + j
                    dve.wait_ge(gb_in[j], it * (16 * TOPK) + 16 * TOPK)
                    for k in range(TOPK):
                        dve.scalar_tensor_tensor(out=y[:, bass.ds(t, 1), :], in0=gb[:, TOPK * j + k].unsqueeze(1),
                                                 scalar=gate_k[:, bass.ds(t, 1), k], in1=y[:, bass.ds(t, 1), :],
                                                 op0=ALU.mult, op1=ALU.add).then_inc(sum_step, 1)
                        dve.wait_ge(sum_step, t * TOPK + (k + 1))

        @block.tensor
        def _(pe):
            pe.wait_ge(silu_done, 1)
            for n in range(4):
                pe.wait_ge(wmod_in[n % 2], 16 * (n // 2 + 1))
                if n >= 2:
                    pe.wait_ge(mrow_out, n - 1)
                for k in range(KD):
                    mm = pe.matmul(PS[7 * (n % 2)][0:2, :], silu_c[:, k, :], wmod[:, n % 2, k], start=(k == 0),
                                   stop=(k == KD - 1))
                mm.then_inc(wmod_used, 1)
            pe.wait_ge(ident_in, 32)
            for n in range(4):
                pe.wait_ge(mrow_out, 4)
                for cb in range(4):
                    col = 2 * (4 * n + cb)
                    mm = pe.transpose(PS[0][:, col:col + 2], mrows[:, n, cb * P:(cb + 1) * P], ident[0:2, 0:2])
            mm.then_inc(mcol_ps, 1)
            pe.wait_ge(ident_in, 32)
            pe.wait_ge(drv_done, 2)
            for q in range(8):
                if q >= 2:
                    pe.wait_ge(drvT_out, q - 1)
                for i in range(4):
                    ri, u = (4 * q + i) // NU, (4 * q + i) % NU
                    mm = pe.transpose(PS[1 + q % 2][:, i * P:(i + 1) * P], drv[:, ri, u], ident[:, :])
                mm.then_inc(drvT_ps, 1)
            def turn_x(b):
                pe.wait_ge(x_scaled, b + 1)
                if b == 0:
                    pe.wait_ge(mod_done, 1)
                    pe.wait_ge(drvT_out, 8)
                for q in range(4):
                    job = 4 * b + q
                    if job >= 2:
                        pe.wait_ge(xn_out, job - 1)
                    for i in range(2):
                        k = 2 * q + i
                        for t in range(TPB):
                            mm = pe.transpose(PS[q % 2][:, i * BLK + t * P:i * BLK + (t + 1) * P],
                                              xs[:, b % 2, t, k * P:(k + 1) * P], ident[:, :])
                    mm.then_inc(xn_ps, 1)

            def columns(bank, b, col):
                for k in range(KD):
                    mm = pe.matmul(bank, w_in[:, k, col:col + P], xnT[:, b % 2, k], start=(k == 0), stop=(k == KD - 1))
                return mm

            def turn(b):
                base = turns_before(b)
                pe.wait_ge(u_out, b + 1)
                if b == 0:
                    pe.wait_ge(K_out, 8)
                pe.wait_ge(k_out, TPB * (b + 1))
                pe.wait_ge(v_out, TPB * (b + 1))
                i = 0

                def bank():
                    if base + i >= 2:
                        pe.wait_ge(turn_out, base + i - 1)
                    return PS[7 - i % 2]

                for i in range(4):
                    o = bank()
                    for sl_ in range(2):
                        for h in range(2):
                            s = 2 * i + sl_
                            col = (2 * sl_ + h) * P
                            mm = pe.transpose(o[0:CB, col:col + P], uT[:, h, s:BLK:CH], ident[:, :])
                    mm.then_inc(turn_ps, 1)
                i = 4
                if b >= 1:
                    for t in range(TPB):
                        pe.wait_ge(qk_done, TPB * b + t + 1)
                        o = bank()
                        for j in range(QPK):
                            mm = pe.transpose(o[:, j * P:(j + 1) * P], qkr[:, t, j * P:(j + 1) * P], ident[:, :])
                        mm.then_inc(turn_ps, 1)
                        i += 1
                pe.wait_ge(qk_done, TPB * (b + 1))
                o = bank()
                for t in range(TPB):
                    mm = pe.transpose(o[:, t * P:(t + 1) * P], qkr[:, t, 512:640], ident[:, :])
                mm.then_inc(turn_ps, 1)
                i += 1
                pe.wait_ge(turn_out, base + 4)
                o = bank()
                for g in range(NG):
                    mm = pe.transpose(o[:, g * CB:(g + 1) * CB], Uc[:, g].rearrange("p s h -> p (s h)"),
                                      ident[0:CB, 0:CB])
                mm.then_inc(turn_ps, 1)

            turn_x(0)
            for b in range(NBLK):
                pe.wait_ge(xn_out, 4 * (b + 1))
                if b >= 1:
                    if b == 1:
                        pe.wait_ge(w_in_in[2], 16)
                        pe.wait_ge(K_out, 8)
                    for h in range(2):
                        n = 2 * (b - 1) + h
                        if n >= 1:
                            pe.wait_ge(cx_out, n)
                        columns(PS[2][:, 0:BLK], b, h * P).then_inc(cx_ps, 1)
                        if n >= 1:
                            pe.wait_ge(cc_out, n)
                        columns(PS[3][:, 0:BLK], b, COL_C + h * P).then_inc(cc_ps, 1)
                        if n >= 1:
                            pe.wait_ge(cb_out, n)
                        if h == 0:
                            pe.wait_ge(u_out, b)
                        columns(PS[4][:, 0:BLK], b, COL_B + h * P).then_inc(cb_ps, 1)
                    if b + 1 < NBLK:
                        turn_x(b + 1)
                    turn(b - 1)
                if b == 0:
                    pe.wait_ge(w_in_in[0], 16)
                else:
                    pe.wait_ge(cb_out, 2 * b)
                for h in range(2):
                    mm = columns(PS[4][:, h * BLK:(h + 1) * BLK], b, COL_U + h * P)
                mm.then_inc(u_ps, 1)
                if b == 0:
                    pe.wait_ge(w_in_in[1], 16)
                else:
                    pe.wait_ge(turn_out, turns_before(b))
                for t in range(TPB):
                    m = TPB * b + t
                    if b >= 1:
                        if m > TPB:
                            pe.wait_ge(q_sq, m - TPB)
                            pe.wait_ge(q_out, m - TPB)
                        for k in range(KD):
                            mm = pe.matmul(PS[5][:, :], xnT[:, b % 2, k, t * P:(t + 1) * P],
                                           w_in[:, k, COL_Q:COL_Q + 512], start=(k == 0), stop=(k == KD - 1))
                        mm.then_inc(q_ps, 1)
                    if m >= 1:
                        pe.wait_ge(k_out, m)
                        pe.wait_ge(v_out, m)
                    for k in range(KD):
                        mm = pe.matmul(PS[6][:, 0:2 * P], xnT[:, b % 2, k, t * P:(t + 1) * P],
                                       w_in[:, k, COL_K:N_IN], start=(k == 0), stop=(k == KD - 1))
                    mm.then_inc(kv_ps, 1)
                if b == 0:
                    pe.wait_ge(mats_done, 2)
                    pe.wait_ge(u_out, 1)
                    pe.wait_ge(v_out, TPB)
                    for q in range(8):
                        if q >= 2:
                            pe.wait_ge(K_out, q - 1)
                        for gi in range(2):
                            rows = slice(NS * gi, NS * gi + NS)
                            for d in range(2):
                                u = d * UP + q
                                cols = slice(d * P, (d + 1) * P)
                                lo = 0 if d == 0 else GH
                                for ri in range(2):
                                    mm = pe.matmul(PS[3 + 2 * (q % 2) + gi][0:GH, cols], bbar[rows, ri, u], cA[rows, ri, u, lo:lo + P],
                                                   start=(ri == 0), stop=(ri == 1))
                        mm.then_inc(K_ps, 1)
                    turn_x(1)
            turn(NBLK - 1)

            pe.wait_ge(xn_out, 4 * NBLK)
            pe.wait_ge(cx_out, 16)
            pe.wait_ge(cc_out, 16)
            pe.wait_ge(u_out, NBLK)
            pe.wait_ge(q_sq, NTILE)
            pe.wait_ge(v_out, TPB * NBLK)
            pe.wait_ge(turn_out, turns_before(NBLK))
            pe.wait_ge(consts_b, 1)

            def scores(g, head):
                i, kv = g // 2, g % 2
                rows = slice(HD * kv, HD * (kv + 1))
                w = window(i)
                W, half = len(w) * P, n_keys(g) // 2
                k0 = CTX + w[0] * P
                lo = min(W, half)
                masks = []
                if i > 0:
                    masks.append((0, 0, P, 0))
                if i < NTILE - 1:
                    at = (len(w) - 1) * P
                    m = max(0, min(P, half - at))
                    if m:
                        masks.append((0, at, m, P))
                    if m < P:
                        masks.append((1, at + m - half, P - m, P + m))
                H = QPK * g + head
                if H >= 2:
                    pe.wait_ge(exp_done, H - 1)
                b = [PS[2 * (H % 2)], PS[2 * (H % 2) + 1]]
                q = mixT[rows, 4 + head, i * P:(i + 1) * P]
                mm = pe.matmul(b[1][:, W - half:W - half + CTX], q, kT[rows, 0:CTX], start=True, stop=True)
                if W > half:
                    mm = pe.matmul(b[1][:, 0:W - half], q, kT[rows, k0 + half:k0 + W], start=True, stop=False)
                in1 = [m for m in masks if m[0] == 1]
                for n, (_, at, m, mc) in enumerate(in1):
                    mm = pe.matmul(b[1][:, at:at + m], identb[:, :], maskb[:, mc:mc + m], start=False,
                                   stop=(n == len(in1) - 1))
                in0 = [m for m in masks if m[0] == 0]
                mm = pe.matmul(b[0][:, 0:lo], q, kT[rows, k0:k0 + lo], start=True, stop=not in0)
                for n, (_, at, m, mc) in enumerate(in0):
                    mm = pe.matmul(b[0][:, at:at + m], identb[:, :], maskb[:, mc:mc + m], start=False,
                                   stop=(n == len(in0) - 1))
                mm.then_inc(s_ps, 1)

            def turn_p(g, n):
                J = pt_before(g) + n
                at = key_tiles(g)[n][0]
                pe.wait_ge(P_done, g + 1)
                if J >= 2:
                    pe.wait_ge(pt_act if J % 2 else pt_dve, J // 2)
                for j in range(QPK):
                    mm = pe.transpose(PS[4 + J % 2][:, j * P:(j + 1) * P], Pb[:, (g % 2) * QPK + j, at:at + P], ident[:, :])
                mm.then_inc(pt_ps, 1)

            def times_v(g, n):
                J, kv, last = pt_before(g) + n, g % 2, len(key_tiles(g)) - 1
                if n == 0 and kv == 0 and g >= 2:
                    pe.wait_ge(o_out, g // 2)
                pe.wait_ge(pt_act if J % 2 else pt_dve, J // 2 + 1)
                pe.matmul(PS[6][HD * kv:HD * (kv + 1), :], V[:, key_tiles(g)[n][1], HD * kv:HD * (kv + 1)], PT[:, J % 2],
                          start=(n == 0), stop=(n == last)).then_inc(pv_ps, 1)

            def drive(u, ri):
                pe.wait_ge(drv_in[u % 2], 16 * (u // 2 + 1))
                if u + ri >= 1:
                    pe.wait_ge(xr_out, 2 * u + ri)
                if u == 0:
                    pe.wait_ge(U_in, 16)
                if ri == 1 and u < 4:
                    pe.wait_ge(m2_out, u + 1)
                if ri == 1 and 4 <= u < 8:
                    pe.wait_ge(mrow_out, 4 + u - 3)
                if ri == 0 and 5 <= u < 9:
                    pe.wait_ge(mod_done, 1 + u - 4)
                for gi in range(2):
                    mm = pe.matmul(PS[7][NS * gi:NS * (gi + 1), 0:NCHUNK],
                                   ust[:, u % 2, ri * P + NS * gi:ri * P + NS * (gi + 1)], U[:, 2 * (u % UP) + gi, :],
                                   start=True, stop=True)
                mm.then_inc(xr_ps, 1)

            def modulation(i):
                pe.wait_ge(wm2_in, 16 * (i + 1))
                pe.wait_ge(xr_out, 2 * i + 1)
                for k in range(KD):
                    if i < 4:
                        mm = pe.matmul(PS[7], silu_c[:, k, 0:1].to_broadcast([P, P]), wm2[:, k], start=(k == 0),
                                       stop=(k == KD - 1))
                    else:
                        mm = pe.matmul(PS[7][0:2, :], silu_c[:, k, :], wm2[:, k], start=(k == 0), stop=(k == KD - 1))
                mm.then_inc(m2_ps, 1)

            def modulation_columns(i):
                pe.wait_ge(mrow_out, 4 + i - 3)
                pe.wait_ge(xr_out, 2 * i + 2)
                for cb in range(4):
                    mm = pe.transpose(PS[7][:, 2 * cb:2 * cb + 2], mrow[:, cb * P:(cb + 1) * P], ident[0:2, 0:2])
                mm.then_inc(mcol_ps, 1)

            for g in range(NGRP + 1):
                for step, n in turn_steps(g):
                    if step == "head":
                        scores(g, n)
                    if step == "drive":
                        drive(g // 2, g % 2)
                    if step == "tile":
                        turn_p(g - 1, n)
                        if n >= 1:
                            times_v(g - 1, n - 1)
                if g >= 1:
                    times_v(g - 1, len(key_tiles(g - 1)) - 1)
                if g % 2 == 0 and g // 2 < 8:
                    modulation(g // 2)
                if g % 2 == 1 and 4 <= g // 2 < 8:
                    modulation_columns(g // 2)

            pe.wait_ge(mats_in, 64)
            pe.wait_ge(unit_done, NU)
            pe.wait_ge(exp_done, QPK * NGRP)
            pe.wait_ge(pt_dve, even_before(NGRP))
            pe.wait_ge(pt_act, odd_before(NGRP))
            pe.wait_ge(o_out, NTILE)
            pe.wait_ge(xr_out, 2 * NU)
            for r in range(8):
                ct, a8, par = r // 4, (r // 2) % 2, r % 2
                rows = slice(NS * par, NS * (par + 1))
                for sl_ in range(4):
                    g = 8 * a8 + 2 * sl_ + par
                    o = PS[r][:, sl_ * P:(sl_ + 1) * P]
                    pe.matmul(o, U[:, g, CCTX + ct * P:CCTX + (ct + 1) * P], M[:, g], start=True, stop=False)
                    for d in range(2):
                        for ri in range(2):
                            u = d * UP + g // 2
                            mm = pe.matmul(o, S[rows, u, ri, ct * P:(ct + 1) * P], R[rows, u, ri], start=False,
                                           stop=(d == 1 and ri == 1))
                mm.then_inc(y_ps, 1)
            for z in range(8):
                ct, half, tq = z // 4, (z // 2) % 2, z % 2
                pe.wait_ge(y_out, 4 * (ct + 1))
                for t in range(4):
                    mm = pe.transpose(PS[z][:, t * P:(t + 1) * P], Yc[:, ct, 4 * tq + t, half * P:(half + 1) * P], ident[:, :])
                mm.then_inc(yt_ps, 1)
            pe.wait_ge(wglu_in, 16)
            for w in range(8):
                tb, half = w // 2, w % 2
                pe.wait_ge(yt_out, 4 if tb < 2 else 8)
                for k in range(2):
                    mm = pe.matmul(PS[w], w_glu[:, k, half * P:(half + 1) * P], mixT[:, 2 + k, tb * 512:(tb + 1) * 512],
                                   start=(k == 0), stop=(k == 1))
                mm.then_inc(z_ps, 1)

            def project_out(pp, r):
                t, half = r // 2, slice((r % 2) * 512, (r % 2 + 1) * 512)
                if pp >= 1:
                    pe.wait_ge(o2_out, 4 * (pp - 1) + r + 1)
                for k in range(KD):
                    mm = pe.matmul(PS[r], mixT[:, k, (TPB * pp + t) * P:(TPB * pp + t + 1) * P], w_out[:, k, half],
                                   start=(k == 0), stop=(k == KD - 1))
                mm.then_inc(o2_ps, 1)

            def turn_x2(pp, q):
                pe.wait_ge(x2_scaled, pp + 1)
                job = 4 * pp + q
                if job >= 2:
                    pe.wait_ge(t2_out, job - 1)
                for i in range(2):
                    k = 2 * q + i
                    for t in range(TPB):
                        mm = pe.transpose(PS[4 + q % 2][:, i * BLK + t * P:i * BLK + (t + 1) * P],
                                          xo[:, pp % 2, t, k * P:(k + 1) * P], ident[:, :])
                mm.then_inc(t2_ps, 1)

            def route(pp):
                pe.wait_ge(t2_out, 4 * (pp + 1))
                if pp >= 2:
                    pe.wait_ge(lg_out, pp - 1)
                for t in range(TPB):
                    for k in range(KD):
                        mm = pe.matmul(PS[6 + pp % 2][:, t * NR:(t + 1) * NR],
                                       tT[:, k, (TPB * pp + t) * P:(TPB * pp + t + 1) * P], r_w[:, k, :],
                                       start=(k == 0), stop=(k == KD - 1))
                mm.then_inc(lg_ps, 1)

            pe.wait_ge(z_out, 8)
            pe.wait_ge(glu_done, 8)
            pe.wait_ge(w_out_in, 32)
            for r in range(4):
                project_out(0, r)
            for pp in range(NPP):
                for q in range(4):
                    if pp + 1 < NPP:
                        project_out(pp + 1, q)
                    if q == 0 and pp >= 1:
                        route(pp - 1)
                    if q >= 1:
                        turn_x2(pp, q - 1)
                turn_x2(pp, 3)
            route(NPP - 1)

            def shared_in(tb):
                for m, ps in enumerate((shg_ps, shu_ps)):
                    if tb >= 2:
                        pe.wait_ge(sh_act, tb - 1)
                    for k in range(KD):
                        mm = pe.matmul(PS[2 * m + tb % 2], wsh[:, m, k * EF:(k + 1) * EF], tT[:, k, tb * TW:(tb + 1) * TW],
                                       start=(k == 0), stop=(k == KD - 1))
                    mm.then_inc(ps, 1)

            def shared_down(tb):
                pe.wait_ge(prod_done, tb + 1)
                for r in range(8):
                    d = 8 * tb + r
                    t, half = r // 2, slice((r % 2) * 512, (r % 2 + 1) * 512)
                    if d >= 4:
                        pe.wait_ge(ysh_out, d - 3)
                    pe.matmul(PS[d % 4], hsh[:, tb, t * P:(t + 1) * P], wsh[:, 2, half], start=True, stop=True)\
                        .then_inc(shy_ps, 1)

            def tokens(k):
                pe.wait_ge(oh_t_done, k + 1)
                for t in range(NTILE):
                    mm = pe.matmul(PS[6][:, 0:2 * NT], oh_p[:, t * P:(t + 1) * P], oh_t[:, t * 2 * NT:(t + 1) * 2 * NT],
                                   start=(k == 0 and t == 0), stop=(k == TOPK - 1 and t == NTILE - 1))
                mm.then_inc(tok_ps, 1)

            pe.wait_ge(wsh_in, 16)
            pe.wait_ge(o2_out, 4 * NPP)
            pe.wait_ge(t2_out, 4 * NPP)
            pe.wait_ge(lg_out, NPP)
            shared_in(0)
            shared_in(1)
            pe.wait_ge(sel_done, 1)
            pe.wait_ge(consts_b, 2)
            pe.matmul(PS[4], earlier, selb, start=True, stop=False)
            for j in range(1, NTILE):
                pe.matmul(PS[4][:, j * NR:NTILE * NR], ones_b, selb[:, 0:(NTILE - j) * NR], start=False,
                          stop=(j == NTILE - 1))
            for t in range(NTILE):
                mm = pe.matmul(PS[5][:, 0:NR], ones_b, selb[:, t * NR:(t + 1) * NR], start=(t == 0), stop=(t == NTILE - 1))
            mm.then_inc(pos_ps, 1)
            shared_in(2)
            shared_in(3)
            pe.wait_ge(sh_act, TB)
            for i in range(TB):
                tokens(i)
                shared_down(i)

            def turn_rows(it, s):
                n = it * STEPS + s
                pe.wait_ge(xg_in[s % 3], it * 32 + 16 * (s // 3 + 1))
                for h, used in enumerate((xt_act, xt_dve)):
                    if not (first(it) and s < 1):
                        pe.wait_ge(used, it * STEPS + s)
                    for i in range(4):
                        mm = pe.transpose(PS[h][:, i * P:(i + 1) * P], xg[:, s % 3, (4 * h + i) * P:(4 * h + i + 1) * P],
                                          ident[:, :])
                    mm.then_inc(xt_ps, 1)

            def down(it, s):
                pe.wait_ge(h_done, it * STEPS + (s + 1))
                for h in range(2):
                    if not (first(it) and s < 1):
                        pe.wait_ge(yo_done, it * (2 * STEPS) + (2 * s + h - 1))
                    pe.matmul(PS[2 + h], hx[:, s % 2], wx[s % 3][:, 2, h * 512:(h + 1) * 512], start=True, stop=True)\
                        .then_inc(yd_ps, 1)

            def gate_and_up(it, s):
                pe.wait_ge(xt_act, it * STEPS + (s + 1))
                pe.wait_ge(xt_dve, it * STEPS + (s + 1))
                pe.wait_ge(wx_in[s % 3], it * 32 + 16 * (s // 3 + 1))
                for m, ps in enumerate((hg_ps, hu_ps)):
                    if not (first(it) and s < 2):
                        pe.wait_ge((sl_out, h_done)[m], it * STEPS + (s - 1))
                    for k in range(KD):
                        mm = pe.matmul(PS[4 + 2 * m + s % 2][:, 0:P], wx[s % 3][:, m, k * EF:(k + 1) * EF], xT[:, s % 2, k],
                                       start=(k == 0), stop=(k == KD - 1))
                    mm.then_inc(ps, 1)

            def experts_step(it, s):
                turn_rows(it, s)
                if not (first(it) and s < 2):
                    down(it, s - 2)
                if not (first(it) and s < 1):
                    gate_and_up(it, s - 1)

            pe.wait_ge(ysh_out, 2 * NTILE)
            pe.wait_ge(idx_done, 1)
            for s in range(STEPS):
                experts_step(0, s)
            with pe.Fori(1, TURNS - 1) as it:
                for s in range(STEPS):
                    experts_step(it, s)
            for s in range(LAST):
                experts_step(TURNS - 1, s)
            down(TURNS - 1, LAST - 2)
            gate_and_up(TURNS - 1, LAST - 1)
            down(TURNS - 1, LAST - 1)


def lay_out(inputs):
    import numpy as np

    f = {k: np.asarray(v) for k, v in inputs.items()}
    f = {k: (v[0] if v.ndim and v.shape[0] == 1 and k not in ("x", "c") else v) for k, v in f.items()}

    def rows(v):
        return v.reshape(-1, P).T

    def same(v):
        return np.broadcast_to(v, (P, v.shape[-1]))

    def by_state(v):
        v = v.reshape((2, UP, 2, NS) + v.shape[3:])
        return np.ascontiguousarray(np.moveaxis(v, (2, 3), (0, 1))).reshape((P, NU) + v.shape[4:])

    cc = np.stack([f["c"][0], f["c_ctx"]])
    parts = {
        "c": np.ascontiguousarray(cc.reshape(2, KD, P).transpose(2, 1, 0)).reshape(P, 2 * KD),
        "b_mod": rows(f["b_mod"]), "norm1": rows(f["norm1_g"]), "norm2": rows(f["norm2_g"]),
        "lam_re": by_state(f["ssm_lam_re"]), "lam_im": by_state(f["ssm_lam_im"]),
        "log_dt": by_state(np.broadcast_to(f["ssm_log_dt"][:, :, None], (2, NG, NS))),
        "q_g": same(f["q_norm_g"]), "k_g": same(f["k_norm_g"]), "sink": same(f["attn_sink"]),
        "b_glu": rows(f["b_glu"]),
        "conv_w": np.ascontiguousarray(f["conv_w"].reshape(3, 2, P).transpose(2, 1, 0)).reshape(P, 6),
        "r_bias": same(f["router_bias"]),
        "mults": same(np.array(MULTS, np.float32)),
        "d_skip": np.concatenate([f["ssm_d"].reshape(NG, GH).T, np.zeros((P - GH, NG), np.float32)]),
    }
    pack = np.concatenate([parts[k] for k in PACK], axis=1)
    assert pack.shape == (P, N_PACK)
    raw = np.stack([by_state(f["ssm_b_re"]), by_state(f["ssm_b_im"]),
                    by_state(f["ssm_c_re"].transpose(0, 1, 3, 2)), by_state(f["ssm_c_im"].transpose(0, 1, 3, 2))], axis=1)
    w = f["w_in"]
    wq = w[:, 1024:1536].reshape(D, NKV, QPK, HD).transpose(0, 2, 1, 3).reshape(D, 512)
    w_in = np.concatenate([w[:, 0:COL_Q], wq, w[:, 1536:N_IN]], axis=1).reshape(KD, P, N_IN).transpose(1, 0, 2)
    wo = f["w_out"]
    wo_att = wo[512:1024].reshape(NKV, QPK, HD, D).transpose(1, 0, 2, 3).reshape(512, D)
    w_out = np.concatenate([wo[0:512], wo_att]).reshape(KD, P, D).transpose(1, 0, 2)
    pairs = HD // 4
    pos = np.arange(SEQ)
    freq = (np.float32(10000.0) ** (-np.arange(pairs, dtype=np.float32) / pairs)).astype(np.float32)
    ang = np.stack([(pos // 64).astype(np.float32)[:, None] * freq, (pos % 64).astype(np.float32)[:, None] * freq], axis=1)
    co, si = np.cos(ang), np.sin(ang)
    table = np.concatenate([np.stack([co, co], 2).reshape(SEQ, HD), np.stack([-si, si], 2).reshape(SEQ, HD)], axis=1)
    rope = table.reshape(NBLK - 1, TPB, P, 2 * HD).transpose(0, 2, 1, 3)
    q_, k_ = np.arange(P)[:, None], np.arange(P)[None, :]
    mask = np.concatenate([np.where(k_ >= q_, 0.0, -1e30), np.where(k_ <= q_, 0.0, -1e30)], axis=1)

    def by_row(w):
        return np.moveaxis(w.reshape((KD, P) + w.shape[1:]), (0, 1), (-2, -3)).reshape(w.shape[1:-1] + (P, D))

    w_exp = np.stack([by_row(f["w_exp_gate"]), by_row(f["w_exp_up"]), f["w_exp_down"]], axis=2)
    w_sh = np.stack([by_row(f["w_sh_gate"]), by_row(f["w_sh_up"]), f["w_sh_down"]], axis=1)
    cst = np.zeros((P, 384 + P), np.float32)
    cst[:, 0:P] = np.arange(P)
    cst[:, P:P + NT] = np.arange(NT)
    cst[:, 224:240] = np.arange(NTILE)
    cst[:, 240] = np.arange(P)
    cst[:, 256:256 + NR] = 1.0
    cst[:, 384:] = q_ < k_
    arrays = {
        "pack": pack, "raw": raw.reshape(P, 4, NU, GH), "w_mod": f["w_mod"], "b_mod": f["b_mod"].reshape(6, D),
        "x": f["x"][0], "ctx": f["ctx"], "w_in": w_in, "w_glu": f["w_glu"], "w_out": w_out,
        "router_w": f["router_w"].reshape(KD, P, NR).transpose(1, 0, 2), "w_exp": w_exp.reshape(NR * P, 3 * D),
        "w_sh": w_sh, "cst": cst, "rope": rope,
        "ident": np.eye(P, dtype=np.float32), "mask": mask.astype(np.float32),
        "restart": same((np.arange(NTILE * NR) % NR != 0).astype(np.float32)),
    }
    return {k: np.ascontiguousarray(v) for k, v in arrays.items()}


def kernel(**inputs):
    import numpy as np
    import concourse.bacc as bacc
    from concourse.bass_utils import run_bass_kernel_spmd

    nc = bacc.Bacc("TRN2", target_bir_lowering=False, num_devices=1)
    arrays = lay_out(inputs)
    a = {k: nc.dram_tensor(f"in_{k}", v.shape, mybir.dt.from_np(v.dtype), kind="ExternalInput").ap()
         for k, v in arrays.items()}
    out = nc.dram_tensor("out", (SEQ, D), F32, kind="ExternalOutput").ap()
    block_kernel(nc, a, out)
    r = run_bass_kernel_spmd(nc, [{f"in_{k}": v for k, v in arrays.items()}], core_ids=[0])
    return r.results[0]["out"].reshape(1, SEQ, D)
```
